# Optimizing a Trainium2 kernel written in Bass

```python
import math
import jax, jax.numpy as jnp
from jax import lax
import numpy as np

D_MODEL = 1024
BATCH = 1
SEQ = 256
DEPTH = 2

CHUNK = 64
Q_BLOCK = 128
N_MIXERS = 2
ATTN_HEADS = 8
ATTN_HEAD_DIM = D_MODEL // (2 * ATTN_HEADS)
ALIBI_MAX_BIAS = 8.0
MLSTM_INNER = 2 * D_MODEL
MLSTM_HEADS = 4
MLSTM_HEAD_DIM = MLSTM_INNER // MLSTM_HEADS
MLSTM_CONV = 4
QKV_BLOCK = 4
FFN_DENSE = ((8 * D_MODEL // 3 + 127) // 128) * 128
N_EXPERTS = 8
TOP_K = 2
FFN_EXPERT = 7 * D_MODEL // 2
N_ATTN_LAYERS = (DEPTH + 1) // 2
N_MLSTM_LAYERS = DEPTH // 2
NORM_EPS = 1e-6

kernel_name = 'hybrid_diffattn_mlstm_moe_trunk'

def rmsnorm(x, g):
    xf = x.astype(jnp.float32)
    y = xf * lax.rsqrt(jnp.mean(xf * xf, axis=-1, keepdims=True) + NORM_EPS)
    return (y * g.astype(jnp.float32)).astype(x.dtype)

def head_layernorm(x, g):
    xf = x.astype(jnp.float32)
    mu = jnp.mean(xf, axis=-1, keepdims=True)
    var = jnp.mean(jnp.square(xf - mu), axis=-1, keepdims=True)
    return (xf - mu) * lax.rsqrt(var + NORM_EPS) * g.astype(jnp.float32)

def modulate(x, shift, scale):
    return x * (1.0 + scale[:, None, :]) + shift[:, None, :]

def swiglu(h, w_gate, w_up, w_down):
    return (jax.nn.silu(h @ w_gate) * (h @ w_up)) @ w_down

def alibi_slopes(n_heads):
    return jnp.exp2(-ALIBI_MAX_BIAS * jnp.arange(1, n_heads + 1, dtype=jnp.float32) / n_heads)

def diff_attention(h, w_in, w_out, lam, subln_g, lambda_init):
    B, S, D = h.shape
    H, DA = ATTN_HEADS, ATTN_HEAD_DIM
    q, k, v = jnp.split(h @ w_in, 3, axis=-1)
    q = q.reshape(B, S, H, 2, DA) * (DA ** -0.5)
    k = k.reshape(B, S, H, 2, DA)
    v = v.reshape(B, S, H, 2 * DA)
    lam_f = lam.astype(jnp.float32)
    lam_full = (jnp.exp(jnp.sum(lam_f[0] * lam_f[1])) - jnp.exp(jnp.sum(lam_f[2] * lam_f[3]))
                + lambda_init)
    slopes = alibi_slopes(H)
    key_pos = jnp.arange(S)
    n_blk = S // Q_BLOCK
    q_blocks = jnp.moveaxis(q.reshape(B, n_blk, Q_BLOCK, H, 2, DA), 1, 0)

    def one_block(args):
        q_blk, blk = args
        qpos = blk * Q_BLOCK + jnp.arange(Q_BLOCK)
        dist = jnp.abs(qpos[:, None] - key_pos[None, :]).astype(jnp.float32)
        allowed = (key_pos[None, :] // CHUNK) <= (qpos[:, None] // CHUNK)
        bias = jnp.where(allowed[None], -slopes[:, None, None] * dist[None], -jnp.inf)
        s = jnp.einsum('bqhcd,bkhcd->bhcqk', q_blk, k, preferred_element_type=jnp.float32)
        p = jax.nn.softmax(s + bias[None, :, None], axis=-1)
        a = p[:, :, 0] - lam_full * p[:, :, 1]
        return jnp.einsum('bhqk,bkhe->bqhe', a.astype(v.dtype), v)

    o = lax.map(one_block, (q_blocks, jnp.arange(n_blk)))
    o = jnp.moveaxis(o, 0, 1).reshape(B, S, H, 2 * DA)
    o = rmsnorm(o, subln_g) * (1.0 - lambda_init)
    return o.reshape(B, S, D) @ w_out

def mlstm_cell(q, k, v, i_pre, f_pre):
    B, S, NH, DH = q.shape
    L = CHUNK
    NC = S // L

    def to_chunks(t):
        t = t.astype(jnp.float32).reshape((B, NC, L) + t.shape[2:])
        return jnp.moveaxis(jnp.moveaxis(t, 1, 0), 3, 2)

    qc = to_chunks(q)
    kc = to_chunks(k) * (DH ** -0.5)
    vc = to_chunks(v)
    ic = to_chunks(i_pre)
    bc = jnp.cumsum(jax.nn.log_sigmoid(to_chunks(f_pre)), axis=-1)
    causal = jnp.tril(jnp.ones((L, L), dtype=bool))

    def step(carry, inp):
        C, n, m = carry
        q_, k_, v_, i_, b_ = inp
        dlog = jnp.where(causal, b_[..., :, None] - b_[..., None, :] + i_[..., None, :], -jnp.inf)
        g = b_ + m[..., None]
        m_t = jnp.maximum(g, jnp.max(dlog, axis=-1))
        w = jnp.exp(dlog - m_t[..., None]) * jnp.einsum('bhtd,bhsd->bhts', q_, k_)
        inter = jnp.exp(g - m_t)
        num = (jnp.einsum('bhts,bhsd->bhtd', w, v_)
               + inter[..., None] * jnp.einsum('bhvd,bhtd->bhtv', C, q_))
        den = jnp.sum(w, axis=-1) + inter * jnp.einsum('bhd,bhtd->bht', n, q_)
        h = num / jnp.maximum(jnp.abs(den), jnp.exp(-m_t))[..., None]
        b_last = b_[..., -1]
        w_state = b_last[..., None] - b_ + i_
        m_new = jnp.maximum(b_last + m, jnp.max(w_state, axis=-1))
        decay = jnp.exp(b_last + m - m_new)
        ws = jnp.exp(w_state - m_new[..., None])
        C_new = decay[..., None, None] * C + jnp.einsum('bhsv,bhsd->bhvd', v_ * ws[..., None], k_)
        n_new = decay[..., None] * n + jnp.einsum('bhs,bhsd->bhd', ws, k_)
        return (C_new, n_new, m_new), h

    init = (jnp.zeros((B, NH, DH, DH), jnp.float32),
            jnp.zeros((B, NH, DH), jnp.float32),
            jnp.zeros((B, NH), jnp.float32))
    _, hs = lax.scan(step, init, (qc, kc, vc, ic, bc))
    hs = jnp.moveaxis(jnp.moveaxis(hs, 2, 3), 0, 1)
    return hs.reshape(B, S, NH, DH)

def mlstm_layer(h, w_in, conv_w, conv_b, w_q, w_k, w_v, w_gate, b_gate, skip, norm_g, w_out):
    B, S, _ = h.shape
    NH, DH = MLSTM_HEADS, MLSTM_HEAD_DIM
    x_m, z = jnp.split(h @ w_in, 2, axis=-1)
    xp = jnp.pad(x_m, ((0, 0), (MLSTM_CONV - 1, 0), (0, 0)))
    conv = sum(xp[:, j:j + S] * conv_w[j] for j in range(MLSTM_CONV)) + conv_b
    x_c = jax.nn.silu(conv)

    def headwise(t, w):
        return jnp.einsum('bsgi,gio->bsgo', t.reshape(B, S, -1, QKV_BLOCK), w).reshape(B, S, MLSTM_INNER)

    q = headwise(x_c, w_q)
    k = headwise(x_c, w_k)
    v = headwise(x_m, w_v)
    gates = (jnp.concatenate([q, k, v], axis=-1) @ w_gate + b_gate).astype(jnp.float32)
    i_pre, f_pre = gates[..., :NH], gates[..., NH:]
    hh = mlstm_cell(q.reshape(B, S, NH, DH), k.reshape(B, S, NH, DH), v.reshape(B, S, NH, DH), i_pre, f_pre)
    hh = head_layernorm(hh, norm_g.reshape(NH, DH)).reshape(B, S, MLSTM_INNER).astype(x_c.dtype)
    out = (hh + skip * x_c) * jax.nn.silu(z)
    return out @ w_out

def moe_swiglu(h, w_router, b_router, w_gate, w_up, w_down):
    B, S, D = h.shape
    t = h.reshape(B * S, D)
    logits = (t @ w_router).astype(jnp.float32) + b_router.astype(jnp.float32)
    probs = jax.nn.softmax(logits, axis=-1)
    top_p, top_i = lax.top_k(probs, TOP_K)
    top_p = top_p / jnp.sum(top_p, axis=-1, keepdims=True)
    combine = jnp.sum(jax.nn.one_hot(top_i, N_EXPERTS, dtype=jnp.float32) * top_p[..., None], axis=1)
    y = jnp.zeros_like(t)
    for e in range(N_EXPERTS):
        y = y + combine[:, e:e + 1].astype(t.dtype) * swiglu(t, w_gate[e], w_up[e], w_down[e])
    return y.reshape(B, S, D)

def setup_inputs(seed: int = 0) -> dict:
    key = jax.random.key(seed)
    ks = jax.random.split(key, 32)
    f32 = jnp.float32
    D, NA, NM = D_MODEL, N_ATTN_LAYERS, N_MLSTM_LAYERS
    DI, NH, DA = MLSTM_INNER, MLSTM_HEADS, ATTN_HEAD_DIM
    G = DI // QKV_BLOCK

    def nrm(k, shape, scale):
        return jax.random.normal(k, shape, f32) * scale

    b_gate = jnp.concatenate([nrm(ks[19], (NM, NH), 0.1),
                              jnp.linspace(3.0, 6.0, NH, dtype=f32)[None, :] + nrm(ks[20], (NM, NH), 0.1)], axis=-1)
    return {
        'x': nrm(ks[0], (BATCH, SEQ, D), 1.0),
        'c': nrm(ks[1], (BATCH, D), 1.0),
        'mod_w': nrm(ks[2], (DEPTH, D, 6 * D), D ** -0.5),
        'mod_b': nrm(ks[3], (DEPTH, 6 * D), 0.02),
        'norm_g': 1.0 + nrm(ks[4], (DEPTH, 4, D), 0.05),
        'attn_w_in': nrm(ks[5], (NA, D, 3 * D), D ** -0.5),
        'attn_w_out': nrm(ks[6], (NA, D, D), D ** -0.5),
        'attn_lambda': nrm(ks[7], (NA, 4, DA), 0.1),
        'attn_subln': 1.0 + nrm(ks[8], (NA, 2 * DA), 0.05),
        'ffn_w_gate': nrm(ks[9], (NA, D, FFN_DENSE), D ** -0.5),
        'ffn_w_up': nrm(ks[10], (NA, D, FFN_DENSE), D ** -0.5),
        'ffn_w_down': nrm(ks[11], (NA, FFN_DENSE, D), FFN_DENSE ** -0.5),
        'mlstm_w_in': nrm(ks[12], (NM, D, 2 * DI), D ** -0.5),
        'mlstm_conv_w': nrm(ks[13], (NM, MLSTM_CONV, DI), MLSTM_CONV ** -0.5),
        'mlstm_conv_b': nrm(ks[14], (NM, DI), 0.02),
        'mlstm_w_q': nrm(ks[15], (NM, G, QKV_BLOCK, QKV_BLOCK), QKV_BLOCK ** -0.5),
        'mlstm_w_k': nrm(ks[16], (NM, G, QKV_BLOCK, QKV_BLOCK), QKV_BLOCK ** -0.5),
        'mlstm_w_v': nrm(ks[17], (NM, G, QKV_BLOCK, QKV_BLOCK), QKV_BLOCK ** -0.5),
        'mlstm_w_gate': nrm(ks[18], (NM, 3 * DI, 2 * NH), (3 * DI) ** -0.5),
        'mlstm_b_gate': b_gate,
        'mlstm_skip': 1.0 + nrm(ks[21], (NM, DI), 0.05),
        'mlstm_norm': 1.0 + nrm(ks[22], (NM, DI), 0.05),
        'mlstm_w_out': nrm(ks[23], (NM, DI, D), DI ** -0.5),
        'moe_w_router': nrm(ks[24], (NM, D, N_EXPERTS), D ** -0.5),
        'moe_b_router': nrm(ks[25], (NM, N_EXPERTS), 0.01),
        'moe_w_gate': nrm(ks[26], (NM, N_EXPERTS, D, FFN_EXPERT), D ** -0.5),
        'moe_w_up': nrm(ks[27], (NM, N_EXPERTS, D, FFN_EXPERT), D ** -0.5),
        'moe_w_down': nrm(ks[28], (NM, N_EXPERTS, FFN_EXPERT, D), FFN_EXPERT ** -0.5),
    }

def reference(x, c, mod_w, mod_b, norm_g, attn_w_in, attn_w_out, attn_lambda, attn_subln,
              ffn_w_gate, ffn_w_up, ffn_w_down, mlstm_w_in, mlstm_conv_w, mlstm_conv_b,
              mlstm_w_q, mlstm_w_k, mlstm_w_v, mlstm_w_gate, mlstm_b_gate, mlstm_skip, mlstm_norm,
              mlstm_w_out, moe_w_router, moe_b_router, moe_w_gate, moe_w_up, moe_w_down):
    B = x.shape[0]
    cond = jax.nn.silu(c)
    for i in range(DEPTH):
        mod = (cond @ mod_w[i] + mod_b[i]).reshape(B, 6, D_MODEL)
        g = norm_g[i]
        j = i // N_MIXERS
        h = modulate(rmsnorm(x, g[0]), mod[:, 0], mod[:, 1])
        if i % N_MIXERS == 0:
            lambda_init = 0.8 - 0.6 * math.exp(-0.3 * i)
            y = diff_attention(h, attn_w_in[j], attn_w_out[j], attn_lambda[j], attn_subln[j], lambda_init)
        else:
            y = mlstm_layer(h, mlstm_w_in[j], mlstm_conv_w[j], mlstm_conv_b[j], mlstm_w_q[j], mlstm_w_k[j],
                            mlstm_w_v[j], mlstm_w_gate[j], mlstm_b_gate[j], mlstm_skip[j], mlstm_norm[j],
                            mlstm_w_out[j])
        x = x + mod[:, 2][:, None, :] * rmsnorm(y, g[1])
        h = modulate(rmsnorm(x, g[2]), mod[:, 3], mod[:, 4])
        if i % 2 == 0:
            y = swiglu(h, ffn_w_gate[j], ffn_w_up[j], ffn_w_down[j])
        else:
            y = moe_swiglu(h, moe_w_router[j], moe_b_router[j], moe_w_gate[j], moe_w_up[j], moe_w_down[j])
        x = x + mod[:, 5][:, None, :] * rmsnorm(y, g[3])
    return x


_drawn_inputs = setup_inputs


def setup_inputs(seed=0):
    import zlib

    import numpy as np

    out = dict(_drawn_inputs(seed))
    spreads = {}
    factors = {}
    for name, (base, spread) in spreads.items():
        noise = np.random.default_rng([zlib.crc32(name.encode()), seed]).standard_normal(out[name].shape)
        drawn = base * np.exp(spread * noise) if base else spread * noise
        out[name] = __import__('jax').numpy.asarray(drawn.astype(out[name].dtype))
    for name, factor in factors.items():
        out[name] = (out[name] * factor).astype(out[name].dtype)
    return out
```

```python
from contextlib import ExitStack

import concourse.bass as bass
from concourse import mybir

ALU = mybir.AluOpType
ACT = mybir.ActivationFunctionType
F32 = mybir.dt.float32
I32 = mybir.dt.int32
U32 = mybir.dt.uint32
AX_X = mybir.AxisListType.X

P = 128
D = 1024
KT = D // P
S = 256
TT = S // P
HEADS, HD, DA = 8, 128, 64
FF = ((8 * D // 3 + 127) // 128) * 128
FT = FF // P
INNER = 2 * D
IT = INNER // P
MH, MD = 4, 512
MK = MD // P
CONV = 4
E = 8
FE = 7 * D // 2
ET = FE // P
CHUNK = 64
EPS = 1e-6
LAMBDA_INIT = 0.2
BIG = 1e30

SLOTS = 7
SLOT = 4096
WC = 512
DK = SLOT // D
UB = 4


def chunk_plan():
    up = lambda m, j, n=WC: (m, j * WC, n, "pe")
    mod = lambda layer, j: (f"mod{layer}", j * WC, WC, "dve")
    plan = [mod(0, j) for j in range(4)]
    after = {0: [4, 5], 1: [6], 2: [7, 8], 3: [9], 4: [10], 5: [11]}
    for j in range(6):
        plan += [up("attn_in", j)] + [mod(0, m) for m in after[j]]
    plan += [("attn_out", k, DK, "pe") for k in range(0, KT, DK)]
    for j in range(6):
        n = min(WC, FF - j * WC)
        plan += [up("gate", j, n), up("up", j, n), mod(1, 2 * j), mod(1, 2 * j + 1)]
    k = 0
    for n in [4, 4, 4, 4, 2, 2, 2]:
        plan.append(("down", k, n, "pe"))
        k += n
    plan += [up("mlstm_in", j) for j in range(8)]
    plan += [("mlstm_out", k, DK, "pe") for k in range(0, IT, DK)]
    return plan


PLAN = chunk_plan()
NPRE = len(PLAN)
EC = 3 * FE // WC
assert NPRE % SLOTS == 0 and EC % SLOTS == 0
PRE_USES = NPRE // SLOTS


FILLS = {}
FILLS["attn"] = 1 + KT // 2
FILLS["ffn"] = FILLS["attn"] + 12 + 2 * HEADS + 2 + KT // 2 + KT // 2
FILLS["x_m"] = FILLS["ffn"] + FT + 2 + KT // 2
FILLS["qkv"] = FILLS["x_m"] + 8
FILLS["z"] = FILLS["qkv"] + 2 * IT + 4 * MH
FILLS["moe"] = FILLS["z"] + IT // 2 + 2 + KT // 2 + 2
EJ = FE // WC


class Count:

    def __init__(self, start=0):
        self.n = start

    def next(self, k=1):
        self.n += k
        return self.n


def trunk(nc, a, out):
    with ExitStack() as ctx:
        def sb(name, shape, dt=F32):
            return ctx.enter_context(nc.sbuf_tensor(name, shape, dt))

        def sem(name):
            return ctx.enter_context(nc.semaphore(name))

        ring = sb("ring", [P, SLOTS, SLOT])
        x = sb("x", [P, TT, D])
        hT = sb("hT", [P, KT, S])
        flat_h = hT[:, :, :].rearrange("p k s -> p (k s)")
        gate_bc = flat_h[:, 0:D]
        scratch = flat_h[:, D:2 * D]
        ident = sb("ident", [P, P])
        ones = sb("ones", [P, P])
        tri = sb("tri", [P, P])
        tri_strict = sb("tri_strict", [P, P])
        causal = sb("causal", [P, P])
        slot_iota = sb("slot_iota", [P, S])
        block4 = sb("block4", [P, P // 4])
        vecs = sb("vecs", [P, 3 * P])
        modc = sb("modc", [P, 2, 48])
        mul_c = sb("mul_c", [P, 4, KT])
        gate_c = sb("gate_c", [P, 4, KT])
        cond = sb("cond", [P, KT])
        qkv_blocks = sb("qkv_blocks", [P, 3, IT, 4])
        w_gates = sb("w_gates", [P, 3 * IT, 2 * MH])
        b_gates = sb("b_gates", [P, 2 * MH])
        w_router = sb("w_router", [P, KT, E])
        b_router = sb("b_router", [P, E])
        small = sb("small", [P, 256])
        used = [0]

        def col(n):
            used[0] += n
            return small[:, used[0] - n:used[0]]

        exponent = col(TT * HEADS)
        sq_sum = col(4 * TT)
        var = col(TT)
        rstd = col(TT)
        lam_s = col(2)
        lam_e = col(2)
        neg_lam = col(1)
        nmax = col(8)
        psum_s = col(8)
        prec = col(8)
        var16 = col(16)
        rstd16 = col(16)
        gates = col(TT * 2 * MH).rearrange("p (t g) -> p t g", t=TT)
        f_abs = col(TT * MH).rearrange("p (t g) -> p t g", t=TT)
        f_exp = col(TT * MH).rearrange("p (t g) -> p t g", t=TT)
        logf = col(TT * MH).rearrange("p (t g) -> p t g", t=TT)
        cumf = col(TT * MH).rearrange("p (t g) -> p t g", t=TT)
        a_col = col(TT * MH).rearrange("p (t g) -> p t g", t=TT)
        run_max = col(TT)
        neg_m = col(TT)
        m_sum = col(TT)
        e_m = col(TT)
        den = col(TT)
        rden = col(TT)
        mean_var = col(TT * 2).rearrange("p (t g) -> p t g", t=TT)
        iota8 = slot_iota[:, 0:E]
        rt = sb("rt", [P, TT, 12, E])
        top_i = sb("top_i", [P, TT, E], U32)
        counts = sb("counts", [P, E], I32)
        per_e = sb("per_e", [P, E, 6])
        cur = sb("cur", [P, 6])
        arena = sb("arena", [P, 17712])
        at = [0]

        def area(n, first=None):
            if first is not None:
                at[0] = first
            at[0] += n
            assert at[0] <= 17712, at[0]
            return arena[:, at[0] - n:at[0]]

        xn = area(2048, 0).rearrange("p (t d) -> p t d", t=TT)
        junk = lambda i: xn[:, i // 2, (i % 2) * 512:(i % 2 + 1) * 512]
        mod_acc = area(1024).rearrange("p (b n) -> p b n", b=2)
        after_acc = at[0]
        rows = area(3 * P, after_acc).rearrange("p (r n) -> p r n", r=3)
        qT = area(2048, after_acc + 3 * P).rearrange("p (k s) -> p k s", k=KT)
        kT = area(2048).rearrange("p (k s) -> p k s", k=KT)
        v_nat = area(2048).rearrange("p (t d) -> p t d", t=TT)
        o_nat = area(2048).rearrange("p (t d) -> p t d", t=TT)
        probs = area(2 * 2 * 384).rearrange("p (b c n) -> p b c n", b=2, c=2)
        aT = area(2 * 384).rearrange("p (b n) -> p b n", b=2)
        oT = area(2048).rearrange("p (k s) -> p k s", k=KT)
        dist = area(384)
        lam_in = area(4 * DA).rearrange("p (i n) -> p i n", i=4)
        hid = area(FT * S, after_acc).rearrange("p (k s) -> p k s", k=FT)
        PAD = CONV - 1
        xm = area(IT * (S + PAD), 0).rearrange("p (k s) -> p k s", k=IT)
        xc = area(IT * S).rearrange("p (k s) -> p k s", k=IT)
        k_in = area(IT * S).rearrange("p (k s) -> p k s", k=IT)
        v_in = area(TT * INNER).rearrange("p (t d) -> p t d", t=TT)
        vT2 = area(2 * S).rearrange("p (b s) -> p b s", b=2)
        m_share = at[0]
        bd = area(2 * 3 * P, m_share).rearrange("p (b m o) -> p b m o", b=2, m=3)
        dw = area(2 * 384, m_share).rearrange("p (b n) -> p b n", b=2)
        diag_m = area(512, m_share)
        zs = v_in[:, 0, 0:1024].rearrange("p (b k s) -> p b k s", b=2, k=2)
        xg = area(KT * S, 2048).rearrange("p (k s) -> p k s", k=KT)
        eh = area(ET * S).rearrange("p (k s) -> p k s", k=ET)
        ye = area(TT * D).rearrange("p (t d) -> p t d", t=TT)
        hx = ye
        y_sum = area(TT * D).rearrange("p (t d) -> p t d", t=TT)
        scat = area(TT * S).rearrange("p (t s) -> p t s", t=TT)
        sel = area(TT * S).rearrange("p (t s) -> p t s", t=TT)
        selw = area(TT * S).rearrange("p (t s) -> p t s", t=TT)
        bn6 = sb("bn6", [P, TT, 6])

        ps = ctx.enter_context(nc.psum_tensor("ps", [P, 8, 512], F32))

        cA, cB, cC = 0, P, 2 * P
        conv_w = lambda j, t: vecs[:, cA + j * IT + t:cA + j * IT + t + 1]
        conv_b = lambda t: vecs[:, cA + 64 + t:cA + 65 + t]
        skip = lambda t: vecs[:, cA + 80 + t:cA + 81 + t]
        norm_m = lambda t: vecs[:, cA + 96 + t:cA + 97 + t]
        c_cols = vecs[:, cB:cB + KT]
        norm_g = lambda layer, i: vecs[:, cB + 8 + (layer * 4 + i) * KT:cB + 8 + (layer * 4 + i + 1) * KT]
        subln = vecs[:, cB + 72:cB + 73]
        mod_b = vecs[:, cC:cC + 96].rearrange("p (l n) -> p l n", l=2)

        consts = sem("consts")
        x_loaded = sem("x_loaded")
        rows_loaded = sem("rows_loaded")
        small_loaded = sem("small_loaded")
        landed = [sem(f"landed{s}") for s in range(SLOTS)]
        pe_read = sem("pe_read")
        freed = sem("freed")
        u_full = sem("u_full")
        u_free = sem("u_free")
        dstep = sem("dstep")
        astep = sem("astep")
        pstep = sem("pstep")
        cond_ready = sem("cond_ready")
        acc_ready = sem("acc_ready")
        mod_summed = sem("mod_summed")
        x_new = sem("x_new")
        sq_ready = sem("sq_ready")
        var_ready = sem("var_ready")
        rstd_ready = sem("rstd_ready")
        xn_ready = sem("xn_ready")
        diag_ready = sem("diag_ready")
        y_full = sem("y_full")
        t_free = sem("t_free")
        lam_ready = sem("lam_ready")
        maxed = sem("maxed")
        probs_ready = sem("probs_ready")
        a_ready = sem("a_ready")
        aT_full = sem("aT_full")
        aT_ready = sem("aT_ready")
        o_full = sem("o_full")
        o_ready = sem("o_ready")
        on_ready = sem("on_ready")
        silu_ready = sem("silu_ready")
        conv_ready = sem("conv_ready")
        xc_ready = sem("xc_ready")
        bd_ready = sem("bd_ready")
        gates_full = sem("gates_full")
        logf_in = sem("logf_in")
        logf_ln = sem("logf_ln")
        logf_ready = sem("logf_ready")
        cum_full = sem("cum_full")
        rmax_ready = sem("rmax_ready")
        dw_ready = sem("dw_ready")
        num_full = sem("num_full")
        hh_ready = sem("hh_ready")
        logits_full = sem("logits_full")
        route = sem("route")
        counts_ready = sem("counts_ready")
        sel_ready = sem("sel_ready")
        scat_full = sem("scat_full")
        scat_ready = sem("scat_ready")
        ye_ready = sem("ye_ready")
        spread = sem("spread")
        y_added = sem("y_added")
        stored = sem("stored")

        def head_weights(h):
            k = k_in[:, MK * h:MK * (h + 1), :].rearrange("p k s -> p (k s)")
            return k[:, 0:384], k[:, 384:768]

        def weights(matrix, first, n):
            if matrix.startswith("mod"):
                w = a["mod_w"][int(matrix[3])]
            else:
                w = {"attn_in": a["attn_w_in"], "attn_out": a["attn_w_out"], "gate": a["ffn_w_gate"],
                     "up": a["ffn_w_up"], "down": a["ffn_w_down"], "mlstm_in": a["mlstm_w_in"],
                     "mlstm_out": a["mlstm_w_out"]}[matrix][0]
            if matrix in ("attn_out", "down", "mlstm_out"):
                return w.rearrange("(k p) n -> p k n", p=P)[:, first:first + n, :]
            return w.rearrange("(k p) n -> p k n", p=P)[:, :, first:first + n]

        def slot_up(s, n=WC):
            return ring[:, s, 0:KT * n].rearrange("p (k n) -> p k n", n=n)

        def slot_down(s, k=DK):
            return ring[:, s, 0:k * D].rearrange("p (k n) -> p k n", n=D)

        order = {(m, f): i for i, (m, f, n, r) in enumerate(PLAN)}
        read_by = []
        n_mod = n_down = n_y = 0
        for m, f, n, r in PLAN:
            j = f // WC
            if r == "dve":
                n_mod += 1
                read_by.append((acc_ready, n_mod))
            elif m == "attn_in":
                read_by.append((u_full, FILLS["attn"] + 2 * (j + 1)))
            elif m in ("gate", "up"):
                read_by.append((u_full, FILLS["ffn"] + min(4 * (j + 1), FT)))
            elif m == "mlstm_in":
                read_by.append((u_full, (FILLS["x_m"] if j < 4 else FILLS["z"]) + 2 * (j % 4 + 1)))
            elif f + n == {"attn_out": KT, "down": FT, "mlstm_out": IT}[m]:
                n_y += 1
                read_by.append((y_full, n_y))
            else:
                n_down += 1
                read_by.append((pe_read, n_down))

        def wait_chunk(eng, i):
            eng.wait_ge(landed[i % SLOTS], 16 * (i // SLOTS + 1))

        def expert_chunk(sp, e, c):
            s = c % SLOTS
            n_up = 2 * (FE // WC)
            if c < n_up:
                w = a["moe_w_gate"] if c % 2 == 0 else a["moe_w_up"]
                src = w[0][e].rearrange("(k p) n -> p k n", p=P)[:, :, (c // 2) * WC:(c // 2 + 1) * WC]
                sp.dma_start(slot_up(s), src).then_inc(landed[s], 16)
            else:
                j = c - n_up
                src = a["moe_w_down"][0][e].rearrange("(k p) n -> p k n", p=P)[:, j * DK:(j + 1) * DK, :]
                sp.dma_start(slot_down(s), src).then_inc(landed[s], 16)

        def sp_program(sp):
            sp.dma_start(x[:], a["x"][0].rearrange("(t p) d -> p t d", p=P)).then_inc(x_loaded, 16)
            for i, (m, f, n, r) in enumerate(PLAN):
                if i >= SLOTS:
                    sp.wait_ge(*read_by[i - SLOTS])
                dst = slot_down(i % SLOTS, n) if m in ("attn_out", "down", "mlstm_out") else slot_up(i % SLOTS, n)
                sp.dma_start(dst, weights(m, f, n)).then_inc(landed[i % SLOTS], 16)
            with sp.Fori(0, E) as e:
                for c in range(EC):
                    sp.wait_ge(freed, e * EC + (c + 1))
                    expert_chunk(sp, e, c)
            sp.wait_ge(x_new, 4)
            sp.dma_start(out[0].rearrange("(t p) d -> p t d", p=P), x[:]).then_inc(stored, 16)
            sp.wait_ge(stored, 16)

        def pool_program(pool):
            steps = Count()

            def link(ins):
                ins.then_inc(pstep, 1)
                pool.wait_ge(pstep, steps.next())

            pool.memset(exponent, -0.5)
            pool.memset(ones[:], 1.0)
            pool.memset(ident[:], 0.0)
            pool.memset(tri[:], 1.0)
            pool.memset(tri_strict[:], 1.0)
            pool.memset(causal[:], 0.0)
            pool.memset(rows, 0.0)
            link(pool.memset(block4[:], 1.0))
            pool.affine_select(out=ident[:], in_=ident[:], compare_op=ALU.not_equal, fill=1.0, base=0,
                               pattern=[[-1, P]], channel_multiplier=1)
            pool.affine_select(out=tri[:], in_=tri[:], compare_op=ALU.is_ge, fill=0.0, base=0,
                               pattern=[[1, P]], channel_multiplier=-1)
            pool.affine_select(out=tri_strict[:], in_=tri_strict[:], compare_op=ALU.is_gt, fill=0.0, base=0,
                               pattern=[[1, P]], channel_multiplier=-1)
            pool.affine_select(out=causal[:], in_=causal[:], compare_op=ALU.is_ge, fill=-BIG, base=0,
                               pattern=[[-1, P]], channel_multiplier=1)
            link(pool.affine_select(out=block4[:], in_=block4[:], compare_op=ALU.is_ge, fill=0.0, base=0,
                                    pattern=[[-4, P // 4]], channel_multiplier=1))
            pool.affine_select(out=block4[:], in_=block4[:], compare_op=ALU.is_ge, fill=0.0, base=3,
                               pattern=[[4, P // 4]], channel_multiplier=-1)
            pool.iota(slot_iota[:], pattern=[[1, S]], base=0, channel_multiplier=0,
                      allow_small_or_imprecise_dtypes=True)
            pool.iota(dist[:, 0:P], pattern=[[1, P]], base=0, channel_multiplier=-1,
                      allow_small_or_imprecise_dtypes=True)
            pool.iota(dist[:, P:3 * P], pattern=[[1, S]], base=-P, channel_multiplier=-1,
                      allow_small_or_imprecise_dtypes=True).then_inc(consts, 1)

            def power(n, src, dst, width):
                pool.wait_ge(var_ready, n)
                pool.tensor_tensor(dst, src, exponent[:, 0:width], ALU.pow).then_inc(rstd_ready, 1)

            power(1, var, rstd, TT)
            power(2, var16, rstd16, TT * HEADS)
            for n in range(3, 7):
                power(n, var, rstd, TT)
            pool.wait_ge(u_free, FILLS["x_m"])
            pool.memset(xm[:, :, 0:PAD], 0.0).then_inc(consts, 1)
            pool.wait_ge(small_loaded, 16 * 8)
            for t in range(IT):
                if t >= 2:
                    pool.wait_ge(gates_full, t - 1)
                pool.tensor_tensor(
                    bd[:, t % 2].rearrange("p m (g o) -> p m g o", o=4),
                    qkv_blocks[:, :, t, :].unsqueeze(2).broadcast_to([P, 3, P // 4, 4]),
                    block4[:].unsqueeze(1).unsqueeze(3).broadcast_to([P, 3, P // 4, 4]),
                    ALU.mult).then_inc(bd_ready, 1)
            for h in range(MH):
                power(7 + h, var, rstd, TT)
            for n in range(11, 14):
                power(n, var, rstd, TT)

        def act_program(act):
            steps = Count()

            def link(ins):
                ins.then_inc(astep, 1)
                act.wait_ge(astep, steps.next())

            act.dma_start(lam_in[:], a["attn_lambda"][0].unsqueeze(0).broadcast_to([P, 4, DA])).then_inc(small_loaded, 16)
            act.wait_ge(consts, 1)
            cw = a["mlstm_conv_w"][0]
            act.dma_start(rows[0:64, 0, :], cw.rearrange("j (t p) -> (j t) p", p=P)).then_inc(rows_loaded, 16)
            act.dma_start(rows[64:80, 0, :], a["mlstm_conv_b"][0].rearrange("(t p) -> t p", p=P)).then_inc(rows_loaded, 16)
            act.dma_start(rows[80:96, 0, :], a["mlstm_skip"][0].rearrange("(t p) -> t p", p=P)).then_inc(rows_loaded, 16)
            act.dma_start(rows[96:112, 0, :], a["mlstm_norm"][0].rearrange("(t p) -> t p", p=P)).then_inc(rows_loaded, 16)
            act.dma_start(rows[0:8, 1, :], a["c"][0].rearrange("(t p) -> t p", p=P)).then_inc(rows_loaded, 16)
            act.dma_start(rows[8:72, 1, :], a["norm_g"].rearrange("l i (t p) -> (l i t) p", p=P)).then_inc(rows_loaded, 16)
            act.dma_start(rows[72:73, 1, :], a["attn_subln"]).then_inc(rows_loaded, 16)
            act.dma_start(rows[0:96, 2, :], a["mod_b"].rearrange("l (t p) -> (l t) p", p=P)).then_inc(rows_loaded, 16)
            for m, name in enumerate(("mlstm_w_q", "mlstm_w_k", "mlstm_w_v")):
                act.dma_start(qkv_blocks[:, m], a[name][0].rearrange("(t g) i o -> (g i) t o", g=P // 4)).then_inc(small_loaded, 16)
            act.dma_start(w_gates[:], a["mlstm_w_gate"][0].rearrange("(k p) n -> p k n", p=P)).then_inc(small_loaded, 16)
            act.dma_start(b_gates[:], a["mlstm_b_gate"].broadcast_to([P, 2 * MH])).then_inc(small_loaded, 16)
            act.dma_start(w_router[:], a["moe_w_router"][0].rearrange("(k p) n -> p k n", p=P)).then_inc(small_loaded, 16)
            act.dma_start(b_router[:], a["moe_b_router"].broadcast_to([P, E])).then_inc(small_loaded, 16)

            def squares_x(n):
                if n == 0:
                    act.wait_ge(x_loaded, 16)
                else:
                    act.wait_ge(x_new, n)
                for t in range(TT):
                    ins = act.activation(xn[:, t], x[:, t], ACT.Square, accum_out=sq_sum[:, t:t + 1])
                ins.then_inc(sq_ready, 1)

            def normed_x(n, powers):
                act.wait_ge(rstd_ready, powers)
                for t in range(TT):
                    ins = act.activation(xn[:, t], x[:, t], ACT.Copy, scale=rstd[:, t:t + 1])
                ins.then_inc(xn_ready, 1)

            def squares_y(n):
                if n < 3:
                    act.wait_ge(y_full, n)
                else:
                    act.wait_ge(freed, SLOTS)
                for i in range(4):
                    ins = act.activation(junk(i), ps[:, 4 + i], ACT.Square, accum_out=sq_sum[:, i:i + 1])
                ins.then_inc(sq_ready, 1)

            act.wait_ge(u_free, 1)
            act.activation(cond[:], c_cols, ACT.Silu).then_inc(cond_ready, 1)
            act.wait_ge(lam_ready, 1)
            act.activation(lam_e, lam_s, ACT.Exp).then_inc(lam_ready, 1)
            squares_x(0)
            normed_x(0, 1)

            def exps(h):
                act.wait_ge(maxed, h + 1)
                b = h % 2
                for c in range(2):
                    for q in range(TT):
                        i = b * 4 + c * 2 + q
                        p = probs[:, b, c, 0:P] if q == 0 else probs[:, b, c, P:3 * P]
                        ins = act.activation(p, p, ACT.Exp, bias=nmax[:, i:i + 1], accum_out=psum_s[:, i:i + 1])
                ins.then_inc(probs_ready, 1)

            def move_aT(h):
                act.wait_ge(aT_full, h + 1)
                if h >= 2:
                    act.wait_ge(o_full, h - 1)
                act.activation(aT[:, h % 2], ps[:, 4 + h % 2, 0:384], ACT.Copy).then_inc(aT_ready, 1)

            def move_o(h):
                act.wait_ge(o_full, h + 1)
                act.activation(o_nat[:, :, h * HD:(h + 1) * HD],
                               ps[:, 6 + h % 2, 0:S].rearrange("p (t d) -> p t d", t=TT), ACT.Copy).then_inc(o_ready, 1)

            for h in range(HEADS + 2):
                if h < HEADS:
                    exps(h)
                if 1 <= h <= HEADS:
                    move_aT(h - 1)
                if h >= 2:
                    move_o(h - 2)
            squares_y(1)

            squares_x(1)
            normed_x(1, 4)
            u = FILLS["ffn"]
            for ft in range(FT):
                act.wait_ge(u_full, u + ft + 1)
                act.activation(hid[:, ft, :], ps[:, (u + ft) % UB, 0:S], ACT.Silu).then_inc(silu_ready, 1)
            squares_y(2)

            squares_x(2)
            normed_x(2, 6)
            for j in range(4):
                act.wait_ge(conv_ready, j + 1)
                for t in range(4 * j, 4 * j + 4):
                    ins = act.activation(xc[:, t], xc[:, t], ACT.Silu, bias=conv_b(t))
                ins.then_inc(xc_ready, 1)
            act.wait_ge(logf_in, 1)
            link(act.activation(f_exp, f_abs, ACT.Exp, scale=-1.0))
            act.activation(f_exp, f_exp, ACT.Ln, bias=1.0).then_inc(logf_ln, 1)
            for h in range(MH):
                act.wait_ge(rmax_ready, h + 1)
                b = h % 2
                act.activation(e_m, m_sum, ACT.Exp, scale=-1.0)
                act.activation(dw[:, b, 0:P], dw[:, b, 0:P], ACT.Exp, bias=neg_m[:, 0:1])
                act.activation(dw[:, b, P:3 * P], dw[:, b, P:3 * P], ACT.Exp, bias=neg_m[:, 1:2]).then_inc(dw_ready, 1)
            u = FILLS["z"]
            for i in range(IT // 2):
                act.wait_ge(u_full, u + i + 1)
                if i >= 2:
                    act.wait_ge(u_free, u + i - 1)
                act.activation(zs[:, i % 2].rearrange("p k s -> p (k s)"), ps[:, (u + i) % UB], ACT.Silu).then_inc(silu_ready, 1)
            squares_y(3)

            squares_x(3)
            normed_x(3, 12)
            act.wait_ge(route, 1)
            act.activation(rt[:, :, 3, 1], rt[:, :, 3, 0], ACT.Exp).then_inc(route, 1)

            act.wait_ge(counts_ready, 1)
            act.wait_ge(hx_ready, 2)
            act.nop().then_inc(silu_moe, 2)
            act.nop().then_inc(turn_free, 2)

            def expert(e, width):
                tiles, sw = shape_of(width)
                act.wait_ge(scat_full, e + 1)
                act.activation(scat[0:sw, 0:tiles, :],
                               ps[0:sw, 4, 0:tiles * S].rearrange("p (t s) -> p t s", t=tiles), ACT.Copy).then_inc(scat_ready, 1)
                for n in range(EJ * tiles + 1):
                    if n < EJ * tiles:
                        act.wait_ge(step_full, step_count(e, n, tiles))
                        if n >= 2:
                            act.wait_ge(turn_full, step_count(e, n - 2, tiles))
                        act.activation(hx[0:sw, n % 2, 0:WC], ps[0:sw, 2 * (n % 2)], ACT.Silu).then_inc(silu_moe, 2 // tiles)
                    if n:
                        m = n - 1
                        act.wait_ge(turn_full, step_count(e, m, tiles))
                        act.activation(eh[:, 4 * (m // tiles):4 * (m // tiles) + 4, (m % tiles) * P:(m % tiles) * P + sw],
                                       ps[:, 6 + m % 2].rearrange("p (c s) -> p c s", c=4)[:, :, 0:sw],
                                       ACT.Copy).then_inc(turn_free, 2 // tiles)
                act.wait_ge(freed, e * EC + (SLOTS + EC))
                for st in range(tiles):
                    for n in range(2):
                        src = ps[P // 2:P, 5] if width < P and n else ps[0:sw, 4 + 2 * st + n]
                        ins = act.activation(ye[0:sw, st, n * 512:(n + 1) * 512], src, ACT.Copy)
                ins.then_inc(ye_ready, 1)

            with act.Fori(0, E) as e:
                by_width(act, e, expert)
            act.wait_ge(y_added, 1 + E)
            for t in range(TT):
                ins = act.activation(xn[:, t], y_sum[:, t], ACT.Square, accum_out=sq_sum[:, t:t + 1])
            ins.then_inc(sq_ready, 1)

        def shape_of(width):
            return (width + P - 1) // P, min(width, P)

        def step_count(e, n, tiles):
            return e * (2 * EJ) + (2 + (n + 1) * (2 // tiles))

        def by_width(eng, e, body):
            n = eng.value_load(counts[0:1, bass.ds(e, 1)], min_val=0, max_val=S)
            with eng.If(n > P):
                body(e, S)
            with eng.Else():
                with eng.If(n > P // 2):
                    body(e, P)
                with eng.Else():
                    body(e, P // 2)
                eng.nop()

        def pe_program(pe):
            u = Count()
            reads = Count()

            def bank():
                n = u.next()
                if n > UB:
                    pe.wait_ge(u_free, n - UB)
                return ps[:, (n - 1) % UB]

            def chunk(m, f, n=WC):
                i = order[(m, f)]
                wait_chunk(pe, i)
                return i

            def mod_sum(layer, j, n):
                pe.wait_ge(acc_ready, n + 1)
                dst = ps[:, 7 if (layer == 1 or j < 4) else 6]
                for i in range(4):
                    ins = pe.matmul(dst[:, 4 * j + i:4 * j + i + 1], mod_acc[:, n % 2, i * P:(i + 1) * P], ones[:, 0:1],
                                    start=True, stop=True)
                ins.then_inc(mod_summed, 1)

            def transposes_x(n):
                pe.wait_ge(xn_ready, n + 1)
                transposes(xn)

            def transposes(src):
                for i in range(KT // 2):
                    b = bank()
                    for j in range(2):
                        for t in range(TT):
                            k = 2 * i + j
                            ins = pe.transpose(b[:, j * S + t * P:j * S + (t + 1) * P], src[:, t, k * P:(k + 1) * P], ident[:])
                    ins.then_inc(u_full, 1)

            def broadcast_gate(diagonals):
                pe.wait_ge(diag_ready, diagonals)
                for i in range(2):
                    b = bank()
                    pe.matmul(b, ones[:], scratch[:, i * 512:(i + 1) * 512], start=True, stop=True).then_inc(u_full, 1)

            def project(matrix, chunks, lhs, free):
                pe.wait_ge(t_free, free)
                last = chunks[-1][0] + chunks[-1][1] - 1
                for first, n in chunks:
                    i = chunk(matrix, first)
                    w = slot_down(i % SLOTS, n)
                    for k in range(n):
                        for t in range(TT):
                            for c in range(2):
                                ins = pe.matmul(ps[:, 4 + 2 * t + c], lhs[:, first + k, t * P:(t + 1) * P],
                                                w[:, k, c * 512:(c + 1) * 512], start=(first + k == 0), stop=(first + k == last))
                    if matrix == "mlstm_out":
                        ins.then_inc(freed, SLOTS - len(chunks) + 1 if first == 0 else 1)
                    else:
                        ins.then_inc(y_full if first + n - 1 == last else pe_read, 1)

            def up_tile(dst, w, c):
                for k in range(KT):
                    ins = pe.matmul(dst, w[:, k, c * P:(c + 1) * P], hT[:, k, :], start=(k == 0), stop=(k == KT - 1))
                return ins

            pe.wait_ge(consts, 1)
            pe.wait_ge(rows_loaded, 16 * 8)
            b = bank()
            for r in range(3):
                ins = pe.transpose(b[:, r * P:(r + 1) * P], rows[:, r, :], ident[:])
            ins.then_inc(u_full, 1)
            mods = 0
            for j in range(4):
                mod_sum(0, j, mods)
                mods += 1
            transposes_x(0)

            pe.wait_ge(u_free, u.n)
            after = {0: [4, 5], 1: [6], 2: [7, 8], 3: [9], 4: [10], 5: [11]}
            for j in range(6):
                i = chunk("attn_in", j * WC)
                w = slot_up(i % SLOTS)
                for g in range(2):
                    b = bank()
                    if j < 4:
                        for c in range(2):
                            ins = up_tile(b[:, c * S:(c + 1) * S], w, 2 * g + c)
                    else:
                        for k in range(KT):
                            ins = pe.matmul(b, hT[:, k, g * P:(g + 1) * P], w[:, k, :], start=(k == 0), stop=(k == KT - 1))
                    ins.then_inc(u_full, 1)
                if j:
                    for m in after[j - 1]:
                        mod_sum(0, m, mods)
                        mods += 1
            for m in after[5]:
                mod_sum(0, m, mods)
                mods += 1
            pe.wait_ge(u_free, u.n)
            pe.wait_ge(t_free, 2)

            def scores(h):
                for c in range(2):
                    b = bank()
                    r = slice(DA * c, DA * (c + 1))
                    pe.matmul(b[:, 0:P], qT[r, h, 0:P], kT[r, h, 0:P], start=True, stop=True)
                    pe.matmul(b[:, P:3 * P], qT[r, h, P:2 * P], kT[r, h, :], start=True, stop=True).then_inc(u_full, 1)

            def turn(h):
                pe.wait_ge(a_ready, h + 1)
                if h >= 2:
                    pe.wait_ge(aT_ready, h - 1)
                for i in range(3):
                    ins = pe.transpose(ps[:, 4 + h % 2, i * P:(i + 1) * P], probs[:, h % 2, 0, i * P:(i + 1) * P], ident[:])
                ins.then_inc(aT_full, 1)

            def values(h):
                pe.wait_ge(aT_ready, h + 1)
                if h >= 2:
                    pe.wait_ge(o_ready, h - 1)
                w = slice(h * HD, (h + 1) * HD)
                b = ps[:, 6 + h % 2]
                pe.matmul(b[:, 0:P], aT[:, h % 2, 0:P], v_nat[:, 0, w], start=True, stop=True)
                pe.matmul(b[:, P:2 * P], aT[:, h % 2, P:2 * P], v_nat[:, 0, w], start=True, stop=False)
                pe.matmul(b[:, P:2 * P], aT[:, h % 2, 2 * P:3 * P], v_nat[:, 1, w], start=False, stop=True).then_inc(o_full, 1)

            for h in range(HEADS + 2):
                if h < HEADS:
                    scores(h)
                if 1 <= h <= HEADS:
                    turn(h - 1)
                if h >= 2:
                    values(h - 2)
            broadcast_gate(1)
            pe.wait_ge(on_ready, 1)
            transposes(o_nat)
            pe.wait_ge(u_free, u.n)
            pe.wait_ge(o_ready, HEADS)
            project("attn_out", [(k, DK) for k in range(0, KT, DK)], oT, 2)

            transposes_x(1)
            pe.wait_ge(u_free, u.n)
            assert u.n == FILLS["ffn"], u.n
            pe.wait_ge(t_free, 3)
            for j in range(6):
                n = min(WC, FF - j * WC)
                ig, iu = chunk("gate", j * WC), chunk("up", j * WC)
                wg, wu = slot_up(ig % SLOTS, n), slot_up(iu % SLOTS, n)
                for c in range(n // P):
                    b = bank()
                    up_tile(b[:, 0:S], wg, c)
                    ins = up_tile(b[:, S:2 * S], wu, c)
                    ins.then_inc(u_full, 1)
                if j:
                    for m in (2 * j - 2, 2 * j - 1):
                        mod_sum(1, m, mods)
                        mods += 1
            for m in (10, 11):
                mod_sum(1, m, mods)
                mods += 1
            broadcast_gate(2)
            pe.wait_ge(u_free, u.n - 2)
            first = 0
            chunks = []
            for n in [4, 4, 4, 4, 2, 2, 2]:
                chunks.append((first, n))
                first += n
            project("down", chunks, hid, 4)

            transposes_x(2)
            pe.wait_ge(u_free, u.n)

            def mlstm_in(j):
                i = chunk("mlstm_in", j * WC)
                w = slot_up(i % SLOTS)
                for g in range(2):
                    b = bank()
                    for c in range(2):
                        ins = up_tile(b[:, c * S:(c + 1) * S], w, 2 * g + c)
                    ins.then_inc(u_full, 1)

            for j in range(4):
                mlstm_in(j)

            def gate_products(t):
                pe.wait_ge(u_free, FILLS["qkv"] + 2 * (t + 1))
                if t == 0:
                    pe.wait_ge(small_loaded, 16 * 8)
                    pe.wait_ge(t_free, 5)
                for tt in range(TT):
                    r = slice(tt * P, (tt + 1) * P)
                    for m, src in enumerate((xm[:, t, PAD:PAD + S], k_in[:, t], vT2[:, t % 2])):
                        ins = pe.matmul(ps[:, 4 + tt, 0:2 * MH], src[:, r], w_gates[:, m * IT + t, :],
                                        start=(t == 0 and m == 0), stop=(t == IT - 1 and m == 2))
                ins.then_inc(gates_full, 1)

            for t in range(IT):
                pe.wait_ge(xc_ready, t // 4 + 1)
                pe.wait_ge(bd_ready, t + 1)
                blocks = bd[:, t % 2]
                xt = xm[:, t, PAD:PAD + S]
                b = bank()
                pe.matmul(b[:, 0:S], blocks[:, 2], xt, start=True, stop=True)
                pe.matmul(b[:, S:S + P], xt[:, 0:P], blocks[:, 2], start=True, stop=True)
                pe.matmul(b[:, S + P:2 * S], xt[:, P:S], blocks[:, 2], start=True, stop=True).then_inc(u_full, 1)
                b = bank()
                pe.matmul(b[:, 0:S], blocks[:, 0], xc[:, t], start=True, stop=True)
                pe.matmul(b[:, S:2 * S], blocks[:, 1], xc[:, t], start=True, stop=True).then_inc(u_full, 1)
                if t:
                    gate_products(t - 1)
            gate_products(IT - 1)
            pe.wait_ge(logf_ready, 1)
            pe.matmul(ps[:, 6, 0:MH], tri[:], logf[:, 0], start=True, stop=True)
            pe.matmul(ps[:, 6, MH:2 * MH], ones[:], logf[:, 0], start=True, stop=False)
            pe.matmul(ps[:, 6, MH:2 * MH], tri[:], logf[:, 1], start=False, stop=True).then_inc(cum_full, 1)
            for t in range(TT):
                pe.wait_ge(diag_ready, 3 + t)
                pe.matmul(ps[:, 4 + t], ones[:], diag_m, start=True, stop=True).then_inc(cum_full, 1)

            def m_scores(h):
                b = bank()
                for k in range(MK):
                    pe.matmul(b[:, 0:P], xm[:, MK * h + k, PAD:PAD + P], k_in[:, MK * h + k, 0:P],
                              start=(k == 0), stop=(k == MK - 1))
                for k in range(MK):
                    ins = pe.matmul(b[:, P:3 * P], xm[:, MK * h + k, PAD + P:PAD + S], k_in[:, MK * h + k, :],
                                    start=(k == 0), stop=(k == MK - 1))
                ins.then_inc(u_full, 1)

            def m_values(h, scored):
                w, wT = head_weights(h)
                pe.wait_ge(u_free, scored)
                b = bank()
                for i in range(3):
                    ins = pe.transpose(b[:, i * P:(i + 1) * P], w[:, i * P:(i + 1) * P], ident[:])
                ins.then_inc(u_full, 1)
                pe.wait_ge(u_free, u.n)
                c = slice(h * MD, (h + 1) * MD)
                pe.matmul(ps[:, 6], wT[:, 0:P], v_in[:, 0, c], start=True, stop=True)
                pe.matmul(ps[:, 7], wT[:, P:2 * P], v_in[:, 0, c], start=True, stop=False)
                pe.matmul(ps[:, 7], wT[:, 2 * P:3 * P], v_in[:, 1, c], start=False, stop=True).then_inc(num_full, 1)

            def m_turn(h):
                pe.wait_ge(hh_ready, h + 1)
                for g in range(2):
                    b = bank()
                    for c in range(2):
                        for t in range(TT):
                            k = MK * h + 2 * g + c
                            ins = pe.transpose(b[:, c * S + t * P:c * S + (t + 1) * P], v_in[:, t, k * P:(k + 1) * P], ident[:])
                    ins.then_inc(u_full, 1)

            for h in range(MH):
                m_scores(h)
                scored = u.n
                if h:
                    m_turn(h - 1)
                m_values(h, scored)
            m_turn(MH - 1)
            assert u.n == FILLS["z"], u.n
            for j in range(4, 8):
                mlstm_in(j)
            broadcast_gate(5)
            pe.wait_ge(u_free, u.n - 2)
            project("mlstm_out", [(k, DK) for k in range(0, IT, DK)], xc, 5)

            transposes_x(3)
            pe.wait_ge(u_free, u.n)
            pe.wait_ge(t_free, 6)
            for t in range(TT):
                for k in range(KT):
                    ins = pe.matmul(ps[:, 4 + t, 0:E], hT[:, k, t * P:(t + 1) * P], w_router[:, k, :],
                                    start=(k == 0), stop=(k == KT - 1))
            ins.then_inc(logits_full, 1)
            pe.wait_ge(route, 3)
            chosen = lambda t: rt[:, t, 6, :]
            b = ps[:, 6]
            pe.matmul(b[:, 0:E], tri_strict[:], chosen(0), start=True, stop=True)
            pe.matmul(b[:, E:2 * E], ones[:], chosen(0), start=True, stop=False)
            pe.matmul(b[:, E:2 * E], tri_strict[:], chosen(1), start=False, stop=True)
            pe.matmul(b[:, 2 * E:3 * E], ones[:], chosen(0), start=True, stop=False)
            pe.matmul(b[:, 2 * E:3 * E], ones[:], chosen(1), start=False, stop=True).then_inc(logits_full, 1)
            broadcast_gate(6)
            assert u.n == FILLS["moe"], u.n

            def expert(e, width):
                tiles, sw = shape_of(width)
                wide = max(width, P)

                def arrived(c):
                    pe.wait_ge(landed[c % SLOTS], e * (16 * EC // SLOTS) + 16 * (PRE_USES + c // SLOTS + 1))

                pe.wait_ge(sel_ready, e + 1)
                pe.wait_ge(y_added, e + 1)
                for st in range(tiles):
                    for t in range(TT):
                        ins = pe.transpose(ps[:, 4, st * S + t * P:st * S + (t + 1) * P],
                                           selw[:, t, st * P:(st + 1) * P], ident[:])
                ins.then_inc(scat_full, 1)
                for i in range(KT // 2):
                    for j in range(2):
                        k = 2 * i + j
                        for t in range(TT):
                            ins = pe.matmul(ps[:, i, j * S:j * S + wide], xn[:, t, k * P:(k + 1) * P], sel[:, t, 0:wide],
                                            start=(t == 0), stop=(t == TT - 1))
                    ins.then_inc(gather_full, 1)
                pe.wait_ge(xg_ready, e + 1)

                def step(n):
                    j, st = n // tiles, n % tiles
                    arrived(2 * j)
                    arrived(2 * j + 1)
                    if n >= 2:
                        pe.wait_ge(hx_ready, step_count(e, n - 2, tiles))
                    wg, wu = slot_up((2 * j) % SLOTS), slot_up((2 * j + 1) % SLOTS)
                    b = 2 * (n % 2)
                    low = slice(P // 2, P) if width < P else slice(0, P)
                    for k in range(KT):
                        x_k = xg[:, k, st * P:st * P + sw]
                        pe.matmul(ps[0:sw, b], x_k, wg[:, k, :], start=(k == 0), stop=(k == KT - 1))
                        ins = pe.matmul(ps[low, b + 1], x_k, wu[:, k, :], start=(k == 0), stop=(k == KT - 1))
                    ins.then_inc(step_full, 2 // tiles)

                def turn(n, chunks_read):
                    pe.wait_ge(hx_ready, step_count(e, n, tiles))
                    if n >= 2:
                        pe.wait_ge(turn_free, step_count(e, n - 2, tiles))
                    elif n == 0:
                        pe.wait_ge(scat_ready, e + 1)
                    for c in range(4):
                        ins = pe.transpose(ps[:, 6 + n % 2, c * P:(c + 1) * P], hx[:, n % 2, c * P:(c + 1) * P], ident[:])
                        if c == 0 and chunks_read:
                            ins.then_inc(freed, chunks_read)
                    ins.then_inc(turn_full, 2 // tiles)

                for n in range(EJ * tiles + 1):
                    if n < EJ * tiles:
                        step(n)
                    if n:
                        last_tile = n < EJ * tiles and n % tiles == tiles - 1
                        turn(n - 1, (4 if tiles == 1 and n == 1 else 2) if last_tile else 0)
                for j in range(ET // DK):
                    c = 2 * EJ + j
                    arrived(c)
                    pe.wait_ge(turn_free, step_count(e, EJ * tiles - 1, tiles) if j == 0 else step_count(e, EJ * tiles - 1, tiles))
                    w = slot_down(c % SLOTS)
                    for k in range(DK):
                        ft = DK * j + k
                        for st in range(tiles):
                            for n in range(2):
                                dst = ps[P // 2:P, 5] if width < P and n else ps[0:sw, 4 + 2 * st + n]
                                ins = pe.matmul(dst, eh[:, ft, st * P:st * P + sw],
                                                w[:, k, n * 512:(n + 1) * 512], start=(ft == 0), stop=(ft == ET - 1))
                    ins.then_inc(freed, 1)
                pe.wait_ge(ye_ready, e + 1)
                for t in range(TT):
                    for n in range(2):
                        for st in range(tiles):
                            ins = pe.matmul(ps[:, 4 + 2 * t + n], scat[0:sw, st, t * P:(t + 1) * P],
                                            ye[0:sw, st, n * 512:(n + 1) * 512], start=(st == 0), stop=(st == tiles - 1))
                ins.then_inc(spread, 1)

            pe.wait_ge(u_free, u.n)
            pe.nop().then_inc(step_full, 2)
            pe.nop().then_inc(turn_full, 2)
            pe.wait_ge(counts_ready, 1)
            with pe.Fori(0, E) as e:
                by_width(pe, e, expert)

        def dve_program(dve):
            steps = Count()
            u = Count()
            powers = Count()
            xs = Count()
            t_reads = [3, 5, 6, 7]

            def link(ins):
                ins.then_inc(dstep, 1)
                dve.wait_ge(dstep, steps.next())

            def full():
                n = u.next()
                dve.wait_ge(u_full, n)
                return ps[:, (n - 1) % UB]

            def mod_chunk(layer, j, n):
                i = order[(f"mod{layer}", j * WC)]
                wait_chunk(dve, i)
                if n >= 2:
                    dve.wait_ge(mod_summed, n - 1)
                w = slot_up(i % SLOTS)
                acc = mod_acc[:, n % 2]
                link(dve.tensor_scalar(acc, w[:, 0], cond[:, 0:1], None, ALU.mult))
                for k in range(1, KT):
                    ins = dve.scalar_tensor_tensor(out=acc, in0=w[:, k], scalar=cond[:, k:k + 1], in1=acc,
                                                   op0=ALU.mult, op1=ALU.add)
                    if k < KT - 1:
                        link(ins)
                ins.then_inc(acc_ready, 1)

            def emptied(ins):
                return ins.then_inc(u_free, 1)

            def variance(src, n_sums, sq):
                dve.wait_ge(sq_ready, sq)
                if n_sums == 2:
                    link(dve.tensor_tensor(var, sq_sum[:, 0:4:2], sq_sum[:, 1:4:2], ALU.add))
                    src = var
                dve.tensor_scalar(var, src, 1.0 / D, EPS, ALU.mult, ALU.add).then_inc(var_ready, 1)
                powers.next()

            def modulated(n):
                layer, i = n // 2, n % 2
                for g in range(KT // 2):
                    b = full()
                    for j in range(2):
                        k = 2 * g + j
                        ins = dve.tensor_scalar(hT[:, k, :], b[:, j * S:(j + 1) * S], mul_c[:, n, k:k + 1],
                                                modc[:, layer, 24 * i + k:24 * i + k + 1], ALU.mult, ALU.add)
                    emptied(ins)

            def gate_diagonals(n):
                for k in range(KT):
                    ins = dve.tensor_scalar(scratch[:, k * P:(k + 1) * P], ident[:], gate_c[:, n, k:k + 1], None, ALU.mult)
                ins.then_inc(diag_ready, 1)

            def gate_rows():
                for i in range(2):
                    emptied(dve.tensor_copy(gate_bc[:, i * 512:(i + 1) * 512], full()))
                dve.wait_ge(u_free, u.n)

            def add_output(y, in_psum=True):
                dve.wait_ge(rstd_ready, powers.n)
                for t in range(TT):
                    for c in range(2):
                        ins = dve.scalar_tensor_tensor(out=scratch[:, c * 512:(c + 1) * 512], in0=y(t, c),
                                                       scalar=rstd[:, t:t + 1], in1=gate_bc[:, c * 512:(c + 1) * 512],
                                                       op0=ALU.mult, op1=ALU.mult)
                    if t == 0:
                        link(ins)
                        link(dve.tensor_tensor(x[:, t], x[:, t], scratch, ALU.add))
                ins.then_inc(t_free, 1)
                dve.wait_ge(t_free, t_reads[xs.n])
                dve.tensor_tensor(x[:, t], x[:, t], scratch, ALU.add).then_inc(x_new, 1)
                xs.next()

            b = full()
            emptied(dve.tensor_copy(vecs[:], b[:, 0:3 * P]))
            dve.wait_ge(u_free, 1)
            dve.wait_ge(small_loaded, 16 * 8)
            link(dve.tensor_tensor(lam_in[:, 0:4:2], lam_in[:, 0:4:2], lam_in[:, 1:4:2], ALU.mult))
            dve.tensor_reduce(lam_s, lam_in[:, 0:4:2], AX_X, ALU.add).then_inc(lam_ready, 1)
            dve.wait_ge(consts, 1)
            link(dve.scalar_tensor_tensor(out=dist, in0=dist, scalar=-1.0, in1=dist, op0=ALU.mult, op1=ALU.max))
            dve.memset(dist[0:CHUNK, CHUNK:P], BIG)
            link(dve.memset(dist[0:CHUNK, 2 * P + CHUNK:3 * P], BIG))
            dve.wait_ge(lam_ready, 2)
            link(dve.tensor_tensor(neg_lam, lam_e[:, 1:2], lam_e[:, 0:1], ALU.subtract))
            link(dve.tensor_scalar(neg_lam, neg_lam, -LAMBDA_INIT, None, ALU.add))
            variance(sq_sum[:, 0:2], 1, 1)
            dve.wait_ge(cond_ready, 1)
            mods = 0
            for j in range(4):
                mod_chunk(0, j, mods)
                mods += 1
            dve.wait_ge(mod_summed, 4)
            dve.tensor_tensor(modc[:, 0, 0:16], ps[:, 7, 0:16], mod_b[:, 0, 0:16], ALU.add).then_inc(t_free, 1)
            dve.wait_ge(t_free, 1)
            link(dve.scalar_tensor_tensor(out=mul_c[:, 0], in0=modc[:, 0, 8:16], scalar=1.0, in1=norm_g(0, 0),
                                          op0=ALU.add, op1=ALU.mult))
            modulated(0)
            after = {0: [4, 5], 1: [6], 2: [7, 8], 3: [9], 4: [10], 5: [11]}
            for j in range(6):
                for g in range(2):
                    b = full()
                    pair = slice((4 * j + 2 * g) % 8, (4 * j + 2 * g) % 8 + 2)
                    b2 = b.rearrange("p (k s) -> p k s", k=2)
                    if j < 2:
                        ins = dve.tensor_scalar(qT[:, pair], b2, float(DA) ** -0.5, None, ALU.mult)
                    elif j < 4:
                        ins = dve.tensor_copy(kT[:, pair], b2)
                    else:
                        ins = dve.tensor_copy(v_nat[:, g, (j - 4) * 512:(j - 3) * 512], b)
                    emptied(ins)
                for m in after[j]:
                    mod_chunk(0, m, mods)
                    mods += 1
            dve.wait_ge(mod_summed, 12)
            dve.tensor_tensor(modc[:, 0, 16:48], ps[:, 6, 16:48], mod_b[:, 0, 16:48], ALU.add).then_inc(t_free, 1)
            dve.wait_ge(t_free, 2)
            dve.tensor_tensor(gate_c[:, 0], modc[:, 0, 16:24], norm_g(0, 1), ALU.mult)
            dve.tensor_tensor(gate_c[:, 1], modc[:, 0, 40:48], norm_g(0, 3), ALU.mult)
            link(dve.scalar_tensor_tensor(out=mul_c[:, 1], in0=modc[:, 0, 32:40], scalar=1.0, in1=norm_g(0, 2),
                                          op0=ALU.add, op1=ALU.mult))
            gate_diagonals(0)

            def logits(h):
                bb = h % 2
                if h >= 2:
                    dve.wait_ge(aT_full, h - 1)
                slope = 2.0 ** (-8.0 * (h + 1) / HEADS)
                for c in range(2):
                    emptied(dve.scalar_tensor_tensor(out=probs[:, bb, c], in0=dist, scalar=-slope, in1=full()[:, 0:384],
                                                     op0=ALU.mult, op1=ALU.add))
                dve.wait_ge(u_free, u.n)
                for c in range(2):
                    i = bb * 4 + c * 2
                    dve.tensor_reduce(nmax[:, i:i + 1], probs[:, bb, c, 0:P], AX_X, ALU.max, negate=True)
                    ins = dve.tensor_reduce(nmax[:, i + 1:i + 2], probs[:, bb, c, P:3 * P], AX_X, ALU.max, negate=True)
                ins.then_inc(maxed, 1)

            def difference(h):
                bb = h % 2
                dve.wait_ge(probs_ready, h + 1)
                link(dve.reciprocal(prec[:, bb * 4:bb * 4 + 4], psum_s[:, bb * 4:bb * 4 + 4]))
                link(dve.tensor_scalar(prec[:, bb * 4 + 2:bb * 4 + 4], prec[:, bb * 4 + 2:bb * 4 + 4], neg_lam, None, ALU.mult))
                for q, r in enumerate((slice(0, P), slice(P, 3 * P))):
                    i = bb * 4 + q
                    ins = dve.tensor_scalar(probs[:, bb, 0, r], probs[:, bb, 0, r], prec[:, i:i + 1], None, ALU.mult)
                link(ins)
                for q, r in enumerate((slice(0, P), slice(P, 3 * P))):
                    i = bb * 4 + 2 + q
                    ins = dve.scalar_tensor_tensor(out=probs[:, bb, 0, r], in0=probs[:, bb, 1, r], scalar=prec[:, i:i + 1],
                                                   in1=probs[:, bb, 0, r], op0=ALU.mult, op1=ALU.add)
                ins.then_inc(a_ready, 1)

            for h in range(HEADS + 1):
                if h < HEADS:
                    logits(h)
                if h:
                    difference(h - 1)
            gate_rows()
            dve.wait_ge(o_ready, HEADS)
            o16 = o_nat.rearrange("p t (h e) -> p (t h) e", e=HD)
            sq = qT.rearrange("p k s -> p (k s)").rearrange("p (h e) -> p h e", e=HD)
            link(dve.tensor_tensor(sq, o16, o16, ALU.mult))
            link(dve.tensor_reduce(var16, sq, AX_X, ALU.add))
            dve.tensor_scalar(var16, var16, 1.0 / HD, EPS, ALU.mult, ALU.add).then_inc(var_ready, 1)
            dve.wait_ge(rstd_ready, powers.next())
            dve.tensor_tensor(o16, o16, rstd16.unsqueeze(2).broadcast_to([P, TT * HEADS, HD]), ALU.mult).then_inc(on_ready, 1)
            for g in range(KT // 2):
                emptied(dve.tensor_scalar(oT[:, 2 * g:2 * g + 2], full().rearrange("p (k s) -> p k s", k=2), subln,
                                          1.0 - LAMBDA_INIT, ALU.mult, ALU.mult))
            variance(None, 2, 2)
            add_output(lambda t, c: ps[:, 4 + 2 * t + c])

            variance(sq_sum[:, 0:2], 1, 3)
            modulated(1)
            for j in range(6):
                n = min(WC, FF - j * WC)
                for c in range(n // P):
                    ft = 4 * j + c
                    b = full()
                    dve.wait_ge(silu_ready, ft + 1)
                    emptied(dve.tensor_tensor(hid[:, ft], hid[:, ft], b[:, S:2 * S], ALU.mult))
                for m in (2 * j, 2 * j + 1):
                    mod_chunk(1, m, mods)
                    mods += 1
            gate_diagonals(1)
            gate_rows()
            dve.wait_ge(mod_summed, 24)
            dve.tensor_tensor(modc[:, 1], ps[:, 7, 0:48], mod_b[:, 1], ALU.add).then_inc(t_free, 1)
            dve.wait_ge(t_free, 4)
            for i in range(2):
                dve.tensor_tensor(gate_c[:, 2 + i], modc[:, 1, 24 * i + 16:24 * i + 24], norm_g(1, 2 * i + 1), ALU.mult)
                ins = dve.scalar_tensor_tensor(out=mul_c[:, 2 + i], in0=modc[:, 1, 24 * i + 8:24 * i + 16], scalar=1.0,
                                               in1=norm_g(1, 2 * i), op0=ALU.add, op1=ALU.mult)
            link(ins)
            variance(None, 2, 4)
            add_output(lambda t, c: ps[:, 4 + 2 * t + c])

            variance(sq_sum[:, 0:2], 1, 5)
            modulated(2)
            dve.wait_ge(consts, 2)
            for j in range(4):
                for g in range(2):
                    t0 = 4 * j + 2 * g
                    emptied(dve.tensor_copy(xm[:, t0:t0 + 2, PAD:PAD + S], full().rearrange("p (k s) -> p k s", k=2)))
                dve.wait_ge(u_free, u.n)
                for tap in range(CONV):
                    for t in range(4 * j, 4 * j + 4):
                        if tap == 0:
                            ins = dve.tensor_scalar(xc[:, t], xm[:, t, 0:S], conv_w(0, t), None, ALU.mult)
                        else:
                            ins = dve.scalar_tensor_tensor(out=xc[:, t], in0=xm[:, t, tap:tap + S], scalar=conv_w(tap, t),
                                                           in1=xc[:, t], op0=ALU.mult, op1=ALU.add)
                    if tap < CONV - 1:
                        link(ins)
                ins.then_inc(conv_ready, 1)
            for t in range(IT):
                b = full()
                if t >= 2:
                    dve.wait_ge(gates_full, t - 1)
                dve.tensor_copy(vT2[:, t % 2], b[:, 0:S])
                emptied(dve.tensor_copy(v_in[:, :, t * P:(t + 1) * P], b[:, S:2 * S].rearrange("p (t s) -> p t s", t=TT)))
                b = full()
                dve.tensor_copy(xm[:, t, PAD:PAD + S], b[:, 0:S])
                emptied(dve.tensor_copy(k_in[:, t], b[:, S:2 * S]))
                dve.tensor_scalar(xc[:, t], xc[:, t], skip(t), None, ALU.mult)
            dve.wait_ge(gates_full, IT)
            for t in range(TT):
                ins = dve.tensor_tensor(gates[:, t], ps[:, 4 + t, 0:2 * MH], b_gates[:], ALU.add)
            link(ins)
            fg = gates[:, :, MH:2 * MH]
            dve.scalar_tensor_tensor(out=f_abs, in0=fg, scalar=-1.0, in1=fg, op0=ALU.mult, op1=ALU.max).then_inc(logf_in, 1)
            link(dve.tensor_scalar(logf, fg, 0.0, None, ALU.min))
            dve.wait_ge(logf_ln, 1)
            dve.tensor_tensor(logf, logf, f_exp, ALU.subtract).then_inc(logf_ready, 1)
            dve.wait_ge(cum_full, 1)
            link(dve.tensor_copy(cumf, ps[:, 6, 0:TT * MH].rearrange("p (t g) -> p t g", t=TT)))
            link(dve.tensor_tensor(a_col, gates[:, :, 0:MH], cumf, ALU.subtract))
            for t in range(TT):
                if t:
                    dve.wait_ge(cum_full, 2)
                for h in range(MH):
                    ins = dve.tensor_scalar(diag_m[:, h * P:(h + 1) * P], ident[:], a_col[:, t, h:h + 1], None, ALU.mult)
                ins.then_inc(diag_ready, 1)
            dve.wait_ge(cum_full, 3)

            def exponents(h):
                b = h % 2
                r = slice(h * P, (h + 1) * P)
                if h:
                    dve.wait_ge(dw_ready, h)
                dve.tensor_tensor(dw[:, b, 0:P], ps[:, 4, r], causal[:], ALU.add)
                dve.tensor_copy(dw[:, b, P:2 * P], ps[:, 4, r])
                link(dve.tensor_tensor(dw[:, b, 2 * P:3 * P], ps[:, 5, r], causal[:], ALU.add))
                dve.tensor_reduce(run_max[:, 0:1], dw[:, b, 0:P], AX_X, ALU.max)
                link(dve.tensor_reduce(run_max[:, 1:2], dw[:, b, P:3 * P], AX_X, ALU.max))
                link(dve.tensor_scalar(run_max, run_max, 0.0, None, ALU.max))
                dve.tensor_scalar(neg_m, run_max, -1.0, None, ALU.mult)
                dve.tensor_tensor(m_sum, cumf[:, :, h], run_max, ALU.add).then_inc(rmax_ready, 1)

            def weigh(h):
                w, wT = head_weights(h)
                b = h % 2
                bank = full()
                dve.wait_ge(dw_ready, h + 1)
                dve.tensor_tensor_reduce(out=w[:, 0:P], in0=bank[:, 0:P], in1=dw[:, b, 0:P], scale=float(MD) ** -0.5,
                                         scalar=0.0, op0=ALU.mult, op1=ALU.add, accum_out=den[:, 0:1])
                emptied(dve.tensor_tensor_reduce(out=w[:, P:3 * P], in0=bank[:, P:3 * P], in1=dw[:, b, P:3 * P],
                                                 scale=float(MD) ** -0.5, scalar=0.0, op0=ALU.mult, op1=ALU.add,
                                                 accum_out=den[:, 1:2]))
                dve.wait_ge(u_free, u.n)
                link(dve.scalar_tensor_tensor(out=rden, in0=den, scalar=-1.0, in1=den, op0=ALU.mult, op1=ALU.max))
                link(dve.tensor_tensor(rden, rden, e_m, ALU.max))
                link(dve.reciprocal(rden, rden))

            def turned_weights(h):
                w, wT = head_weights(h)
                emptied(dve.tensor_copy(wT, full()[:, 0:3 * P]))

            def outputs(h):
                c = slice(h * MD, (h + 1) * MD)
                dve.wait_ge(num_full, h + 1)
                for t in range(TT):
                    ins = dve.tensor_scalar(v_in[:, t, c], ps[:, 6 + t], rden[:, t:t + 1], None, ALU.mult)
                link(ins)
                for t in range(TT):
                    ins = dve.bn_stats(bn6[:, t], v_in[:, t, c])
                link(ins)
                for t in range(TT):
                    ins = dve.bn_aggr(mean_var[:, t], bn6[:, t])
                link(ins)
                dve.tensor_scalar(var, mean_var[:, :, 1], EPS, None, ALU.add).then_inc(var_ready, 1)
                dve.wait_ge(rstd_ready, powers.next())
                for t in range(TT):
                    ins = dve.tensor_scalar(v_in[:, t, c], v_in[:, t, c], mean_var[:, t, 0:1], rstd[:, t:t + 1],
                                            ALU.subtract, ALU.mult)
                ins.then_inc(hh_ready, 1)

            def turned_outputs(h):
                for g in range(2):
                    b = full()
                    for c in range(2):
                        t = MK * h + 2 * g + c
                        ins = dve.scalar_tensor_tensor(out=xc[:, t], in0=b[:, c * S:(c + 1) * S], scalar=norm_m(t),
                                                       in1=xc[:, t], op0=ALU.mult, op1=ALU.add)
                    emptied(ins)

            for h in range(MH):
                exponents(h)
                weigh(h)
                if h:
                    turned_outputs(h - 1)
                turned_weights(h)
                outputs(h)
            turned_outputs(MH - 1)
            dve.wait_ge(u_free, u.n)
            for i in range(IT // 2):
                b = full()
                dve.wait_ge(silu_ready, FT + i + 1)
                emptied(dve.tensor_tensor(xc[:, 2 * i:2 * i + 2], xc[:, 2 * i:2 * i + 2], zs[:, i % 2], ALU.mult))
            gate_diagonals(2)
            gate_rows()
            variance(None, 2, 6)
            add_output(lambda t, c: ps[:, 4 + 2 * t + c])

            variance(sq_sum[:, 0:2], 1, 7)
            modulated(3)
            logit, top, e2, w12 = rt[:, :, 0], rt[:, :, 1], rt[:, :, 3], rt[:, :, 4]
            index, chosen, weight, pick = rt[:, :, 5], rt[:, :, 6], rt[:, :, 7], rt[:, :, 8]
            dve.wait_ge(logits_full, 1)
            for t in range(TT):
                ins = dve.tensor_tensor(logit[:, t], ps[:, 4 + t, 0:E], b_router[:], ALU.add)
            link(ins)
            for t in range(TT):
                ins = dve.max(top[:, t], logit[:, t])
            link(ins)
            for t in range(TT):
                ins = dve.max_index(top_i[:, t], top[:, t], logit[:, t])
            link(ins)
            dve.tensor_tensor(e2[:, :, 0], top[:, :, 1], top[:, :, 0], ALU.subtract).then_inc(route, 1)
            link(dve.tensor_copy(index, top_i[:]))
            dve.wait_ge(route, 2)
            link(dve.tensor_scalar(w12[:, :, 0], e2[:, :, 1], 1.0, None, ALU.add))
            link(dve.reciprocal(w12[:, :, 0], w12[:, :, 0]))
            link(dve.tensor_tensor(w12[:, :, 1], w12[:, :, 0], e2[:, :, 1], ALU.mult))
            for t in range(TT):
                dve.tensor_scalar(chosen[:, t], iota8, index[:, t, 0:1], None, ALU.is_equal)
                dve.tensor_scalar(weight[:, t], iota8, index[:, t, 0:1], w12[:, t, 0:1], ALU.is_equal, ALU.mult)
                dve.tensor_scalar(pick[:, t], iota8, index[:, t, 1:2], None, ALU.is_equal)
                ins = dve.tensor_scalar(rt[:, t, 9], iota8, index[:, t, 1:2], w12[:, t, 1:2], ALU.is_equal, ALU.mult)
            link(ins)
            dve.tensor_tensor(weight, weight, rt[:, :, 9], ALU.add)
            ins = dve.tensor_tensor(chosen, chosen, pick, ALU.add)
            ins.then_inc(route, 1)
            dve.wait_ge(route, 3)
            for t in range(TT):
                dve.tensor_copy(per_e[:, :, 2 + t], chosen[:, t])
                dve.tensor_copy(per_e[:, :, 4 + t], weight[:, t])
            dve.wait_ge(logits_full, 2)
            dve.tensor_copy(counts[:], ps[:, 6, 2 * E:3 * E]).then_inc(counts_ready, 1)
            for t in range(TT):
                ins = dve.tensor_copy(per_e[:, :, t], ps[:, 6, t * E:(t + 1) * E])
            link(ins)
            gate_diagonals(3)
            gate_rows()
            dve.memset(y_sum, 0.0).then_inc(y_added, 1)
            dve.memset(ye, 0.0).then_inc(hx_ready, 2)
            dve.wait_ge(counts_ready, 1)
            assert u.n == FILLS["moe"], u.n

            def expert(e, width):
                tiles, sw = shape_of(width)
                dve.tensor_copy(cur[:], per_e[:, bass.ds(e, 1), :].rearrange("p a n -> p (a n)")).then_inc(cur_ready, 1)
                dve.wait_ge(cur_ready, e + 1)
                for t in range(TT):
                    n = max(width, P)
                    dve.tensor_scalar(sel[:, t, 0:n], slot_iota[:, 0:n], cur[:, t:t + 1], cur[:, 2 + t:3 + t],
                                      ALU.is_equal, ALU.mult)
                    ins = dve.tensor_scalar(selw[:, t, 0:n], slot_iota[:, 0:n], cur[:, t:t + 1], cur[:, 4 + t:5 + t],
                                            ALU.is_equal, ALU.mult)
                ins.then_inc(sel_ready, 1)
                for i in range(KT // 2):
                    dve.wait_ge(gather_full, e * (KT // 2) + (i + 1))
                    for j in range(2):
                        k = 2 * i + j
                        ins = dve.tensor_scalar(xg[:, k, 0:width], ps[:, i, j * S:j * S + width], mul_c[:, 3, k:k + 1],
                                                modc[:, 1, 24 + k:25 + k], ALU.mult, ALU.add)
                ins.then_inc(xg_ready, 1)
                up = slice(P // 2, P) if width < P else slice(0, P)
                for n in range(EJ * tiles):
                    dve.wait_ge(silu_moe, step_count(e, n, tiles))
                    dve.tensor_tensor(hx[0:sw, n % 2, 0:WC], hx[0:sw, n % 2, 0:WC], ps[up, 2 * (n % 2) + 1],
                                      ALU.mult).then_inc(hx_ready, 2 // tiles)
                dve.wait_ge(y_added, e + 1)
                dve.wait_ge(spread, e + 1)
                for t in range(TT):
                    for c in range(2):
                        r = slice(c * 512, (c + 1) * 512)
                        ins = dve.tensor_tensor(y_sum[:, t, r], y_sum[:, t, r], ps[:, 4 + 2 * t + c], ALU.add)
                ins.then_inc(y_added, 1)

            with dve.Fori(0, E) as e:
                by_width(dve, e, expert)
            variance(sq_sum[:, 0:2], 1, 8)
            add_output(lambda t, c: y_sum[:, t, c * 512:(c + 1) * 512])

        silu_moe = sem("silu_moe")
        gather_full = sem("gather_full")
        xg_ready = sem("xg_ready")
        step_full = sem("step_full")
        hx_ready = sem("hx_ready")
        turn_full = sem("turn_full")
        turn_free = sem("turn_free")
        cur_ready = sem("cur_ready")

        block = ctx.enter_context(nc.Block())

        @block.sync
        def _(sp):
            sp_program(sp)

        @block.gpsimd
        def _(pool):
            pool_program(pool)

        @block.scalar
        def _(act):
            act_program(act)

        @block.tensor
        def _(pe):
            pe_program(pe)

        @block.vector
        def _(dve):
            dve_program(dve)


_NAMES = ["x", "c", "mod_w", "mod_b", "norm_g", "attn_w_in", "attn_w_out", "attn_lambda", "attn_subln",
          "ffn_w_gate", "ffn_w_up", "ffn_w_down", "mlstm_w_in", "mlstm_conv_w", "mlstm_conv_b", "mlstm_w_q",
          "mlstm_w_k", "mlstm_w_v", "mlstm_w_gate", "mlstm_b_gate", "mlstm_skip", "mlstm_norm", "mlstm_w_out",
          "moe_w_router", "moe_b_router", "moe_w_gate", "moe_w_up", "moe_w_down"]


def kernel(**inputs):
    import numpy as np
    import concourse.bacc as bacc
    from concourse.bass_utils import run_bass_kernel_spmd

    nc = bacc.Bacc("TRN2", target_bir_lowering=False, num_devices=1)
    arrays, args = {}, {}
    for name in _NAMES:
        v = np.ascontiguousarray(inputs[name])
        arrays[f"in_{name}"] = v
        args[name] = nc.dram_tensor(f"in_{name}", v.shape, mybir.dt.from_np(v.dtype), kind="ExternalInput").ap()
    out = nc.dram_tensor("out_0", (1, S, D), F32, kind="ExternalOutput").ap()
    trunk(nc, args, out)
    r = run_bass_kernel_spmd(nc, [arrays], core_ids=[0])
    return r.results[0]["out_0"]
```

```python
from contextlib import ExitStack

import concourse.bass as bass
from concourse import mybir

ALU = mybir.AluOpType
ACT = mybir.ActivationFunctionType
F32 = mybir.dt.float32
I32 = mybir.dt.int32
U32 = mybir.dt.uint32
AX_X = mybir.AxisListType.X

P = 128
D = 1024
KT = D // P
S = 256
TT = S // P
HEADS, HD, DA = 8, 128, 64
FF = ((8 * D // 3 + 127) // 128) * 128
FT = FF // P
INNER = 2 * D
IT = INNER // P
MH, MD = 4, 512
MK = MD // P
CONV = 4
E = 8
FE = 7 * D // 2
ET = FE // P
CHUNK = 64
EPS = 1e-6
LAMBDA_INIT = 0.2
BIG = 1e30

MOD_ENDS = (4, 12, 24)
MOD_PARTS = {0: (0, 4, 12), 1: (0, 12)}

SLOTS = 7
SLOT = 4096
WC = 512
DK = SLOT // D
UB = 4


def chunk_plan():
    up = lambda m, j, n=WC: (m, j * WC, n, "pe")
    mod = lambda layer, j: (f"mod{layer}", j * WC, WC, "dve")
    plan = [mod(0, j) for j in range(4)]
    after = {0: [4, 5], 1: [6], 2: [7, 8], 3: [9], 4: [10], 5: [11]}
    for j in range(6):
        plan += [up("attn_in", j)] + [mod(0, m) for m in after[j]]
    plan += [("attn_out", k, DK, "pe") for k in range(0, KT, DK)]
    for j in range(6):
        n = min(WC, FF - j * WC)
        plan += [up("gate", j, n), up("up", j, n), mod(1, 2 * j), mod(1, 2 * j + 1)]
    k = 0
    for n in [4, 4, 4, 4, 2, 2, 2]:
        plan.append(("down", k, n, "pe"))
        k += n
    plan += [up("mlstm_in", j) for j in range(8)]
    plan += [("mlstm_out", k, DK, "pe") for k in range(0, IT, DK)]
    return plan


PLAN = chunk_plan()
NPRE = len(PLAN)
EC = 3 * FE // WC
assert NPRE % SLOTS == 0 and EC % SLOTS == 0
PRE_USES = NPRE // SLOTS


FILLS = {}
FILLS["attn"] = 1 + KT // 2
FILLS["ffn"] = FILLS["attn"] + 12 + 2 * HEADS + 2 + KT // 2 + KT // 2
FILLS["x_m"] = FILLS["ffn"] + FT + 2 + KT // 2
FILLS["qkv"] = FILLS["x_m"] + 8
FILLS["cell"] = FILLS["qkv"] + 2 * IT
FILLS["moe"] = FILLS["cell"] + 6 * MH + 2 + KT // 2 + 2


def fills_after_z(h):
    return FILLS["cell"] + (6 * h - 2 if h else 0) + 3
EJ = FE // WC
STEP = WC // P
WIDTHS = [P // 2] + list(range(P, S + 1, 16))


class Count:

    def __init__(self, start=0):
        self.n = start

    def next(self, k=1):
        self.n += k
        return self.n


def trunk(nc, a, out):
    with ExitStack() as ctx:
        def sb(name, shape, dt=F32):
            return ctx.enter_context(nc.sbuf_tensor(name, shape, dt))

        def sem(name):
            return ctx.enter_context(nc.semaphore(name))

        ring = sb("ring", [P, SLOTS, SLOT])
        x = sb("x", [P, TT, D])
        hT = sb("hT", [P, KT, S])
        flat_h = hT[:, :, :].rearrange("p k s -> p (k s)")
        gate_bc = flat_h[:, 0:D]
        scratch = flat_h[:, D:2 * D]
        ident = sb("ident", [P, P])
        ones = sb("ones", [P, P])
        tri = sb("tri", [P, P])
        tri_strict = sb("tri_strict", [P, P])
        causal = sb("causal", [P, P])
        slot_iota = sb("slot_iota", [P, S])
        block4 = sb("block4", [P, P // 4])
        ones_col = sb("ones_col", [P, 63])
        eight = sb("eight", [P, 2 * MH])
        vecs = sb("vecs", [P, 3 * P])
        modc = sb("modc", [P, 2, 48])
        mul_c = sb("mul_c", [P, 4, KT])
        gate_c = sb("gate_c", [P, 4, KT])
        cond = sb("cond", [P, KT])
        qkv_blocks = sb("qkv_blocks", [P, 3, IT, 4])
        w_gates = sb("w_gates", [P, 3 * IT, 2 * MH])
        b_gates = sb("b_gates", [P, 2 * MH])
        w_router = sb("w_router", [P, KT, E])
        b_router = sb("b_router", [P, E])
        small = sb("small", [P, 176])
        used = [0]

        def col(n):
            used[0] += n
            return small[:, used[0] - n:used[0]]

        exponent = col(TT * HEADS)
        sq_sum = col(4 * TT)
        var = col(TT)
        rstd = col(TT)
        lam_s = col(2)
        lam_e = col(2)
        neg_lam = col(1)
        nmax = col(8)
        psum_s = col(8)
        prec = col(8)
        var16 = col(16)
        rstd16 = col(16)
        gates = col(TT * 2 * MH).rearrange("p (t g) -> p t g", t=TT)
        f_abs = col(TT * MH).rearrange("p (t g) -> p t g", t=TT)
        f_exp = col(TT * MH).rearrange("p (t g) -> p t g", t=TT)
        logf = col(TT * MH).rearrange("p (t g) -> p t g", t=TT)
        cumf = col(TT * MH).rearrange("p (t g) -> p t g", t=TT)
        a_col = col(TT * MH).rearrange("p (t g) -> p t g", t=TT)
        run_max = col(TT)
        neg_m = col(TT)
        m_sum = col(TT)
        e_m = col(TT)
        den = col(TT)
        rden = col(TT)
        mean_var = col(TT * 2).rearrange("p (t g) -> p t g", t=TT)
        iota8 = slot_iota[:, 0:E]
        rt = sb("rt", [P, TT, 12, E])
        top_i = sb("top_i", [P, TT, E], U32)
        counts = sb("counts", [P, E], I32)
        per_e = sb("per_e", [P, E, 6])
        cur = sb("cur", [P, 6])
        arena = sb("arena", [P, 17712])
        at = [0]

        def area(n, first=None):
            if first is not None:
                at[0] = first
            at[0] += n
            assert at[0] <= 17712, at[0]
            return arena[:, at[0] - n:at[0]]

        xn = area(2048, 0).rearrange("p (t d) -> p t d", t=TT)
        junk = lambda i: xn[:, i // 2, (i % 2) * 512:(i % 2 + 1) * 512]
        mod_acc = area(1024).rearrange("p (b n) -> p b n", b=2)
        mod_rows = area(P)
        after_acc = at[0]
        rows = area(3 * P, after_acc).rearrange("p (r n) -> p r n", r=3)
        qT = area(2048, after_acc + 3 * P).rearrange("p (k s) -> p k s", k=KT)
        kT = area(2048).rearrange("p (k s) -> p k s", k=KT)
        v_nat = area(2048).rearrange("p (t d) -> p t d", t=TT)
        o_nat = area(2048).rearrange("p (t d) -> p t d", t=TT)
        probs = area(2 * 2 * 384).rearrange("p (b c n) -> p b c n", b=2, c=2)
        aT = area(2 * 384).rearrange("p (b n) -> p b n", b=2)
        oT = area(2048).rearrange("p (k s) -> p k s", k=KT)
        dist = area(384)
        lam_in = area(4 * DA).rearrange("p (i n) -> p i n", i=4)
        hid = area(FT * S, after_acc).rearrange("p (k s) -> p k s", k=FT)
        PAD = CONV - 1
        xm = area(IT * (S + PAD), 0).rearrange("p (k s) -> p k s", k=IT)
        xc = area(IT * S).rearrange("p (k s) -> p k s", k=IT)
        k_in = area(IT * S).rearrange("p (k s) -> p k s", k=IT)
        v_in = area(TT * INNER).rearrange("p (t d) -> p t d", t=TT)
        vT2 = area(2 * S).rearrange("p (b s) -> p b s", b=2)
        m_share = at[0]
        bd = area(2 * 3 * P, m_share).rearrange("p (b m o) -> p b m o", b=2, m=3)
        dw = area(2 * 384, m_share).rearrange("p (b n) -> p b n", b=2)
        gates_T = area(S, m_share)
        diag_m = area(512, m_share)
        xg = area(KT * S, 2048).rearrange("p (k s) -> p k s", k=KT)
        eh = area(ET * S).rearrange("p (k s) -> p k s", k=ET)
        ye = area(TT * D).rearrange("p (t d) -> p t d", t=TT)
        hx = ye
        y_sum = area(TT * D).rearrange("p (t d) -> p t d", t=TT)
        scat = area(TT * S).rearrange("p (t s) -> p t s", t=TT)
        sel = area(TT * S).rearrange("p (t s) -> p t s", t=TT)
        selw = area(TT * S).rearrange("p (t s) -> p t s", t=TT)
        bn6 = sb("bn6", [P, TT, 6])

        ps = ctx.enter_context(nc.psum_tensor("ps", [P, 8, 512], F32))

        cA, cB, cC = 0, P, 2 * P
        conv_w = lambda j, t: vecs[:, cA + j * IT + t:cA + j * IT + t + 1]
        conv_b = lambda t: vecs[:, cA + 64 + t:cA + 65 + t]
        skip = lambda t: vecs[:, cA + 80 + t:cA + 81 + t]
        norm_m = lambda t: vecs[:, cA + 96 + t:cA + 97 + t]
        c_cols = vecs[:, cB:cB + KT]
        norm_g = lambda layer, i: vecs[:, cB + 8 + (layer * 4 + i) * KT:cB + 8 + (layer * 4 + i + 1) * KT]
        subln = vecs[:, cB + 72:cB + 73]
        mod_b = vecs[:, cC:cC + 96].rearrange("p (l n) -> p l n", l=2)

        consts = sem("consts")
        x_loaded = sem("x_loaded")
        rows_loaded = sem("rows_loaded")
        rows_clear = sem("rows_clear")
        lam_loaded = sem("lam_loaded")
        small_loaded = sem("small_loaded")
        landed = [sem(f"landed{s}") for s in range(SLOTS)]
        pe_read = sem("pe_read")
        freed = sem("freed")
        u_full = sem("u_full")
        u_free = sem("u_free")
        dstep = sem("dstep")
        astep = sem("astep")
        pstep = sem("pstep")
        cond_ready = sem("cond_ready")
        acc_ready = sem("acc_ready")
        mod_summed = sem("mod_summed")
        mod_rows_ready = sem("mod_rows_ready")
        mod_turned = sem("mod_turned")
        x_new = sem("x_new")
        sq_ready = sem("sq_ready")
        var_ready = sem("var_ready")
        rstd_ready = sem("rstd_ready")
        xn_ready = sem("xn_ready")
        diag_ready = sem("diag_ready")
        y_full = sem("y_full")
        t_free = sem("t_free")
        lam_ready = sem("lam_ready")
        maxed = sem("maxed")
        probs_ready = sem("probs_ready")
        a_ready = sem("a_ready")
        aT_full = sem("aT_full")
        aT_ready = sem("aT_ready")
        o_full = sem("o_full")
        o_ready = sem("o_ready")
        on_ready = sem("on_ready")
        silu_ready = sem("silu_ready")
        conv_ready = sem("conv_ready")
        xc_ready = sem("xc_ready")
        bd_ready = sem("bd_ready")
        gates_full = sem("gates_full")
        gates_T_clear = sem("gates_T_clear")
        gates_T_ready = sem("gates_T_ready")
        logf_in = sem("logf_in")
        logf_ln = sem("logf_ln")
        logf_ready = sem("logf_ready")
        cum_full = sem("cum_full")
        rmax_ready = sem("rmax_ready")
        dw_ready = sem("dw_ready")
        m_out_ready = sem("m_out_ready")
        num_full = sem("num_full")
        hh_ready = sem("hh_ready")
        logits_full = sem("logits_full")
        route = sem("route")
        counts_ready = sem("counts_ready")
        sel_ready = sem("sel_ready")
        scat_full = sem("scat_full")
        scat_ready = sem("scat_ready")
        ye_ready = sem("ye_ready")
        spread = sem("spread")
        y_added = sem("y_added")
        stored = sem("stored")

        def z_in(h):
            return xm[:, MK * h:MK * (h + 1), PAD:PAD + S]

        def head_weights(h):
            k = k_in[:, MK * h:MK * (h + 1), :].rearrange("p k s -> p (k s)")
            return k[:, 0:384], k[:, 384:768]

        def weights(matrix, first, n):
            if matrix.startswith("mod"):
                w = a["mod_w"][int(matrix[3])]
            else:
                w = {"attn_in": a["attn_w_in"], "attn_out": a["attn_w_out"], "gate": a["ffn_w_gate"],
                     "up": a["ffn_w_up"], "down": a["ffn_w_down"], "mlstm_in": a["mlstm_w_in"],
                     "mlstm_out": a["mlstm_w_out"]}[matrix][0]
            if matrix in ("attn_out", "down", "mlstm_out"):
                return w.rearrange("(k p) n -> p k n", p=P)[:, first:first + n, :]
            return w.rearrange("(k p) n -> p k n", p=P)[:, :, first:first + n]

        def slot_up(s, n=WC):
            return ring[:, s, 0:KT * n].rearrange("p (k n) -> p k n", n=n)

        def slot_down(s, k=DK):
            return ring[:, s, 0:k * D].rearrange("p (k n) -> p k n", n=D)

        order = {(m, f): i for i, (m, f, n, r) in enumerate(PLAN)}
        read_by = []
        n_mod = n_down = n_y = 0
        for m, f, n, r in PLAN:
            j = f // WC
            if r == "dve":
                n_mod += 1
                read_by.append((acc_ready, n_mod))
            elif m == "attn_in":
                read_by.append((u_full, FILLS["attn"] + 2 * (j + 1)))
            elif m in ("gate", "up"):
                read_by.append((u_full, FILLS["ffn"] + min(4 * (j + 1), FT)))
            elif m == "mlstm_in":
                read_by.append((u_full, FILLS["x_m"] + 2 * (j + 1) if j < 4 else fills_after_z(j - 4)))
            elif f + n == {"attn_out": KT, "down": FT, "mlstm_out": IT}[m]:
                n_y += 1
                read_by.append((y_full, n_y))
            else:
                n_down += 1
                read_by.append((pe_read, n_down))

        def wait_chunk(eng, i):
            eng.wait_ge(landed[i % SLOTS], 16 * (i // SLOTS + 1))

        def expert_chunk(sp, e, c):
            s = c % SLOTS
            n_up = 2 * (FE // WC)
            if c < n_up:
                w = a["moe_w_gate"] if c % 2 == 0 else a["moe_w_up"]
                src = w[0][e].rearrange("(k p) n -> p k n", p=P)[:, :, (c // 2) * WC:(c // 2 + 1) * WC]
                sp.dma_start(slot_up(s), src).then_inc(landed[s], 16)
            else:
                j = c - n_up
                src = a["moe_w_down"][0][e].rearrange("(k p) n -> p k n", p=P)[:, j * DK:(j + 1) * DK, :]
                sp.dma_start(slot_down(s), src).then_inc(landed[s], 16)

        def sp_program(sp):
            sp.wait_ge(rows_clear, 1)
            cw = a["mlstm_conv_w"][0]
            sp.dma_start(rows[0:64, 0, :], cw.rearrange("j (t p) -> (j t) p", p=P)).then_inc(rows_loaded, 16)
            sp.dma_start(rows[64:80, 0, :], a["mlstm_conv_b"][0].rearrange("(t p) -> t p", p=P)).then_inc(rows_loaded, 16)
            sp.dma_start(rows[80:96, 0, :], a["mlstm_skip"][0].rearrange("(t p) -> t p", p=P)).then_inc(rows_loaded, 16)
            sp.dma_start(rows[96:112, 0, :], a["mlstm_norm"][0].rearrange("(t p) -> t p", p=P)).then_inc(rows_loaded, 16)
            sp.dma_start(rows[0:8, 1, :], a["c"][0].rearrange("(t p) -> t p", p=P)).then_inc(rows_loaded, 16)
            sp.dma_start(rows[8:72, 1, :], a["norm_g"].rearrange("l i (t p) -> (l i t) p", p=P)).then_inc(rows_loaded, 16)
            sp.dma_start(rows[72:73, 1, :], a["attn_subln"]).then_inc(rows_loaded, 16)
            sp.dma_start(rows[0:96, 2, :], a["mod_b"].rearrange("l (t p) -> (l t) p", p=P)).then_inc(rows_loaded, 16)
            sp.dma_start(x[:], a["x"][0].rearrange("(t p) d -> p t d", p=P)).then_inc(x_loaded, 16)
            for i, (m, f, n, r) in enumerate(PLAN):
                if i >= SLOTS:
                    sp.wait_ge(*read_by[i - SLOTS])
                dst = slot_down(i % SLOTS, n) if m in ("attn_out", "down", "mlstm_out") else slot_up(i % SLOTS, n)
                sp.dma_start(dst, weights(m, f, n)).then_inc(landed[i % SLOTS], 16)
            with sp.Fori(0, E) as e:
                for c in range(EC):
                    sp.wait_ge(freed, e * EC + (c + 1))
                    expert_chunk(sp, e, c)
            sp.wait_ge(x_new, 4)
            sp.dma_start(out[0].rearrange("(t p) d -> p t d", p=P), x[:]).then_inc(stored, 16)
            sp.wait_ge(stored, 16)

        def pool_program(pool):
            steps = Count()

            def link(ins):
                ins.then_inc(pstep, 1)
                pool.wait_ge(pstep, steps.next())

            pool.memset(rows, 0.0).then_inc(rows_clear, 1)
            pool.memset(exponent, -0.5)
            pool.memset(ones[:], 1.0)
            pool.memset(ident[:], 0.0)
            pool.memset(ones_col[:, 0:31], 0.0)
            pool.memset(ones_col[:, 31:32], 1.0)
            pool.memset(ones_col[:, 32:63], 0.0)
            pool.memset(tri[:], 1.0)
            pool.memset(tri_strict[:], 1.0)
            pool.memset(causal[:], 0.0)
            link(pool.memset(block4[:], 1.0))
            pool.affine_select(out=ident[:], in_=ident[:], compare_op=ALU.not_equal, fill=1.0, base=0,
                               pattern=[[-1, P]], channel_multiplier=1)
            pool.affine_select(out=tri[:], in_=tri[:], compare_op=ALU.is_ge, fill=0.0, base=0,
                               pattern=[[1, P]], channel_multiplier=-1)
            pool.affine_select(out=tri_strict[:], in_=tri_strict[:], compare_op=ALU.is_gt, fill=0.0, base=0,
                               pattern=[[1, P]], channel_multiplier=-1)
            pool.affine_select(out=causal[:], in_=causal[:], compare_op=ALU.is_ge, fill=-BIG, base=0,
                               pattern=[[-1, P]], channel_multiplier=1)
            link(pool.affine_select(out=block4[:], in_=block4[:], compare_op=ALU.is_ge, fill=0.0, base=0,
                                    pattern=[[-4, P // 4]], channel_multiplier=1))
            pool.affine_select(out=block4[:], in_=block4[:], compare_op=ALU.is_ge, fill=0.0, base=3,
                               pattern=[[4, P // 4]], channel_multiplier=-1)
            pool.iota(slot_iota[:], pattern=[[1, S]], base=0, channel_multiplier=0,
                      allow_small_or_imprecise_dtypes=True)
            pool.iota(dist[:, 0:P], pattern=[[1, P]], base=0, channel_multiplier=-1,
                      allow_small_or_imprecise_dtypes=True)
            pool.iota(dist[:, P:3 * P], pattern=[[1, S]], base=-P, channel_multiplier=-1,
                      allow_small_or_imprecise_dtypes=True).then_inc(consts, 1)

            def power(n, src, dst, width):
                pool.wait_ge(var_ready, n)
                pool.tensor_tensor(dst, src, exponent[:, 0:width], ALU.pow).then_inc(rstd_ready, 1)

            power(1, var, rstd, TT)
            power(2, var16, rstd16, TT * HEADS)
            for n in range(3, 7):
                power(n, var, rstd, TT)
            pool.wait_ge(u_free, FILLS["x_m"])
            pool.memset(xm[:, :, 0:PAD], 0.0).then_inc(consts, 1)
            pool.wait_ge(small_loaded, 16 * 7)
            for t in range(IT):
                if t >= 2:
                    pool.wait_ge(gates_full, t - 1)
                pool.tensor_tensor(
                    bd[:, t % 2].rearrange("p m (g o) -> p m g o", o=4),
                    qkv_blocks[:, :, t, :].unsqueeze(2).broadcast_to([P, 3, P // 4, 4]),
                    block4[:].unsqueeze(1).unsqueeze(3).broadcast_to([P, 3, P // 4, 4]),
                    ALU.mult).then_inc(bd_ready, 1)
            for h in range(MH):
                power(7 + h, var, rstd, TT)
            for n in range(11, 14):
                power(n, var, rstd, TT)

        def act_program(act):
            steps = Count()

            def link(ins):
                ins.then_inc(astep, 1)
                act.wait_ge(astep, steps.next())

            act.dma_start(lam_in[:], a["attn_lambda"][0].unsqueeze(0).broadcast_to([P, 4, DA])).then_inc(lam_loaded, 16)
            def squares_x(n):
                if n == 0:
                    act.wait_ge(x_loaded, 16)
                else:
                    act.wait_ge(x_new, n)
                for t in range(TT):
                    ins = act.activation(xn[:, t], x[:, t], ACT.Square, accum_out=sq_sum[:, t:t + 1])
                ins.then_inc(sq_ready, 1)

            def normed_x(n, powers):
                act.wait_ge(rstd_ready, powers)
                for t in range(TT):
                    ins = act.activation(xn[:, t], x[:, t], ACT.Copy, scale=rstd[:, t:t + 1])
                ins.then_inc(xn_ready, 1)

            def squares_y(n):
                if n < 3:
                    act.wait_ge(y_full, n)
                else:
                    act.wait_ge(freed, SLOTS)
                for i in range(4):
                    ins = act.activation(junk(i), ps[:, 4 + i], ACT.Square, accum_out=sq_sum[:, i:i + 1])
                ins.then_inc(sq_ready, 1)

            act.wait_ge(u_free, 1)
            act.activation(cond[:], c_cols, ACT.Silu).then_inc(cond_ready, 1)
            for m, name in enumerate(("mlstm_w_q", "mlstm_w_k", "mlstm_w_v")):
                act.dma_start(qkv_blocks[:, m], a[name][0].rearrange("(t g) i o -> (g i) t o", g=P // 4)).then_inc(small_loaded, 16)
            act.dma_start(w_gates[:], a["mlstm_w_gate"][0].rearrange("(k p) n -> p k n", p=P)).then_inc(small_loaded, 16)
            act.dma_start(b_gates[:], a["mlstm_b_gate"].broadcast_to([P, 2 * MH])).then_inc(small_loaded, 16)
            act.dma_start(w_router[:], a["moe_w_router"][0].rearrange("(k p) n -> p k n", p=P)).then_inc(small_loaded, 16)
            act.dma_start(b_router[:], a["moe_b_router"].broadcast_to([P, E])).then_inc(small_loaded, 16)
            act.wait_ge(lam_ready, 1)
            act.activation(lam_e, lam_s, ACT.Exp).then_inc(lam_ready, 1)
            squares_x(0)
            normed_x(0, 1)

            def exps(h):
                act.wait_ge(maxed, h + 1)
                b = h % 2
                for c in range(2):
                    for q in range(TT):
                        i = b * 4 + c * 2 + q
                        p = probs[:, b, c, 0:P] if q == 0 else probs[:, b, c, P:3 * P]
                        ins = act.activation(p, p, ACT.Exp, bias=nmax[:, i:i + 1], accum_out=psum_s[:, i:i + 1])
                ins.then_inc(probs_ready, 1)

            def move_aT(h):
                act.wait_ge(aT_full, h + 1)
                if h >= 2:
                    act.wait_ge(o_full, h - 1)
                act.activation(aT[:, h % 2], ps[:, 4 + h % 2, 0:384], ACT.Copy).then_inc(aT_ready, 1)

            def move_o(h):
                act.wait_ge(o_full, h + 1)
                act.activation(o_nat[:, :, h * HD:(h + 1) * HD],
                               ps[:, 6 + h % 2, 0:S].rearrange("p (t d) -> p t d", t=TT), ACT.Copy).then_inc(o_ready, 1)

            for h in range(HEADS + 2):
                if h < HEADS:
                    exps(h)
                if 1 <= h <= HEADS:
                    move_aT(h - 1)
                if h >= 2:
                    move_o(h - 2)
            squares_y(1)

            squares_x(1)
            normed_x(1, 4)
            u = FILLS["ffn"]
            for ft in range(FT):
                act.wait_ge(u_full, u + ft + 1)
                act.activation(hid[:, ft, :], ps[:, (u + ft) % UB, 0:S], ACT.Silu).then_inc(silu_ready, 1)
            squares_y(2)

            squares_x(2)
            normed_x(2, 6)
            for j in range(4):
                act.wait_ge(conv_ready, j + 1)
                for t in range(4 * j, 4 * j + 4):
                    ins = act.activation(xc[:, t], xc[:, t], ACT.Silu, bias=conv_b(t))
                ins.then_inc(xc_ready, 1)
            act.wait_ge(logf_in, 1)
            link(act.activation(f_exp, f_abs, ACT.Exp, scale=-1.0))
            act.activation(f_exp, f_exp, ACT.Ln, bias=1.0).then_inc(logf_ln, 1)
            for h in range(MH):
                act.wait_ge(rmax_ready, h + 1)
                b = h % 2
                act.activation(e_m, m_sum, ACT.Exp, scale=-1.0)
                act.activation(dw[:, b, 0:P], dw[:, b, 0:P], ACT.Exp, bias=neg_m[:, 0:1])
                act.activation(dw[:, b, P:3 * P], dw[:, b, P:3 * P], ACT.Exp, bias=neg_m[:, 1:2]).then_inc(dw_ready, 1)
                act.wait_ge(u_free, fills_after_z(h))
                act.activation(z_in(h), z_in(h), ACT.Silu).then_inc(silu_ready, 1)
            squares_y(3)

            squares_x(3)
            normed_x(3, 12)
            act.wait_ge(route, 1)
            act.activation(rt[:, :, 3, 1], rt[:, :, 3, 0], ACT.Exp).then_inc(route, 1)

            act.wait_ge(counts_ready, 1)
            act.wait_ge(hx_ready, 2)
            act.nop().then_inc(silu_moe, 2)
            act.nop().then_inc(turn_free, 2)

            def expert(e, width):
                tiles, sw = shape_of(width)
                act.wait_ge(scat_full, e + 1)
                act.activation(scat[:, 0:tiles, :],
                               ps[:, 4, 0:tiles * S].rearrange("p (t s) -> p t s", t=tiles), ACT.Copy).then_inc(scat_ready, 1)
                if tiles == 1:
                    for j in range(EJ + 1):
                        if j < EJ:
                            act.wait_ge(step_full, step_count(e, j))
                            if j >= 2:
                                act.wait_ge(turn_full, step_count(e, j - 2))
                            act.activation(hx[0:width, j % 2, 0:WC], ps[0:width, 2 * (j % 2)], ACT.Silu).then_inc(silu_moe, STEP)
                        if j:
                            m = j - 1
                            act.wait_ge(turn_full, step_count(e, m))
                            act.activation(eh[:, STEP * m:STEP * j, 0:width],
                                           ps[:, 6 + m % 2].rearrange("p (c s) -> p c s", c=STEP)[:, :, 0:width],
                                           ACT.Copy).then_inc(turn_free, STEP)
                else:
                    for ft in range(ET):
                        act.wait_ge(step_full, ft_count(e, ft))
                        act.activation(eh[:, ft, 0:width], ps[:, ft % UB, 0:width], ACT.Silu).then_inc(silu_moe, 1)
                    act.nop().then_inc(turn_free, ET)
                act.wait_ge(freed, e * EC + (SLOTS + EC))
                for st in range(tiles):
                    for n in range(2):
                        r = second_half(sw[st]) if n else slice(0, sw[st])
                        src = ps[r, 4 + 2 * st + n]
                        ins = act.activation(ye[0:sw[st], st, n * 512:(n + 1) * 512], src, ACT.Copy)
                ins.then_inc(ye_ready, 1)

            with act.Fori(0, E) as e:
                by_width(act, e, expert)
            act.wait_ge(y_added, 1 + E)
            for t in range(TT):
                ins = act.activation(xn[:, t], y_sum[:, t], ACT.Square, accum_out=sq_sum[:, t:t + 1])
            ins.then_inc(sq_ready, 1)

        def shape_of(width):
            return (width + P - 1) // P, [min(width - t, P) for t in range(0, width, P)]

        def second_half(sw):
            return slice(P // 2, P // 2 + sw) if sw <= P // 2 else slice(0, sw)

        def ft_count(e, ft):
            return e * ET + (2 + ft + 1)

        def step_count(e, j):
            return ft_count(e, STEP * j + STEP - 1)

        def by_width(eng, e, body):
            n = eng.value_load(counts[0:1, bass.ds(e, 1)], min_val=0, max_val=S)

            def choose(widths):
                if len(widths) == 1:
                    body(e, widths[0])
                    return
                half = len(widths) // 2
                with eng.If(n > widths[half - 1]):
                    choose(widths[half:])
                    eng.nop()
                with eng.Else():
                    choose(widths[:half])
                    eng.nop()

            choose(WIDTHS)

        def pe_program(pe):
            u = Count()
            reads = Count()

            def bank():
                n = u.next()
                if n > UB:
                    pe.wait_ge(u_free, n - UB)
                return ps[:, (n - 1) % UB]

            def chunk(m, f, n=WC):
                i = order[(m, f)]
                wait_chunk(pe, i)
                return i

            def mod_sum(layer, j, n):
                pe.wait_ge(acc_ready, n + 1)
                for i in range(4):
                    r = slice(32 * i, 32 * (i + 1))
                    ins = pe.matmul(ps[r, 7, 0:P], ones_col[:, 31 - j:63 - j], mod_acc[:, n % 2, i * P:(i + 1) * P],
                                    start=(j in MOD_PARTS[layer]), stop=(j + 1 in MOD_PARTS[layer]))
                ins.then_inc(mod_summed, 1)

            def mod_turn(n):
                pe.wait_ge(mod_rows_ready, n)
                pe.transpose(ps[:, 6, 0:P], mod_rows, ident[:]).then_inc(mod_turned, 1)

            def transposes_x(n):
                pe.wait_ge(xn_ready, n + 1)
                transposes(xn)

            def transposes(src):
                for i in range(KT // 2):
                    b = bank()
                    for j in range(2):
                        for t in range(TT):
                            k = 2 * i + j
                            ins = pe.transpose(b[:, j * S + t * P:j * S + (t + 1) * P], src[:, t, k * P:(k + 1) * P], ident[:])
                    ins.then_inc(u_full, 1)

            def broadcast_gate(diagonals):
                pe.wait_ge(diag_ready, diagonals)
                for i in range(2):
                    b = bank()
                    pe.matmul(b, ones[:], scratch[:, i * 512:(i + 1) * 512], start=True, stop=True).then_inc(u_full, 1)

            def project(matrix, chunks, lhs, free):
                pe.wait_ge(t_free, free)
                last = chunks[-1][0] + chunks[-1][1] - 1
                for first, n in chunks:
                    i = chunk(matrix, first)
                    w = slot_down(i % SLOTS, n)
                    for k in range(n):
                        for t in range(TT):
                            for c in range(2):
                                ins = pe.matmul(ps[:, 4 + 2 * t + c], lhs[:, first + k, t * P:(t + 1) * P],
                                                w[:, k, c * 512:(c + 1) * 512], start=(first + k == 0), stop=(first + k == last))
                    if matrix == "mlstm_out":
                        ins.then_inc(freed, SLOTS - len(chunks) + 1 if first == 0 else 1)
                    else:
                        ins.then_inc(y_full if first + n - 1 == last else pe_read, 1)

            def up_tile(dst, w, c):
                for k in range(KT):
                    ins = pe.matmul(dst, w[:, k, c * P:(c + 1) * P], hT[:, k, :], start=(k == 0), stop=(k == KT - 1))
                return ins

            pe.wait_ge(consts, 1)
            pe.wait_ge(rows_loaded, 16 * 8)
            b = bank()
            for r in range(3):
                ins = pe.transpose(b[:, r * P:(r + 1) * P], rows[:, r, :], ident[:])
            ins.then_inc(u_full, 1)
            mods = 0
            for j in range(4):
                mod_sum(0, j, mods)
                mods += 1
            mod_turn(1)
            transposes_x(0)

            pe.wait_ge(u_free, u.n)
            after = {0: [4, 5], 1: [6], 2: [7, 8], 3: [9], 4: [10], 5: [11]}
            for j in range(6):
                i = chunk("attn_in", j * WC)
                w = slot_up(i % SLOTS)
                for g in range(2):
                    b = bank()
                    if j < 4:
                        for c in range(2):
                            ins = up_tile(b[:, c * S:(c + 1) * S], w, 2 * g + c)
                    else:
                        for k in range(KT):
                            ins = pe.matmul(b, hT[:, k, g * P:(g + 1) * P], w[:, k, :], start=(k == 0), stop=(k == KT - 1))
                    ins.then_inc(u_full, 1)
                if j:
                    for m in after[j - 1]:
                        mod_sum(0, m, mods)
                        mods += 1
            for m in after[5]:
                mod_sum(0, m, mods)
                mods += 1
            mod_turn(2)
            pe.wait_ge(u_free, u.n)
            pe.wait_ge(t_free, 2)

            def scores(h):
                for c in range(2):
                    b = bank()
                    r = slice(DA * c, DA * (c + 1))
                    pe.matmul(b[:, 0:P], qT[r, h, 0:P], kT[r, h, 0:P], start=True, stop=True)
                    pe.matmul(b[:, P:3 * P], qT[r, h, P:2 * P], kT[r, h, :], start=True, stop=True).then_inc(u_full, 1)

            def turn(h):
                pe.wait_ge(a_ready, h + 1)
                if h >= 2:
                    pe.wait_ge(aT_ready, h - 1)
                for i in range(3):
                    ins = pe.transpose(ps[:, 4 + h % 2, i * P:(i + 1) * P], probs[:, h % 2, 0, i * P:(i + 1) * P], ident[:])
                ins.then_inc(aT_full, 1)

            def values(h):
                pe.wait_ge(aT_ready, h + 1)
                if h >= 2:
                    pe.wait_ge(o_ready, h - 1)
                w = slice(h * HD, (h + 1) * HD)
                b = ps[:, 6 + h % 2]
                pe.matmul(b[:, 0:P], aT[:, h % 2, 0:P], v_nat[:, 0, w], start=True, stop=True)
                pe.matmul(b[:, P:2 * P], aT[:, h % 2, P:2 * P], v_nat[:, 0, w], start=True, stop=False)
                pe.matmul(b[:, P:2 * P], aT[:, h % 2, 2 * P:3 * P], v_nat[:, 1, w], start=False, stop=True).then_inc(o_full, 1)

            scores(0)
            for h in range(HEADS + 2):
                if h + 1 < HEADS:
                    scores(h + 1)
                if 1 <= h <= HEADS:
                    turn(h - 1)
                if h >= 2:
                    values(h - 2)
            broadcast_gate(1)
            pe.wait_ge(on_ready, 1)
            transposes(o_nat)
            pe.wait_ge(u_free, u.n)
            pe.wait_ge(o_ready, HEADS)
            project("attn_out", [(k, DK) for k in range(0, KT, DK)], oT, 2)

            transposes_x(1)
            pe.wait_ge(u_free, u.n)
            assert u.n == FILLS["ffn"], u.n
            pe.wait_ge(t_free, 3)
            for j in range(6):
                n = min(WC, FF - j * WC)
                ig, iu = chunk("gate", j * WC), chunk("up", j * WC)
                wg, wu = slot_up(ig % SLOTS, n), slot_up(iu % SLOTS, n)
                for c in range(n // P):
                    b = bank()
                    up_tile(b[:, 0:S], wg, c)
                    ins = up_tile(b[:, S:2 * S], wu, c)
                    ins.then_inc(u_full, 1)
                if j:
                    for m in (2 * j - 2, 2 * j - 1):
                        mod_sum(1, m, mods)
                        mods += 1
            for m in (10, 11):
                mod_sum(1, m, mods)
                mods += 1
            mod_turn(3)
            broadcast_gate(2)
            pe.wait_ge(u_free, u.n - 2)
            first = 0
            chunks = []
            for n in [4, 4, 4, 4, 2, 2, 2]:
                chunks.append((first, n))
                first += n
            project("down", chunks, hid, 4)

            transposes_x(2)
            pe.wait_ge(u_free, u.n)

            def mlstm_in(j):
                i = chunk("mlstm_in", j * WC)
                w = slot_up(i % SLOTS)
                for g in range(2):
                    b = bank()
                    for c in range(2):
                        ins = up_tile(b[:, c * S:(c + 1) * S], w, 2 * g + c)
                    ins.then_inc(u_full, 1)

            for j in range(4):
                mlstm_in(j)

            def gate_products(t):
                pe.wait_ge(u_free, FILLS["qkv"] + 2 * (t + 1))
                if t == 0:
                    pe.wait_ge(small_loaded, 16 * 7)
                    pe.wait_ge(t_free, 5)
                for m, src in enumerate((xm[:, t, PAD:PAD + S], k_in[:, t], vT2[:, t % 2])):
                    ins = pe.matmul(ps[32 * m:32 * m + 2 * MH, 4 + m, 0:S], w_gates[:, m * IT + t, :], src,
                                    start=(t == 0), stop=(t == IT - 1))
                ins.then_inc(gates_full, 1)

            for t in range(IT):
                pe.wait_ge(xc_ready, t // 4 + 1)
                pe.wait_ge(bd_ready, t + 1)
                blocks = bd[:, t % 2]
                xt = xm[:, t, PAD:PAD + S]
                b = bank()
                pe.matmul(b[:, 0:S], blocks[:, 2], xt, start=True, stop=True)
                pe.matmul(b[:, S:S + P], xt[:, 0:P], blocks[:, 2], start=True, stop=True)
                pe.matmul(b[:, S + P:2 * S], xt[:, P:S], blocks[:, 2], start=True, stop=True).then_inc(u_full, 1)
                b = bank()
                pe.matmul(b[:, 0:S], blocks[:, 0], xc[:, t], start=True, stop=True)
                pe.matmul(b[:, S:2 * S], blocks[:, 1], xc[:, t], start=True, stop=True).then_inc(u_full, 1)
                if t:
                    gate_products(t - 1)
            gate_products(IT - 1)
            pe.wait_ge(gates_T_ready, 1)
            for t in range(TT):
                ins = pe.matmul(ps[:, 7, t * 2 * MH:(t + 1) * 2 * MH], gates_T[:, t * P:(t + 1) * P], eight[:], start=True, stop=True)
            ins.then_inc(gates_full, 1)
            pe.wait_ge(logf_ready, 1)
            pe.matmul(ps[:, 6, 0:MH], tri[:], logf[:, 0], start=True, stop=True)
            pe.matmul(ps[:, 6, MH:2 * MH], ones[:], logf[:, 0], start=True, stop=False)
            pe.matmul(ps[:, 6, MH:2 * MH], tri[:], logf[:, 1], start=False, stop=True).then_inc(cum_full, 1)
            for t in range(TT):
                pe.wait_ge(diag_ready, 3 + t)
                pe.matmul(ps[:, 4 + t], ones[:], diag_m, start=True, stop=True).then_inc(cum_full, 1)

            def m_scores(h):
                b = bank()
                for k in range(MK):
                    pe.matmul(b[:, 0:P], xm[:, MK * h + k, PAD:PAD + P], k_in[:, MK * h + k, 0:P],
                              start=(k == 0), stop=(k == MK - 1))
                for k in range(MK):
                    ins = pe.matmul(b[:, P:3 * P], xm[:, MK * h + k, PAD + P:PAD + S], k_in[:, MK * h + k, :],
                                    start=(k == 0), stop=(k == MK - 1))
                ins.then_inc(u_full, 1)

            def m_values(h, scored):
                w, wT = head_weights(h)
                pe.wait_ge(u_free, scored)
                b = bank()
                for i in range(3):
                    ins = pe.transpose(b[:, i * P:(i + 1) * P], w[:, i * P:(i + 1) * P], ident[:])
                ins.then_inc(u_full, 1)
                pe.wait_ge(u_free, u.n)
                c = slice(h * MD, (h + 1) * MD)
                pe.matmul(ps[:, 6], wT[:, 0:P], v_in[:, 0, c], start=True, stop=True)
                pe.matmul(ps[:, 7], wT[:, P:2 * P], v_in[:, 0, c], start=True, stop=False)
                pe.matmul(ps[:, 7], wT[:, 2 * P:3 * P], v_in[:, 1, c], start=False, stop=True).then_inc(num_full, 1)

            def m_turn(h):
                pe.wait_ge(hh_ready, h + 1)
                for g in range(2):
                    b = bank()
                    for c in range(2):
                        for t in range(TT):
                            k = MK * h + 2 * g + c
                            ins = pe.transpose(b[:, c * S + t * P:c * S + (t + 1) * P], v_in[:, t, k * P:(k + 1) * P], ident[:])
                    ins.then_inc(u_full, 1)

            for h in range(MH):
                m_scores(h)
                scored = u.n
                mlstm_in(4 + h)
                if h:
                    m_turn(h - 1)
                m_values(h, scored)
            m_turn(MH - 1)
            broadcast_gate(5)
            pe.wait_ge(m_out_ready, MH)
            project("mlstm_out", [(k, DK) for k in range(0, IT, DK)], xc, 5)

            transposes_x(3)
            pe.wait_ge(u_free, u.n)
            pe.wait_ge(t_free, 6)
            for t in range(TT):
                for k in range(KT):
                    ins = pe.matmul(ps[:, 4 + t, 0:E], hT[:, k, t * P:(t + 1) * P], w_router[:, k, :],
                                    start=(k == 0), stop=(k == KT - 1))
            ins.then_inc(logits_full, 1)
            pe.wait_ge(route, 3)
            chosen = lambda t: rt[:, t, 6, :]
            b = ps[:, 6]
            pe.matmul(b[:, 0:E], tri_strict[:], chosen(0), start=True, stop=True)
            pe.matmul(b[:, E:2 * E], ones[:], chosen(0), start=True, stop=False)
            pe.matmul(b[:, E:2 * E], tri_strict[:], chosen(1), start=False, stop=True)
            pe.matmul(b[:, 2 * E:3 * E], ones[:], chosen(0), start=True, stop=False)
            pe.matmul(b[:, 2 * E:3 * E], ones[:], chosen(1), start=False, stop=True).then_inc(logits_full, 1)
            broadcast_gate(6)
            assert u.n == FILLS["moe"], u.n

            def expert(e, width):
                tiles, sw = shape_of(width)
                wide = max(width, P)

                def arrived(c):
                    pe.wait_ge(landed[c % SLOTS], e * (16 * EC // SLOTS) + 16 * (PRE_USES + c // SLOTS + 1))

                pe.wait_ge(sel_ready, e + 1)
                pe.wait_ge(y_added, e + 1)
                for st in range(tiles):
                    for t in range(TT):
                        ins = pe.transpose(ps[:, 4, st * S + t * P:st * S + (t + 1) * P],
                                           selw[:, t, st * P:(st + 1) * P], ident[:])
                ins.then_inc(scat_full, 1)
                for i in range(KT // 2):
                    for j in range(2):
                        k = 2 * i + j
                        for t in range(TT):
                            ins = pe.matmul(ps[:, i, j * S:j * S + wide], xn[:, t, k * P:(k + 1) * P], sel[:, t, 0:wide],
                                            start=(t == 0), stop=(t == TT - 1))
                    ins.then_inc(gather_full, 1)
                pe.wait_ge(xg_ready, e + 1)

                def step(j):
                    arrived(2 * j)
                    arrived(2 * j + 1)
                    if j >= 2:
                        pe.wait_ge(hx_ready, step_count(e, j - 2))
                    wg, wu = slot_up((2 * j) % SLOTS), slot_up((2 * j + 1) % SLOTS)
                    b = 2 * (j % 2)
                    low = second_half(width)
                    for k in range(KT):
                        x_k = xg[:, k, 0:width]
                        pe.matmul(ps[0:width, b], x_k, wg[:, k, :], start=(k == 0), stop=(k == KT - 1))
                        ins = pe.matmul(ps[low, b + 1], x_k, wu[:, k, :], start=(k == 0), stop=(k == KT - 1))
                    ins.then_inc(step_full, STEP)

                def turn(j, chunks_read):
                    pe.wait_ge(hx_ready, step_count(e, j))
                    if j >= 2:
                        pe.wait_ge(turn_free, step_count(e, j - 2))
                    for c in range(STEP):
                        ins = pe.transpose(ps[:, 6 + j % 2, c * P:(c + 1) * P], hx[:, j % 2, c * P:(c + 1) * P], ident[:])
                        if c == 0 and chunks_read:
                            ins.then_inc(freed, chunks_read)
                    ins.then_inc(turn_full, STEP)

                def hidden_tile(ft):
                    j, c = ft // STEP, ft % STEP
                    if c == 0:
                        arrived(2 * j)
                        arrived(2 * j + 1)
                    if ft >= UB:
                        pe.wait_ge(hx_ready, ft_count(e, ft - UB))
                    for half in range(2):
                        w = slot_up((2 * j + half) % SLOTS)
                        dst = ps[:, ft % UB, half * S:half * S + width]
                        for k in range(KT):
                            ins = pe.matmul(dst, w[:, k, c * P:(c + 1) * P], xg[:, k, 0:width], start=(k == 0), stop=(k == KT - 1))
                            if half == 0 and k == 0 and c == 0 and j:
                                ins.then_inc(freed, 2)
                    ins.then_inc(step_full, 1)

                if tiles == 1:
                    for j in range(EJ + 1):
                        if j < EJ:
                            step(j)
                        if j:
                            turn(j - 1, 0 if j == EJ else 4 if j == 1 else 2)
                    pe.wait_ge(scat_ready, e + 1)
                    pe.wait_ge(turn_free, step_count(e, EJ - 1))
                else:
                    for ft in range(ET):
                        hidden_tile(ft)
                    pe.nop().then_inc(turn_full, ET)
                    pe.wait_ge(scat_ready, e + 1)
                    pe.wait_ge(hx_ready, ft_count(e, ET - 1))
                for j in range(ET // DK):
                    c = 2 * EJ + j
                    arrived(c)
                    w = slot_down(c % SLOTS)
                    for st in range(tiles):
                        for k in range(DK):
                            ft = DK * j + k
                            for n in range(2):
                                r = second_half(sw[st]) if n else slice(0, sw[st])
                                ins = pe.matmul(ps[r, 4 + 2 * st + n], eh[:, ft, st * P:st * P + sw[st]],
                                                w[:, k, n * 512:(n + 1) * 512], start=(ft == 0), stop=(ft == ET - 1))
                                if tiles == 2 and ft == st == n == 0:
                                    ins.then_inc(freed, 2)
                    ins.then_inc(freed, 1)
                pe.wait_ge(ye_ready, e + 1)
                for t in range(TT):
                    for n in range(2):
                        for st in range(tiles):
                            ins = pe.matmul(ps[:, 4 + 2 * t + n], scat[0:sw[st], st, t * P:(t + 1) * P],
                                            ye[0:sw[st], st, n * 512:(n + 1) * 512], start=(st == 0), stop=(st == tiles - 1))
                ins.then_inc(spread, 1)

            pe.wait_ge(u_free, u.n)
            pe.nop().then_inc(step_full, 2)
            pe.nop().then_inc(turn_full, 2)
            pe.wait_ge(counts_ready, 1)
            with pe.Fori(0, E) as e:
                by_width(pe, e, expert)

        def dve_program(dve):
            steps = Count()
            u = Count()
            powers = Count()
            xs = Count()
            t_reads = [3, 5, 6, 7]

            def link(ins):
                ins.then_inc(dstep, 1)
                dve.wait_ge(dstep, steps.next())

            def full():
                n = u.next()
                dve.wait_ge(u_full, n)
                return ps[:, (n - 1) % UB]

            def mod_chunk(layer, j, n):
                i = order[(f"mod{layer}", j * WC)]
                wait_chunk(dve, i)
                if n >= 2:
                    dve.wait_ge(mod_summed, n - 1)
                w = slot_up(i % SLOTS)
                acc = mod_acc[:, n % 2]
                link(dve.tensor_scalar(acc, w[:, 0], cond[:, 0:1], None, ALU.mult))
                for k in range(1, KT):
                    ins = dve.scalar_tensor_tensor(out=acc, in0=w[:, k], scalar=cond[:, k:k + 1], in1=acc,
                                                   op0=ALU.mult, op1=ALU.add)
                    if k < KT - 1:
                        link(ins)
                ins.then_inc(acc_ready, 1)

            def modulation(n, first, last):
                layer = n // 3
                dve.wait_ge(mod_summed, MOD_ENDS[n - 1])
                dve.tensor_copy(mod_rows, ps[:, 7, 0:P]).then_inc(mod_rows_ready, 1)
                dve.wait_ge(mod_turned, n)
                c = lambda v: v[:, layer, 4 * first:4 * last].rearrange("p (j i) -> p j i", i=4)
                turned = ps[:, 6, 0:P].rearrange("p (i j) -> p j i", i=4)[:, first:last]
                dve.tensor_tensor(c(modc), turned, c(mod_b), ALU.add).then_inc(t_free, 1)
                dve.wait_ge(t_free, (1, 2, 4)[n - 1])

            def emptied(ins):
                return ins.then_inc(u_free, 1)

            def variance(src, n_sums, sq):
                dve.wait_ge(sq_ready, sq)
                if n_sums == 2:
                    link(dve.tensor_tensor(var, sq_sum[:, 0:4:2], sq_sum[:, 1:4:2], ALU.add))
                    src = var
                dve.tensor_scalar(var, src, 1.0 / D, EPS, ALU.mult, ALU.add).then_inc(var_ready, 1)
                powers.next()

            def modulated(n):
                layer, i = n // 2, n % 2
                for g in range(KT // 2):
                    b = full()
                    for j in range(2):
                        k = 2 * g + j
                        ins = dve.tensor_scalar(hT[:, k, :], b[:, j * S:(j + 1) * S], mul_c[:, n, k:k + 1],
                                                modc[:, layer, 24 * i + k:24 * i + k + 1], ALU.mult, ALU.add)
                    emptied(ins)

            def gate_diagonals(n):
                for k in range(KT):
                    ins = dve.tensor_scalar(scratch[:, k * P:(k + 1) * P], ident[:], gate_c[:, n, k:k + 1], None, ALU.mult)
                ins.then_inc(diag_ready, 1)

            def gate_rows():
                for i in range(2):
                    emptied(dve.tensor_copy(gate_bc[:, i * 512:(i + 1) * 512], full()))
                dve.wait_ge(u_free, u.n)

            def add_output(y, in_psum=True):
                dve.wait_ge(rstd_ready, powers.n)
                for t in range(TT):
                    for c in range(2):
                        ins = dve.scalar_tensor_tensor(out=scratch[:, c * 512:(c + 1) * 512], in0=y(t, c),
                                                       scalar=rstd[:, t:t + 1], in1=gate_bc[:, c * 512:(c + 1) * 512],
                                                       op0=ALU.mult, op1=ALU.mult)
                    if t == 0:
                        link(ins)
                        link(dve.tensor_tensor(x[:, t], x[:, t], scratch, ALU.add))
                ins.then_inc(t_free, 1)
                dve.wait_ge(t_free, t_reads[xs.n])
                dve.tensor_tensor(x[:, t], x[:, t], scratch, ALU.add).then_inc(x_new, 1)
                xs.next()

            b = full()
            emptied(dve.tensor_copy(vecs[:], b[:, 0:3 * P]))
            dve.wait_ge(u_free, 1)
            dve.wait_ge(lam_loaded, 16)
            link(dve.tensor_tensor(lam_in[:, 0:4:2], lam_in[:, 0:4:2], lam_in[:, 1:4:2], ALU.mult))
            dve.tensor_reduce(lam_s, lam_in[:, 0:4:2], AX_X, ALU.add).then_inc(lam_ready, 1)
            dve.wait_ge(consts, 1)
            link(dve.tensor_tensor(eight[:], ident[:, 0:2 * MH], ident[:, 32:32 + 2 * MH], ALU.add))
            link(dve.tensor_tensor(eight[:], eight[:], ident[:, 64:64 + 2 * MH], ALU.add))
            link(dve.scalar_tensor_tensor(out=dist, in0=dist, scalar=-1.0, in1=dist, op0=ALU.mult, op1=ALU.max))
            dve.memset(dist[0:CHUNK, CHUNK:P], BIG)
            link(dve.memset(dist[0:CHUNK, 2 * P + CHUNK:3 * P], BIG))
            dve.wait_ge(lam_ready, 2)
            link(dve.tensor_tensor(neg_lam, lam_e[:, 1:2], lam_e[:, 0:1], ALU.subtract))
            link(dve.tensor_scalar(neg_lam, neg_lam, -LAMBDA_INIT, None, ALU.add))
            variance(sq_sum[:, 0:2], 1, 1)
            dve.wait_ge(cond_ready, 1)
            mods = 0
            for j in range(4):
                mod_chunk(0, j, mods)
                mods += 1
            modulation(1, 0, 4)
            link(dve.scalar_tensor_tensor(out=mul_c[:, 0], in0=modc[:, 0, 8:16], scalar=1.0, in1=norm_g(0, 0),
                                          op0=ALU.add, op1=ALU.mult))
            modulated(0)
            after = {0: [4, 5], 1: [6], 2: [7, 8], 3: [9], 4: [10], 5: [11]}
            for j in range(6):
                for g in range(2):
                    b = full()
                    pair = slice((4 * j + 2 * g) % 8, (4 * j + 2 * g) % 8 + 2)
                    b2 = b.rearrange("p (k s) -> p k s", k=2)
                    if j < 2:
                        ins = dve.tensor_scalar(qT[:, pair], b2, float(DA) ** -0.5, None, ALU.mult)
                    elif j < 4:
                        ins = dve.tensor_copy(kT[:, pair], b2)
                    else:
                        ins = dve.tensor_copy(v_nat[:, g, (j - 4) * 512:(j - 3) * 512], b)
                    emptied(ins)
                for m in after[j]:
                    mod_chunk(0, m, mods)
                    mods += 1
            modulation(2, 4, 12)
            dve.tensor_tensor(gate_c[:, 0], modc[:, 0, 16:24], norm_g(0, 1), ALU.mult)
            dve.tensor_tensor(gate_c[:, 1], modc[:, 0, 40:48], norm_g(0, 3), ALU.mult)
            link(dve.scalar_tensor_tensor(out=mul_c[:, 1], in0=modc[:, 0, 32:40], scalar=1.0, in1=norm_g(0, 2),
                                          op0=ALU.add, op1=ALU.mult))
            gate_diagonals(0)

            def logits(h):
                bb = h % 2
                if h >= 2:
                    dve.wait_ge(aT_full, h - 1)
                slope = 2.0 ** (-8.0 * (h + 1) / HEADS)
                for c in range(2):
                    emptied(dve.scalar_tensor_tensor(out=probs[:, bb, c], in0=dist, scalar=-slope, in1=full()[:, 0:384],
                                                     op0=ALU.mult, op1=ALU.add))
                dve.wait_ge(u_free, u.n)
                for c in range(2):
                    i = bb * 4 + c * 2
                    dve.tensor_reduce(nmax[:, i:i + 1], probs[:, bb, c, 0:P], AX_X, ALU.max, negate=True)
                    ins = dve.tensor_reduce(nmax[:, i + 1:i + 2], probs[:, bb, c, P:3 * P], AX_X, ALU.max, negate=True)
                ins.then_inc(maxed, 1)

            def difference(h):
                bb = h % 2
                dve.wait_ge(probs_ready, h + 1)
                link(dve.reciprocal(prec[:, bb * 4:bb * 4 + 4], psum_s[:, bb * 4:bb * 4 + 4]))
                link(dve.tensor_scalar(prec[:, bb * 4 + 2:bb * 4 + 4], prec[:, bb * 4 + 2:bb * 4 + 4], neg_lam, None, ALU.mult))
                for q, r in enumerate((slice(0, P), slice(P, 3 * P))):
                    i = bb * 4 + q
                    ins = dve.tensor_scalar(probs[:, bb, 0, r], probs[:, bb, 0, r], prec[:, i:i + 1], None, ALU.mult)
                link(ins)
                for q, r in enumerate((slice(0, P), slice(P, 3 * P))):
                    i = bb * 4 + 2 + q
                    ins = dve.scalar_tensor_tensor(out=probs[:, bb, 0, r], in0=probs[:, bb, 1, r], scalar=prec[:, i:i + 1],
                                                   in1=probs[:, bb, 0, r], op0=ALU.mult, op1=ALU.add)
                ins.then_inc(a_ready, 1)

            for h in range(HEADS + 1):
                if h < HEADS:
                    logits(h)
                if h:
                    difference(h - 1)
            gate_rows()
            dve.wait_ge(o_ready, HEADS)
            o16 = o_nat.rearrange("p t (h e) -> p (t h) e", e=HD)
            sq = qT.rearrange("p k s -> p (k s)").rearrange("p (h e) -> p h e", e=HD)
            link(dve.tensor_tensor(sq, o16, o16, ALU.mult))
            link(dve.tensor_reduce(var16, sq, AX_X, ALU.add))
            dve.tensor_scalar(var16, var16, 1.0 / HD, EPS, ALU.mult, ALU.add).then_inc(var_ready, 1)
            dve.wait_ge(rstd_ready, powers.next())
            dve.tensor_tensor(o16, o16, rstd16.unsqueeze(2).broadcast_to([P, TT * HEADS, HD]), ALU.mult).then_inc(on_ready, 1)
            for g in range(KT // 2):
                emptied(dve.tensor_scalar(oT[:, 2 * g:2 * g + 2], full().rearrange("p (k s) -> p k s", k=2), subln,
                                          1.0 - LAMBDA_INIT, ALU.mult, ALU.mult))
            variance(None, 2, 2)
            add_output(lambda t, c: ps[:, 4 + 2 * t + c])

            variance(sq_sum[:, 0:2], 1, 3)
            modulated(1)
            for j in range(6):
                n = min(WC, FF - j * WC)
                for c in range(n // P):
                    ft = 4 * j + c
                    b = full()
                    dve.wait_ge(silu_ready, ft + 1)
                    emptied(dve.tensor_tensor(hid[:, ft], hid[:, ft], b[:, S:2 * S], ALU.mult))
                for m in (2 * j, 2 * j + 1):
                    mod_chunk(1, m, mods)
                    mods += 1
            gate_diagonals(1)
            modulation(3, 0, 12)
            gate_rows()
            for i in range(2):
                dve.tensor_tensor(gate_c[:, 2 + i], modc[:, 1, 24 * i + 16:24 * i + 24], norm_g(1, 2 * i + 1), ALU.mult)
                ins = dve.scalar_tensor_tensor(out=mul_c[:, 2 + i], in0=modc[:, 1, 24 * i + 8:24 * i + 16], scalar=1.0,
                                               in1=norm_g(1, 2 * i), op0=ALU.add, op1=ALU.mult)
            link(ins)
            variance(None, 2, 4)
            add_output(lambda t, c: ps[:, 4 + 2 * t + c])

            variance(sq_sum[:, 0:2], 1, 5)
            modulated(2)
            dve.wait_ge(consts, 2)
            for j in range(4):
                for g in range(2):
                    t0 = 4 * j + 2 * g
                    emptied(dve.tensor_copy(xm[:, t0:t0 + 2, PAD:PAD + S], full().rearrange("p (k s) -> p k s", k=2)))
                dve.wait_ge(u_free, u.n)
                for tap in range(CONV):
                    for t in range(4 * j, 4 * j + 4):
                        if tap == 0:
                            ins = dve.tensor_scalar(xc[:, t], xm[:, t, 0:S], conv_w(0, t), None, ALU.mult)
                        else:
                            ins = dve.scalar_tensor_tensor(out=xc[:, t], in0=xm[:, t, tap:tap + S], scalar=conv_w(tap, t),
                                                           in1=xc[:, t], op0=ALU.mult, op1=ALU.add)
                    if tap < CONV - 1:
                        link(ins)
                ins.then_inc(conv_ready, 1)
            for t in range(IT):
                b = full()
                if t >= 2:
                    dve.wait_ge(gates_full, t - 1)
                dve.tensor_copy(vT2[:, t % 2], b[:, 0:S])
                emptied(dve.tensor_copy(v_in[:, :, t * P:(t + 1) * P], b[:, S:2 * S].rearrange("p (t s) -> p t s", t=TT)))
                b = full()
                dve.tensor_copy(xm[:, t, PAD:PAD + S], b[:, 0:S])
                emptied(dve.tensor_copy(k_in[:, t], b[:, S:2 * S]))
                dve.tensor_scalar(xc[:, t], xc[:, t], skip(t), None, ALU.mult)
            dve.wait_ge(bd_ready, IT)
            dve.wait_ge(u_full, u.n)
            dve.memset(gates_T, 0.0).then_inc(gates_T_clear, 1)
            dve.wait_ge(gates_T_clear, 1)
            dve.wait_ge(gates_full, IT)
            for m in range(3):
                r = slice(32 * m, 32 * m + 2 * MH)
                ins = dve.tensor_copy(gates_T[r], ps[r, 4 + m, 0:S])
            ins.then_inc(gates_T_ready, 1)
            dve.wait_ge(gates_full, IT + 1)
            for t in range(TT):
                ins = dve.tensor_tensor(gates[:, t], ps[:, 7, t * 2 * MH:(t + 1) * 2 * MH], b_gates[:], ALU.add)
            link(ins)
            fg = gates[:, :, MH:2 * MH]
            dve.scalar_tensor_tensor(out=f_abs, in0=fg, scalar=-1.0, in1=fg, op0=ALU.mult, op1=ALU.max).then_inc(logf_in, 1)
            link(dve.tensor_scalar(logf, fg, 0.0, None, ALU.min))
            dve.wait_ge(logf_ln, 1)
            dve.tensor_tensor(logf, logf, f_exp, ALU.subtract).then_inc(logf_ready, 1)
            dve.wait_ge(cum_full, 1)
            link(dve.tensor_copy(cumf, ps[:, 6, 0:TT * MH].rearrange("p (t g) -> p t g", t=TT)))
            link(dve.tensor_tensor(a_col, gates[:, :, 0:MH], cumf, ALU.subtract))
            for t in range(TT):
                if t:
                    dve.wait_ge(cum_full, 2)
                for h in range(MH):
                    ins = dve.tensor_scalar(diag_m[:, h * P:(h + 1) * P], ident[:], a_col[:, t, h:h + 1], None, ALU.mult)
                ins.then_inc(diag_ready, 1)
            dve.wait_ge(cum_full, 3)

            def exponents(h):
                b = h % 2
                r = slice(h * P, (h + 1) * P)
                if h:
                    dve.wait_ge(dw_ready, h)
                dve.tensor_tensor(dw[:, b, 0:P], ps[:, 4, r], causal[:], ALU.add)
                dve.tensor_copy(dw[:, b, P:2 * P], ps[:, 4, r])
                link(dve.tensor_tensor(dw[:, b, 2 * P:3 * P], ps[:, 5, r], causal[:], ALU.add))
                dve.tensor_reduce(run_max[:, 0:1], dw[:, b, 0:P], AX_X, ALU.max)
                link(dve.tensor_reduce(run_max[:, 1:2], dw[:, b, P:3 * P], AX_X, ALU.max))
                link(dve.tensor_scalar(run_max, run_max, 0.0, None, ALU.max))
                dve.tensor_scalar(neg_m, run_max, -1.0, None, ALU.mult)
                dve.tensor_tensor(m_sum, cumf[:, :, h], run_max, ALU.add).then_inc(rmax_ready, 1)

            def weigh(h):
                w, wT = head_weights(h)
                b = h % 2
                bank = full()
                dve.wait_ge(dw_ready, h + 1)
                dve.tensor_tensor_reduce(out=w[:, 0:P], in0=bank[:, 0:P], in1=dw[:, b, 0:P], scale=float(MD) ** -0.5,
                                         scalar=0.0, op0=ALU.mult, op1=ALU.add, accum_out=den[:, 0:1])
                emptied(dve.tensor_tensor_reduce(out=w[:, P:3 * P], in0=bank[:, P:3 * P], in1=dw[:, b, P:3 * P],
                                                 scale=float(MD) ** -0.5, scalar=0.0, op0=ALU.mult, op1=ALU.add,
                                                 accum_out=den[:, 1:2]))
                dve.wait_ge(u_free, u.n)
                link(dve.scalar_tensor_tensor(out=rden, in0=den, scalar=-1.0, in1=den, op0=ALU.mult, op1=ALU.max))
                link(dve.tensor_tensor(rden, rden, e_m, ALU.max))
                link(dve.reciprocal(rden, rden))

            def turned_weights(h):
                w, wT = head_weights(h)
                emptied(dve.tensor_copy(wT, full()[:, 0:3 * P]))

            def outputs(h):
                c = slice(h * MD, (h + 1) * MD)
                dve.wait_ge(num_full, h + 1)
                for t in range(TT):
                    ins = dve.tensor_scalar(v_in[:, t, c], ps[:, 6 + t], rden[:, t:t + 1], None, ALU.mult)
                link(ins)
                for t in range(TT):
                    ins = dve.bn_stats(bn6[:, t], v_in[:, t, c])
                link(ins)
                for t in range(TT):
                    ins = dve.bn_aggr(mean_var[:, t], bn6[:, t])
                link(ins)
                dve.tensor_scalar(var, mean_var[:, :, 1], EPS, None, ALU.add).then_inc(var_ready, 1)
                dve.wait_ge(rstd_ready, powers.next())
                for t in range(TT):
                    ins = dve.tensor_scalar(v_in[:, t, c], v_in[:, t, c], mean_var[:, t, 0:1], rstd[:, t:t + 1],
                                            ALU.subtract, ALU.mult)
                ins.then_inc(hh_ready, 1)

            def turned_outputs(h):
                for g in range(2):
                    b = full()
                    for c in range(2):
                        t = MK * h + 2 * g + c
                        ins = dve.scalar_tensor_tensor(out=xc[:, t], in0=b[:, c * S:(c + 1) * S], scalar=norm_m(t),
                                                       in1=xc[:, t], op0=ALU.mult, op1=ALU.add)
                    emptied(ins)
                dve.wait_ge(u_free, u.n)
                dve.wait_ge(silu_ready, FT + h + 1)
                dve.tensor_tensor(xc[:, MK * h:MK * (h + 1)], xc[:, MK * h:MK * (h + 1)], z_in(h), ALU.mult)\
                    .then_inc(m_out_ready, 1)

            for h in range(MH):
                exponents(h)
                weigh(h)
                for g in range(2):
                    t0 = MK * h + 2 * g
                    emptied(dve.tensor_copy(xm[:, t0:t0 + 2, PAD:PAD + S], full().rearrange("p (k s) -> p k s", k=2)))
                if h:
                    turned_outputs(h - 1)
                turned_weights(h)
                outputs(h)
            turned_outputs(MH - 1)
            gate_diagonals(2)
            gate_rows()
            variance(None, 2, 6)
            add_output(lambda t, c: ps[:, 4 + 2 * t + c])

            variance(sq_sum[:, 0:2], 1, 7)
            modulated(3)
            logit, top, e2, w12 = rt[:, :, 0], rt[:, :, 1], rt[:, :, 3], rt[:, :, 4]
            index, chosen, weight, pick = rt[:, :, 5], rt[:, :, 6], rt[:, :, 7], rt[:, :, 8]
            dve.wait_ge(logits_full, 1)
            for t in range(TT):
                ins = dve.tensor_tensor(logit[:, t], ps[:, 4 + t, 0:E], b_router[:], ALU.add)
            link(ins)
            for t in range(TT):
                ins = dve.max(top[:, t], logit[:, t])
            link(ins)
            for t in range(TT):
                ins = dve.max_index(top_i[:, t], top[:, t], logit[:, t])
            link(ins)
            dve.tensor_tensor(e2[:, :, 0], top[:, :, 1], top[:, :, 0], ALU.subtract).then_inc(route, 1)
            link(dve.tensor_copy(index, top_i[:]))
            dve.wait_ge(route, 2)
            link(dve.tensor_scalar(w12[:, :, 0], e2[:, :, 1], 1.0, None, ALU.add))
            link(dve.reciprocal(w12[:, :, 0], w12[:, :, 0]))
            link(dve.tensor_tensor(w12[:, :, 1], w12[:, :, 0], e2[:, :, 1], ALU.mult))
            for t in range(TT):
                dve.tensor_scalar(chosen[:, t], iota8, index[:, t, 0:1], None, ALU.is_equal)
                dve.tensor_scalar(weight[:, t], iota8, index[:, t, 0:1], w12[:, t, 0:1], ALU.is_equal, ALU.mult)
                dve.tensor_scalar(pick[:, t], iota8, index[:, t, 1:2], None, ALU.is_equal)
                ins = dve.tensor_scalar(rt[:, t, 9], iota8, index[:, t, 1:2], w12[:, t, 1:2], ALU.is_equal, ALU.mult)
            link(ins)
            dve.tensor_tensor(weight, weight, rt[:, :, 9], ALU.add)
            ins = dve.tensor_tensor(chosen, chosen, pick, ALU.add)
            ins.then_inc(route, 1)
            dve.wait_ge(route, 3)
            for t in range(TT):
                dve.tensor_copy(per_e[:, :, 2 + t], chosen[:, t])
                dve.tensor_copy(per_e[:, :, 4 + t], weight[:, t])
            dve.wait_ge(logits_full, 2)
            dve.tensor_copy(counts[:], ps[:, 6, 2 * E:3 * E]).then_inc(counts_ready, 1)
            for t in range(TT):
                ins = dve.tensor_copy(per_e[:, :, t], ps[:, 6, t * E:(t + 1) * E])
            link(ins)
            gate_diagonals(3)
            gate_rows()
            dve.memset(y_sum, 0.0).then_inc(y_added, 1)
            dve.memset(ye, 0.0).then_inc(hx_ready, 2)
            dve.wait_ge(counts_ready, 1)
            assert u.n == FILLS["moe"], u.n

            def expert(e, width):
                tiles, sw = shape_of(width)
                dve.tensor_copy(cur[:], per_e[:, bass.ds(e, 1), :].rearrange("p a n -> p (a n)")).then_inc(cur_ready, 1)
                dve.wait_ge(cur_ready, e + 1)
                for t in range(TT):
                    n = tiles * P
                    dve.tensor_scalar(sel[:, t, 0:n], slot_iota[:, 0:n], cur[:, t:t + 1], cur[:, 2 + t:3 + t],
                                      ALU.is_equal, ALU.mult)
                    ins = dve.tensor_scalar(selw[:, t, 0:n], slot_iota[:, 0:n], cur[:, t:t + 1], cur[:, 4 + t:5 + t],
                                            ALU.is_equal, ALU.mult)
                ins.then_inc(sel_ready, 1)
                for i in range(KT // 2):
                    dve.wait_ge(gather_full, e * (KT // 2) + (i + 1))
                    for j in range(2):
                        k = 2 * i + j
                        ins = dve.tensor_scalar(xg[:, k, 0:width], ps[:, i, j * S:j * S + width], mul_c[:, 3, k:k + 1],
                                                modc[:, 1, 24 + k:25 + k], ALU.mult, ALU.add)
                ins.then_inc(xg_ready, 1)
                if tiles == 1:
                    for j in range(EJ):
                        dve.wait_ge(silu_moe, step_count(e, j))
                        dve.tensor_tensor(hx[0:width, j % 2, 0:WC], hx[0:width, j % 2, 0:WC],
                                          ps[second_half(width), 2 * (j % 2) + 1], ALU.mult).then_inc(hx_ready, STEP)
                else:
                    for ft in range(ET):
                        dve.wait_ge(silu_moe, ft_count(e, ft))
                        dve.tensor_tensor(eh[:, ft, 0:width], eh[:, ft, 0:width], ps[:, ft % UB, S:S + width],
                                          ALU.mult).then_inc(hx_ready, 1)
                dve.wait_ge(y_added, e + 1)
                dve.wait_ge(spread, e + 1)
                for t in range(TT):
                    for c in range(2):
                        r = slice(c * 512, (c + 1) * 512)
                        ins = dve.tensor_tensor(y_sum[:, t, r], y_sum[:, t, r], ps[:, 4 + 2 * t + c], ALU.add)
                ins.then_inc(y_added, 1)

            with dve.Fori(0, E) as e:
                by_width(dve, e, expert)
            variance(sq_sum[:, 0:2], 1, 8)
            add_output(lambda t, c: y_sum[:, t, c * 512:(c + 1) * 512])

        silu_moe = sem("silu_moe")
        gather_full = sem("gather_full")
        xg_ready = sem("xg_ready")
        step_full = sem("step_full")
        hx_ready = sem("hx_ready")
        turn_full = sem("turn_full")
        turn_free = sem("turn_free")
        cur_ready = sem("cur_ready")

        block = ctx.enter_context(nc.Block())

        @block.sync
        def _(sp):
            sp_program(sp)

        @block.gpsimd
        def _(pool):
            pool_program(pool)

        @block.scalar
        def _(act):
            act_program(act)

        @block.tensor
        def _(pe):
            pe_program(pe)

        @block.vector
        def _(dve):
            dve_program(dve)


_NAMES = ["x", "c", "mod_w", "mod_b", "norm_g", "attn_w_in", "attn_w_out", "attn_lambda", "attn_subln",
          "ffn_w_gate", "ffn_w_up", "ffn_w_down", "mlstm_w_in", "mlstm_conv_w", "mlstm_conv_b", "mlstm_w_q",
          "mlstm_w_k", "mlstm_w_v", "mlstm_w_gate", "mlstm_b_gate", "mlstm_skip", "mlstm_norm", "mlstm_w_out",
          "moe_w_router", "moe_b_router", "moe_w_gate", "moe_w_up", "moe_w_down"]


def kernel(**inputs):
    import numpy as np
    import concourse.bacc as bacc
    from concourse.bass_utils import run_bass_kernel_spmd

    nc = bacc.Bacc("TRN2", target_bir_lowering=False, num_devices=1)
    arrays, args = {}, {}
    for name in _NAMES:
        v = np.ascontiguousarray(inputs[name])
        arrays[f"in_{name}"] = v
        args[name] = nc.dram_tensor(f"in_{name}", v.shape, mybir.dt.from_np(v.dtype), kind="ExternalInput").ap()
    out = nc.dram_tensor("out_0", (1, S, D), F32, kind="ExternalOutput").ap()
    trunk(nc, args, out)
    r = run_bass_kernel_spmd(nc, [arrays], core_ids=[0])
    return r.results[0]["out_0"]
```

```python
from contextlib import ExitStack

import concourse.bass as bass
from concourse import mybir

ALU = mybir.AluOpType
ACT = mybir.ActivationFunctionType
F32 = mybir.dt.float32
I32 = mybir.dt.int32
U32 = mybir.dt.uint32
AX_X = mybir.AxisListType.X

P = 128
D = 1024
KT = D // P
S = 256
TT = S // P
HEADS, HD, DA = 8, 128, 64
FF = ((8 * D // 3 + 127) // 128) * 128
FT = FF // P
INNER = 2 * D
IT = INNER // P
MH, MD = 4, 512
MK = MD // P
CONV = 4
E = 8
FE = 7 * D // 2
ET = FE // P
CHUNK = 64
EPS = 1e-6
LAMBDA_INIT = 0.2
BIG = 1e30

MOD_ENDS = (4, 12, 24)
MOD_PARTS = {0: (0, 4, 12), 1: (0, 12)}

SLOTS = 7
SLOT = 4096
WC = 512
DK = SLOT // D
DOWN_CHUNKS = [2, 2, 2, 4, 4, 4, 4]
UB = 4


MODS = {0: [[4, 5], [6, 7], [8, 9], [10], [11], []], 1: [[0, 1, 2], [3, 4, 5], [6, 7], [8, 9], [10, 11], []]}


def chunk_plan():
    up = lambda m, j, n=WC: (m, j * WC, n, "pe")
    mod = lambda layer, j: (f"mod{layer}", j * WC, WC, "dve")
    plan = [mod(0, j) for j in range(4)]
    for j in range(6):
        plan += [up("attn_in", j)] + [mod(0, m) for m in MODS[0][j]]
    plan += [("attn_out", k, DK, "pe") for k in range(0, KT, DK)]
    for j in range(6):
        n = min(WC, FF - j * WC)
        plan += [up("gate", j, n), up("up", j, n)] + [mod(1, m) for m in MODS[1][j]]
    k = 0
    for n in DOWN_CHUNKS:
        plan.append(("down", k, n, "pe"))
        k += n
    plan += [up("mlstm_in", j) for j in range(8)]
    plan += [("mlstm_out", k, DK, "pe") for k in range(0, IT, DK)]
    return plan


PLAN = chunk_plan()
NPRE = len(PLAN)
EC = 3 * FE // WC
assert NPRE % SLOTS == 0 and EC % SLOTS == 0
PRE_USES = NPRE // SLOTS


FILLS = {}
FILLS["attn"] = 1 + KT // 2
FILLS["ffn"] = FILLS["attn"] + 12 + 2 * HEADS + 2 + KT // 2 + KT // 2
FILLS["x_m"] = FILLS["ffn"] + FT + 2 + KT // 2
FILLS["qkv"] = FILLS["x_m"] + 8
FILLS["cell"] = FILLS["qkv"] + 2 * IT
FILLS["moe"] = FILLS["cell"] + 6 * MH + 2 + KT // 2 + 2


def fills_after_z(h):
    return FILLS["cell"] + (6 * h - 2 if h else 0) + 3
EJ = FE // WC
FIRST = E - 1
RANKS = [0] + [(i + 1) // 2 if i % 2 else E - i // 2 for i in range(1, E)]
STEP = WC // P
WIDTHS = [P // 2] + list(range(P, S + 1, 16))


class Count:

    def __init__(self, start=0):
        self.n = start

    def next(self, k=1):
        self.n += k
        return self.n


def trunk(nc, a, out):
    with ExitStack() as ctx:
        def sb(name, shape, dt=F32):
            return ctx.enter_context(nc.sbuf_tensor(name, shape, dt))

        def sem(name):
            return ctx.enter_context(nc.semaphore(name))

        ring = sb("ring", [P, SLOTS, SLOT])
        x = sb("x", [P, TT, D])
        hT = sb("hT", [P, KT, S])
        flat_h = hT[:, :, :].rearrange("p k s -> p (k s)")
        gate_bc = flat_h[:, 0:D]
        scratch = flat_h[:, D:2 * D]
        ident = sb("ident", [P, P])
        ones = sb("ones", [P, P])
        tri = sb("tri", [P, P])
        tri_strict = sb("tri_strict", [P, P])
        causal = sb("causal", [P, P])
        slot_iota = sb("slot_iota", [P, S])
        block4 = sb("block4", [P, P // 4])
        ones_col = sb("ones_col", [P, 63])
        eight = sb("eight", [P, 2 * MH])
        vecs = sb("vecs", [P, 3 * P])
        modc = sb("modc", [P, 2, 48])
        mul_c = sb("mul_c", [P, 4, KT])
        gate_c = sb("gate_c", [P, 4, KT])
        cond = sb("cond", [P, KT])
        qkv_blocks = sb("qkv_blocks", [P, 3, IT, 4])
        w_gates = sb("w_gates", [P, 3 * IT, 2 * MH])
        b_gates = sb("b_gates", [P, 2 * MH])
        w_router = sb("w_router", [P, KT, E])
        b_router = sb("b_router", [P, E])
        small = sb("small", [P, 180])
        used = [0]

        def col(n):
            used[0] += n
            return small[:, used[0] - n:used[0]]

        exponent = col(TT * HEADS)
        sq_sum = col(4 * TT)
        var = col(TT)
        rstd = col(TT)
        lam_s = col(2)
        lam_e = col(2)
        neg_lam = col(1)
        nmax = col(8)
        psum_s = col(8)
        prec = col(8)
        sq16 = col(16)
        var16 = col(16)
        rstd16 = col(16)
        gates = col(TT * 2 * MH).rearrange("p (t g) -> p t g", t=TT)
        f_abs = col(TT * MH).rearrange("p (t g) -> p t g", t=TT)
        f_exp = col(TT * MH).rearrange("p (t g) -> p t g", t=TT)
        logf = col(TT * MH).rearrange("p (t g) -> p t g", t=TT)
        cumf = col(TT * MH).rearrange("p (t g) -> p t g", t=TT)
        a_col = col(TT * MH).rearrange("p (t g) -> p t g", t=TT)
        run_max = col(TT)
        neg_m = col(TT)
        m_sum = col(TT)
        e_m = col(TT)
        den = col(TT)
        rden = col(TT)
        mean_var = col(TT * 2).rearrange("p (t g) -> p t g", t=TT)
        iota8 = slot_iota[:, 0:E]
        rt = sb("rt", [P, TT, 12, E])
        top_i = sb("top_i", [P, TT, E], U32)
        counts = sb("counts", [P, E], I32)
        order_e = sb("order_e", [P, E + 1], I32)
        rank_at = sb("rank_at", [P, E])
        per_e = sb("per_e", [P, E, 6])
        cur = sb("cur", [P, 6])
        arena = sb("arena", [P, 17712])
        at = [0]

        def area(n, first=None):
            if first is not None:
                at[0] = first
            at[0] += n
            assert at[0] <= 17712, at[0]
            return arena[:, at[0] - n:at[0]]

        xn = area(2048, 0).rearrange("p (t d) -> p t d", t=TT)
        mod_acc = area(1024).rearrange("p (b n) -> p b n", b=2)
        mod_rows = area(P)
        after_acc = at[0]
        rows = area(3 * P, after_acc).rearrange("p (r n) -> p r n", r=3)
        qT = area(2048, after_acc + 3 * P).rearrange("p (k s) -> p k s", k=KT)
        kT = area(2048).rearrange("p (k s) -> p k s", k=KT)
        v_nat = area(2048).rearrange("p (t d) -> p t d", t=TT)
        o_nat = area(2048).rearrange("p (t d) -> p t d", t=TT)
        probs = area(2 * 2 * 384).rearrange("p (b c n) -> p b c n", b=2, c=2)
        aT = area(2 * 384).rearrange("p (b n) -> p b n", b=2)
        oT = area(2048).rearrange("p (k s) -> p k s", k=KT)
        dist = area(384)
        lam_in = area(4 * DA).rearrange("p (i n) -> p i n", i=4)
        hid = area(FT * S, after_acc).rearrange("p (k s) -> p k s", k=FT)
        PAD = CONV - 1
        xm = area(IT * (S + PAD), 0).rearrange("p (k s) -> p k s", k=IT)
        xc = area(IT * S).rearrange("p (k s) -> p k s", k=IT)
        k_in = area(IT * S).rearrange("p (k s) -> p k s", k=IT)
        v_in = area(TT * INNER).rearrange("p (t d) -> p t d", t=TT)
        vT2 = area(2 * S).rearrange("p (b s) -> p b s", b=2)
        m_share = at[0]
        bd = area(2 * 3 * P, m_share).rearrange("p (b m o) -> p b m o", b=2, m=3)
        dw = area(2 * 384, m_share).rearrange("p (b n) -> p b n", b=2)
        gates_T = area(S, m_share)
        diag_m = area(512, m_share)
        xg = area(KT * S, 2048).rearrange("p (k s) -> p k s", k=KT)
        eh = area(ET * S).rearrange("p (k s) -> p k s", k=ET)
        ye = area(TT * D).rearrange("p (t d) -> p t d", t=TT)
        hx = ye
        y_sum = area(TT * D).rearrange("p (t d) -> p t d", t=TT)
        scat = area(TT * S).rearrange("p (t s) -> p t s", t=TT)
        sel = area(TT * S).rearrange("p (t s) -> p t s", t=TT)
        selw = area(TT * S).rearrange("p (t s) -> p t s", t=TT)
        pairs = area(2 * E * E).rearrange("p (b i e) -> p b i e", b=2, i=E)
        keys = area(E)
        ranks = area(E)
        placed = area(2 * E).rearrange("p (b e) -> p b e", b=2)
        bn6 = sb("bn6", [P, TT, 6])

        ps = ctx.enter_context(nc.psum_tensor("ps", [P, 8, 512], F32))

        cA, cB, cC = 0, P, 2 * P
        conv_w = lambda j, t: vecs[:, cA + j * IT + t:cA + j * IT + t + 1]
        conv_b = lambda t: vecs[:, cA + 64 + t:cA + 65 + t]
        skip = lambda t: vecs[:, cA + 80 + t:cA + 81 + t]
        norm_m = lambda t: vecs[:, cA + 96 + t:cA + 97 + t]
        c_cols = vecs[:, cB:cB + KT]
        norm_g = lambda layer, i: vecs[:, cB + 8 + (layer * 4 + i) * KT:cB + 8 + (layer * 4 + i + 1) * KT]
        subln = vecs[:, cB + 72:cB + 73]
        mod_b = vecs[:, cC:cC + 96].rearrange("p (l n) -> p l n", l=2)

        consts = sem("consts")
        x_loaded = sem("x_loaded")
        rows_loaded = sem("rows_loaded")
        rows_clear = sem("rows_clear")
        lam_loaded = sem("lam_loaded")
        small_loaded = sem("small_loaded")
        landed = [sem(f"landed{s}") for s in range(SLOTS)]
        pe_read = sem("pe_read")
        freed = sem("freed")
        u_full = sem("u_full")
        u_free = sem("u_free")
        dstep = sem("dstep")
        astep = sem("astep")
        pstep = sem("pstep")
        cond_ready = sem("cond_ready")
        acc_ready = sem("acc_ready")
        mod_summed = sem("mod_summed")
        mod_rows_ready = sem("mod_rows_ready")
        mod_turned = sem("mod_turned")
        x_new = sem("x_new")
        sq_ready = sem("sq_ready")
        var_ready = sem("var_ready")
        rstd_ready = sem("rstd_ready")
        xn_ready = sem("xn_ready")
        diag_ready = sem("diag_ready")
        y_full = sem("y_full")
        t_free = sem("t_free")
        lam_ready = sem("lam_ready")
        maxed = sem("maxed")
        probs_ready = sem("probs_ready")
        a_ready = sem("a_ready")
        aT_full = sem("aT_full")
        aT_ready = sem("aT_ready")
        o_full = sem("o_full")
        o_ready = sem("o_ready")
        on_ready = sem("on_ready")
        silu_ready = sem("silu_ready")
        conv_ready = sem("conv_ready")
        xc_ready = sem("xc_ready")
        bd_ready = sem("bd_ready")
        gates_full = sem("gates_full")
        gates_T_clear = sem("gates_T_clear")
        gates_T_ready = sem("gates_T_ready")
        logf_in = sem("logf_in")
        logf_ln = sem("logf_ln")
        logf_ready = sem("logf_ready")
        cum_full = sem("cum_full")
        rmax_ready = sem("rmax_ready")
        dw_ready = sem("dw_ready")
        m_out_ready = sem("m_out_ready")
        num_full = sem("num_full")
        hh_ready = sem("hh_ready")
        logits_full = sem("logits_full")
        route = sem("route")
        counts_ready = sem("counts_ready")
        sel_ready = sem("sel_ready")
        scat_full = sem("scat_full")
        scat_ready = sem("scat_ready")
        ye_ready = sem("ye_ready")
        spread = sem("spread")
        y_added = sem("y_added")
        stored = sem("stored")

        def y_banks(t):
            return ps[:, 4 + 2 * t:6 + 2 * t].rearrange("p b n -> p (b n)")

        def z_in(h):
            return xm[:, MK * h:MK * (h + 1), PAD:PAD + S]

        def head_weights(h):
            k = k_in[:, MK * h:MK * (h + 1), :].rearrange("p k s -> p (k s)")
            return k[:, 0:384], k[:, 384:768]

        def weights(matrix, first, n):
            if matrix.startswith("mod"):
                w = a["mod_w"][int(matrix[3])]
            else:
                w = {"attn_in": a["attn_w_in"], "attn_out": a["attn_w_out"], "gate": a["ffn_w_gate"],
                     "up": a["ffn_w_up"], "down": a["ffn_w_down"], "mlstm_in": a["mlstm_w_in"],
                     "mlstm_out": a["mlstm_w_out"]}[matrix][0]
            if matrix in ("attn_out", "down", "mlstm_out"):
                return w.rearrange("(k p) n -> p k n", p=P)[:, first:first + n, :]
            return w.rearrange("(k p) n -> p k n", p=P)[:, :, first:first + n]

        def slot_up(s, n=WC):
            return ring[:, s, 0:KT * n].rearrange("p (k n) -> p k n", n=n)

        def slot_down(s, k=DK):
            return ring[:, s, 0:k * D].rearrange("p (k n) -> p k n", n=D)

        order = {(m, f): i for i, (m, f, n, r) in enumerate(PLAN)}
        read_by = []
        n_mod = n_down = n_y = 0
        for m, f, n, r in PLAN:
            j = f // WC
            if r == "dve":
                n_mod += 1
                read_by.append((acc_ready, n_mod))
            elif m == "attn_in":
                read_by.append((u_full, FILLS["attn"] + 2 * (j + 1)))
            elif m in ("gate", "up"):
                read_by.append((u_full, FILLS["ffn"] + min(4 * (j + 1), FT)))
            elif m == "mlstm_in":
                read_by.append((u_full, FILLS["x_m"] + 2 * (j + 1) if j < 4 else fills_after_z(j - 4)))
            elif f + n == {"attn_out": KT, "down": FT, "mlstm_out": IT}[m]:
                n_y += 1
                read_by.append((y_full, 2 * n_y))
            else:
                n_down += 1
                read_by.append((pe_read, n_down))

        def wait_chunk(eng, i):
            eng.wait_ge(landed[i % SLOTS], 16 * (i // SLOTS + 1))

        def expert_chunk(sp, e, c):
            s = c % SLOTS
            n_up = 2 * (FE // WC)
            if c < n_up:
                w = a["moe_w_gate"] if c % 2 == 0 else a["moe_w_up"]
                src = w[0][e].rearrange("(k p) n -> p k n", p=P)[:, :, (c // 2) * WC:(c // 2 + 1) * WC]
                sp.dma_start(slot_up(s), src).then_inc(landed[s], 16)
            else:
                j = c - n_up
                src = a["moe_w_down"][0][e].rearrange("(k p) n -> p k n", p=P)[:, j * DK:(j + 1) * DK, :]
                sp.dma_start(slot_down(s), src).then_inc(landed[s], 16)

        def sp_program(sp):
            sp.wait_ge(rows_clear, 1)
            cw = a["mlstm_conv_w"][0]
            sp.dma_start(rows[0:64, 0, :], cw.rearrange("j (t p) -> (j t) p", p=P)).then_inc(rows_loaded, 16)
            sp.dma_start(rows[64:80, 0, :], a["mlstm_conv_b"][0].rearrange("(t p) -> t p", p=P)).then_inc(rows_loaded, 16)
            sp.dma_start(rows[80:96, 0, :], a["mlstm_skip"][0].rearrange("(t p) -> t p", p=P)).then_inc(rows_loaded, 16)
            sp.dma_start(rows[96:112, 0, :], a["mlstm_norm"][0].rearrange("(t p) -> t p", p=P)).then_inc(rows_loaded, 16)
            sp.dma_start(rows[0:8, 1, :], a["c"][0].rearrange("(t p) -> t p", p=P)).then_inc(rows_loaded, 16)
            sp.dma_start(rows[8:72, 1, :], a["norm_g"].rearrange("l i (t p) -> (l i t) p", p=P)).then_inc(rows_loaded, 16)
            sp.dma_start(rows[72:73, 1, :], a["attn_subln"]).then_inc(rows_loaded, 16)
            sp.dma_start(rows[0:96, 2, :], a["mod_b"].rearrange("l (t p) -> (l t) p", p=P)).then_inc(rows_loaded, 16)
            sp.dma_start(x[:], a["x"][0].rearrange("(t p) d -> p t d", p=P)).then_inc(x_loaded, 16)
            for i, (m, f, n, r) in enumerate(PLAN):
                if i >= SLOTS:
                    sp.wait_ge(*read_by[i - SLOTS])
                dst = slot_down(i % SLOTS, n) if m in ("attn_out", "down", "mlstm_out") else slot_up(i % SLOTS, n)
                sp.dma_start(dst, weights(m, f, n)).then_inc(landed[i % SLOTS], 16)
            for c in range(EC):
                sp.wait_ge(freed, c + 1)
                expert_chunk(sp, FIRST, c)
            sp.wait_ge(counts_ready, 1)
            with sp.Fori(1, E) as i:
                e = sp.value_load(order_e[0:1, bass.ds(i, 1)], min_val=0, max_val=E - 1)
                for c in range(EC):
                    sp.wait_ge(freed, i * EC + (c + 1))
                    expert_chunk(sp, e, c)
            for t in range(TT):
                sp.wait_ge(x_new, 3 * TT + t + 1)
                sp.dma_start(out[0, t * P:(t + 1) * P, :], x[:, t]).then_inc(stored, 16)
            sp.wait_ge(stored, 16 * TT)

        def pool_program(pool):
            steps = Count()
            powers = Count()

            def link(ins):
                ins.then_inc(pstep, 1)
                pool.wait_ge(pstep, steps.next())

            pool.memset(rows, 0.0).then_inc(rows_clear, 1)
            pool.memset(exponent, -0.5)
            pool.memset(ones[:], 1.0)
            pool.memset(ident[:], 0.0)
            for i, r in enumerate(RANKS):
                pool.memset(rank_at[:, i:i + 1], float(r))
            pool.memset(ones_col[:, 0:31], 0.0)
            pool.memset(ones_col[:, 31:32], 1.0)
            pool.memset(ones_col[:, 32:63], 0.0)
            pool.memset(tri[:], 1.0)
            pool.memset(tri_strict[:], 1.0)
            pool.memset(causal[:], 0.0)
            link(pool.memset(block4[:], 1.0))
            pool.affine_select(out=ident[:], in_=ident[:], compare_op=ALU.not_equal, fill=1.0, base=0,
                               pattern=[[-1, P]], channel_multiplier=1)
            pool.affine_select(out=tri[:], in_=tri[:], compare_op=ALU.is_ge, fill=0.0, base=0,
                               pattern=[[1, P]], channel_multiplier=-1)
            pool.affine_select(out=tri_strict[:], in_=tri_strict[:], compare_op=ALU.is_gt, fill=0.0, base=0,
                               pattern=[[1, P]], channel_multiplier=-1)
            pool.affine_select(out=causal[:], in_=causal[:], compare_op=ALU.is_ge, fill=-BIG, base=0,
                               pattern=[[-1, P]], channel_multiplier=1)
            link(pool.affine_select(out=block4[:], in_=block4[:], compare_op=ALU.is_ge, fill=0.0, base=0,
                                    pattern=[[-4, P // 4]], channel_multiplier=1))
            pool.affine_select(out=block4[:], in_=block4[:], compare_op=ALU.is_ge, fill=0.0, base=3,
                               pattern=[[4, P // 4]], channel_multiplier=-1)
            pool.iota(slot_iota[:], pattern=[[1, S]], base=0, channel_multiplier=0,
                      allow_small_or_imprecise_dtypes=True)
            pool.iota(dist[:, 0:P], pattern=[[1, P]], base=0, channel_multiplier=-1,
                      allow_small_or_imprecise_dtypes=True)
            pool.iota(dist[:, P:3 * P], pattern=[[1, S]], base=-P, channel_multiplier=-1,
                      allow_small_or_imprecise_dtypes=True).then_inc(consts, 1)

            def power(src, dst, width):
                pool.wait_ge(var_ready, powers.next())
                pool.tensor_tensor(dst, src, exponent[:, 0:width], ALU.pow).then_inc(rstd_ready, 1)

            def tile_power(t):
                power(var[:, t:t + 1], rstd[:, t:t + 1], 1)

            def output_and_input_powers():
                for t in range(TT):
                    tile_power(t)
                    tile_power(t)

            for t in range(TT):
                tile_power(t)
            power(var16, rstd16, TT * HEADS)
            output_and_input_powers()
            output_and_input_powers()
            pool.wait_ge(u_free, FILLS["x_m"])
            pool.memset(xm[:, :, 0:PAD], 0.0).then_inc(consts, 1)
            pool.wait_ge(small_loaded, 16 * 7)
            for t in range(IT):
                if t >= 2:
                    pool.wait_ge(gates_full, t - 1)
                pool.tensor_tensor(
                    bd[:, t % 2].rearrange("p m (g o) -> p m g o", o=4),
                    qkv_blocks[:, :, t, :].unsqueeze(2).broadcast_to([P, 3, P // 4, 4]),
                    block4[:].unsqueeze(1).unsqueeze(3).broadcast_to([P, 3, P // 4, 4]),
                    ALU.mult).then_inc(bd_ready, 1)
            for h in range(MH):
                power(var, rstd, TT)
            output_and_input_powers()
            for t in range(TT):
                tile_power(t)

        def act_program(act):
            steps = Count()

            def link(ins):
                ins.then_inc(astep, 1)
                act.wait_ge(astep, steps.next())

            act.dma_start(lam_in[:], a["attn_lambda"][0].unsqueeze(0).broadcast_to([P, 4, DA])).then_inc(lam_loaded, 16)
            def squares_x(n, t):
                if n == 0:
                    act.wait_ge(x_loaded, 16)
                else:
                    act.wait_ge(x_new, TT * (n - 1) + t + 1)
                act.activation(xn[:, t], x[:, t], ACT.Square, accum_out=sq_sum[:, t:t + 1]).then_inc(sq_ready, 1)

            def normed_x(t, powers):
                act.wait_ge(rstd_ready, powers)
                act.activation(xn[:, t], x[:, t], ACT.Copy, scale=rstd[:, t:t + 1]).then_inc(xn_ready, 1)

            def squares_y(n, t):
                if n == 3 and t == 1:
                    act.wait_ge(freed, SLOTS)
                else:
                    act.wait_ge(y_full, TT * (n - 1) + t + 1)
                act.activation(xn[:, t], y_banks(t), ACT.Square, accum_out=sq_sum[:, t:t + 1]).then_inc(sq_ready, 1)

            def output_to_input(n, powers):
                for t in range(TT):
                    squares_y(n, t)
                    squares_x(n, t)
                    normed_x(t, powers + 2 * t + 2)

            act.wait_ge(u_free, 1)
            act.activation(cond[:], c_cols, ACT.Silu).then_inc(cond_ready, 1)
            for m, name in enumerate(("mlstm_w_q", "mlstm_w_k", "mlstm_w_v")):
                act.dma_start(qkv_blocks[:, m], a[name][0].rearrange("(t g) i o -> (g i) t o", g=P // 4)).then_inc(small_loaded, 16)
            act.dma_start(w_gates[:], a["mlstm_w_gate"][0].rearrange("(k p) n -> p k n", p=P)).then_inc(small_loaded, 16)
            act.dma_start(b_gates[:], a["mlstm_b_gate"].broadcast_to([P, 2 * MH])).then_inc(small_loaded, 16)
            act.dma_start(w_router[:], a["moe_w_router"][0].rearrange("(k p) n -> p k n", p=P)).then_inc(small_loaded, 16)
            act.dma_start(b_router[:], a["moe_b_router"].broadcast_to([P, E])).then_inc(small_loaded, 16)
            act.wait_ge(lam_ready, 1)
            act.activation(lam_e, lam_s, ACT.Exp).then_inc(lam_ready, 1)
            for t in range(TT):
                squares_x(0, t)
            for t in range(TT):
                normed_x(t, t + 1)

            def exps(h):
                act.wait_ge(maxed, h + 1)
                b = h % 2
                for c in range(2):
                    for q in range(TT):
                        i = b * 4 + c * 2 + q
                        p = probs[:, b, c, 0:P] if q == 0 else probs[:, b, c, P:3 * P]
                        ins = act.activation(p, p, ACT.Exp, bias=nmax[:, i:i + 1], accum_out=psum_s[:, i:i + 1])
                ins.then_inc(probs_ready, 1)

            def move_aT(h):
                act.wait_ge(aT_full, h + 1)
                if h >= 2:
                    act.wait_ge(o_full, h - 1)
                act.activation(aT[:, h % 2], ps[:, 4 + h % 2, 0:384], ACT.Copy).then_inc(aT_ready, 1)

            def move_o(h):
                act.wait_ge(o_full, h + 1)
                act.activation(o_nat[:, :, h * HD:(h + 1) * HD],
                               ps[:, 6 + h % 2, 0:S].rearrange("p (t d) -> p t d", t=TT), ACT.Copy)
                for t in range(TT):
                    ins = act.activation(oT[:, h, t * HD:(t + 1) * HD], ps[:, 6 + h % 2, t * HD:(t + 1) * HD], ACT.Square,
                                         accum_out=sq16[:, t * HEADS + h:t * HEADS + h + 1])
                ins.then_inc(o_ready, 1)

            for h in range(HEADS + 2):
                if h < HEADS:
                    exps(h)
                if 1 <= h <= HEADS:
                    move_aT(h - 1)
                if h >= 2:
                    move_o(h - 2)
            output_to_input(1, 3)
            u = FILLS["ffn"]
            for ft in range(FT):
                act.wait_ge(u_full, u + ft + 1)
                act.activation(hid[:, ft, :], ps[:, (u + ft) % UB, 0:S], ACT.Silu).then_inc(silu_ready, 1)
            output_to_input(2, 7)
            for j in range(4):
                act.wait_ge(conv_ready, j + 1)
                for t in range(4 * j, 4 * j + 4):
                    ins = act.activation(xc[:, t], xc[:, t], ACT.Silu, bias=conv_b(t))
                ins.then_inc(xc_ready, 1)
            act.wait_ge(logf_in, 1)
            link(act.activation(f_exp, f_abs, ACT.Exp, scale=-1.0))
            act.activation(f_exp, f_exp, ACT.Ln, bias=1.0).then_inc(logf_ln, 1)
            for h in range(MH):
                act.wait_ge(rmax_ready, h + 1)
                b = h % 2
                act.activation(e_m, m_sum, ACT.Exp, scale=-1.0)
                act.activation(dw[:, b, 0:P], dw[:, b, 0:P], ACT.Exp, bias=neg_m[:, 0:1])
                act.activation(dw[:, b, P:3 * P], dw[:, b, P:3 * P], ACT.Exp, bias=neg_m[:, 1:2]).then_inc(dw_ready, 1)
                act.wait_ge(u_free, fills_after_z(h))
                act.activation(z_in(h), z_in(h), ACT.Silu).then_inc(silu_ready, 1)
            output_to_input(3, 11 + MH)
            act.wait_ge(route, 1)
            act.activation(rt[:, :, 3, 1], rt[:, :, 3, 0], ACT.Exp).then_inc(route, 1)

            act.wait_ge(counts_ready, 1)
            act.wait_ge(hx_ready, 2)
            act.nop().then_inc(silu_moe, 2)
            act.nop().then_inc(turn_free, 2)

            def expert(e, width):
                tiles, sw = shape_of(width)
                act.wait_ge(scat_full, e + 1)
                act.activation(scat[:, 0:tiles, :],
                               ps[:, 4, 0:tiles * S].rearrange("p (t s) -> p t s", t=tiles), ACT.Copy).then_inc(scat_ready, 1)
                if tiles == 1:
                    for j in range(EJ + 1):
                        if j < EJ:
                            act.wait_ge(step_full, step_count(e, j))
                            if j >= 2:
                                act.wait_ge(turn_full, step_count(e, j - 2))
                            act.activation(hx[0:width, j % 2, 0:WC], ps[0:width, 2 * (j % 2)], ACT.Silu).then_inc(silu_moe, STEP)
                        if j:
                            m = j - 1
                            act.wait_ge(turn_full, step_count(e, m))
                            act.activation(eh[:, STEP * m:STEP * j, 0:width],
                                           ps[:, 6 + m % 2].rearrange("p (c s) -> p c s", c=STEP)[:, :, 0:width],
                                           ACT.Copy).then_inc(turn_free, STEP)
                else:
                    for ft in range(ET):
                        act.wait_ge(step_full, ft_count(e, ft))
                        act.activation(eh[:, ft, 0:width], ps[:, ft % UB, 0:width], ACT.Silu).then_inc(silu_moe, 1)
                    act.nop().then_inc(turn_free, ET)
                act.wait_ge(freed, e * EC + (SLOTS + EC))
                for st in range(tiles):
                    for n in range(tiles):
                        r = second_half(sw[st]) if n else slice(0, sw[st])
                        src = ps[r, 4 + 2 * st + n]
                        ins = act.activation(ye[0:sw[st], st, n * 512:(n + 1) * 512], src, ACT.Copy)
                ins.then_inc(ye_ready, 1)

            with act.Fori(0, E) as e:
                by_width(act, e, expert)
            act.wait_ge(y_added, 1 + E)
            for t in range(TT):
                act.activation(xn[:, t], y_sum[:, t], ACT.Square, accum_out=sq_sum[:, t:t + 1]).then_inc(sq_ready, 1)

        def shape_of(width):
            return (width + P - 1) // P, [min(width - t, P) for t in range(0, width, P)]

        def second_half(sw):
            return slice(P // 2, P // 2 + sw) if sw <= P // 2 else slice(0, sw)

        def ft_count(e, ft):
            return e * ET + (2 + ft + 1)

        def step_count(e, j):
            return ft_count(e, STEP * j + STEP - 1)

        def by_width(eng, e, body):
            n = eng.value_load(counts[0:1, bass.ds(e, 1)], min_val=0, max_val=S)

            def choose(widths):
                if len(widths) == 1:
                    body(e, widths[0])
                    return
                half = len(widths) // 2
                with eng.If(n > widths[half - 1]):
                    choose(widths[half:])
                    eng.nop()
                with eng.Else():
                    choose(widths[:half])
                    eng.nop()

            choose(WIDTHS)

        def pe_program(pe):
            u = Count()
            reads = Count()

            def bank():
                n = u.next()
                if n > UB:
                    pe.wait_ge(u_free, n - UB)
                return ps[:, (n - 1) % UB]

            def chunk(m, f, n=WC):
                i = order[(m, f)]
                wait_chunk(pe, i)
                return i

            def mod_sum(layer, j, n):
                pe.wait_ge(acc_ready, n + 1)
                for i in range(4):
                    r = slice(32 * i, 32 * (i + 1))
                    ins = pe.matmul(ps[r, 7, 0:P], ones_col[:, 31 - j:63 - j], mod_acc[:, n % 2, i * P:(i + 1) * P],
                                    start=(j in MOD_PARTS[layer]), stop=(j + 1 in MOD_PARTS[layer]))
                ins.then_inc(mod_summed, 1)

            def mod_turn(n):
                pe.wait_ge(mod_rows_ready, n)
                pe.transpose(ps[:, 6, 0:P], mod_rows, ident[:]).then_inc(mod_turned, 1)

            def transposes(src, ready, before):
                fills = [bank() for _ in range(KT // 2)]
                for t in range(TT):
                    pe.wait_ge(ready, before + t + 1)
                    for i, b in enumerate(fills):
                        for j in range(2):
                            k = 2 * i + j
                            ins = pe.transpose(b[:, j * S + t * P:j * S + (t + 1) * P], src[:, t, k * P:(k + 1) * P], ident[:])
                        if t == TT - 1:
                            ins.then_inc(u_full, 1)

            def transposes_x(n):
                transposes(xn, xn_ready, TT * n)

            def broadcast_gate(diagonals):
                pe.wait_ge(diag_ready, diagonals)
                for i in range(2):
                    b = bank()
                    pe.matmul(b, ones[:], scratch[:, i * 512:(i + 1) * 512], start=True, stop=True).then_inc(u_full, 1)

            def project(matrix, chunks, lhs, free):
                pe.wait_ge(t_free, free)
                last = chunks[-1][0] + chunks[-1][1] - 1
                for first, n in chunks:
                    i = chunk(matrix, first)
                    w = slot_down(i % SLOTS, n)
                    final = first + n - 1 == last
                    for k, t in ([(k, t) for t in range(TT) for k in range(n)] if final else
                                 [(k, t) for k in range(n) for t in range(TT)]):
                        for c in range(2):
                            ins = pe.matmul(ps[:, 4 + 2 * t + c], lhs[:, first + k, t * P:(t + 1) * P],
                                            w[:, k, c * 512:(c + 1) * 512], start=(first + k == 0), stop=(first + k == last))
                        if final and t == 0 and k == n - 1:
                            ins.then_inc(y_full, 1)
                    if matrix == "mlstm_out":
                        ins.then_inc(freed, SLOTS - len(chunks) + 1 if first == 0 else 1)
                    else:
                        ins.then_inc(y_full if final else pe_read, 1)

            def up_tile(dst, w, c):
                for k in range(KT):
                    ins = pe.matmul(dst, w[:, k, c * P:(c + 1) * P], hT[:, k, :], start=(k == 0), stop=(k == KT - 1))
                return ins

            pe.wait_ge(consts, 1)
            pe.wait_ge(rows_loaded, 16 * 8)
            b = bank()
            for r in range(3):
                ins = pe.transpose(b[:, r * P:(r + 1) * P], rows[:, r, :], ident[:])
            ins.then_inc(u_full, 1)
            mods = 0
            for j in range(4):
                mod_sum(0, j, mods)
                mods += 1
            mod_turn(1)
            transposes_x(0)

            pe.wait_ge(u_free, u.n)
            for j in range(6):
                i = chunk("attn_in", j * WC)
                w = slot_up(i % SLOTS)
                for g in range(2):
                    b = bank()
                    if j < 4:
                        for c in range(2):
                            ins = up_tile(b[:, c * S:(c + 1) * S], w, 2 * g + c)
                    else:
                        for k in range(KT):
                            ins = pe.matmul(b, hT[:, k, g * P:(g + 1) * P], w[:, k, :], start=(k == 0), stop=(k == KT - 1))
                    ins.then_inc(u_full, 1)
                if j:
                    for m in MODS[0][j - 1]:
                        mod_sum(0, m, mods)
                        mods += 1
            mod_turn(2)
            pe.wait_ge(u_free, u.n)
            pe.wait_ge(t_free, 2)

            def scores(h):
                for c in range(2):
                    b = bank()
                    r = slice(DA * c, DA * (c + 1))
                    pe.matmul(b[:, 0:P], qT[r, h, 0:P], kT[r, h, 0:P], start=True, stop=True)
                    pe.matmul(b[:, P:3 * P], qT[r, h, P:2 * P], kT[r, h, :], start=True, stop=True).then_inc(u_full, 1)

            def turn(h):
                pe.wait_ge(a_ready, h + 1)
                if h >= 2:
                    pe.wait_ge(aT_ready, h - 1)
                for i in range(3):
                    ins = pe.transpose(ps[:, 4 + h % 2, i * P:(i + 1) * P], probs[:, h % 2, 0, i * P:(i + 1) * P], ident[:])
                ins.then_inc(aT_full, 1)

            def values(h):
                pe.wait_ge(aT_ready, h + 1)
                if h >= 2:
                    pe.wait_ge(o_ready, h - 1)
                w = slice(h * HD, (h + 1) * HD)
                b = ps[:, 6 + h % 2]
                pe.matmul(b[:, 0:P], aT[:, h % 2, 0:P], v_nat[:, 0, w], start=True, stop=True)
                pe.matmul(b[:, P:2 * P], aT[:, h % 2, P:2 * P], v_nat[:, 0, w], start=True, stop=False)
                pe.matmul(b[:, P:2 * P], aT[:, h % 2, 2 * P:3 * P], v_nat[:, 1, w], start=False, stop=True).then_inc(o_full, 1)

            scores(0)
            for h in range(HEADS + 2):
                if h + 1 < HEADS:
                    scores(h + 1)
                if 1 <= h <= HEADS:
                    turn(h - 1)
                if h >= 2:
                    values(h - 2)
            broadcast_gate(1)
            transposes(o_nat, on_ready, 0)
            pe.wait_ge(u_free, u.n)
            pe.wait_ge(o_ready, HEADS)
            project("attn_out", [(k, DK) for k in range(0, KT, DK)], oT, 2)

            transposes_x(1)
            pe.wait_ge(u_free, u.n)
            assert u.n == FILLS["ffn"], u.n
            pe.wait_ge(t_free, 3)
            for j in range(6):
                n = min(WC, FF - j * WC)
                ig, iu = chunk("gate", j * WC), chunk("up", j * WC)
                wg, wu = slot_up(ig % SLOTS, n), slot_up(iu % SLOTS, n)
                for c in range(n // P):
                    b = bank()
                    up_tile(b[:, 0:S], wg, c)
                    ins = up_tile(b[:, S:2 * S], wu, c)
                    ins.then_inc(u_full, 1)
                    if j and c < len(MODS[1][j - 1]):
                        mod_sum(1, MODS[1][j - 1][c], mods)
                        mods += 1
            mod_turn(3)
            broadcast_gate(2)
            pe.wait_ge(u_free, u.n - 2)
            first = 0
            chunks = []
            for n in DOWN_CHUNKS:
                chunks.append((first, n))
                first += n
            project("down", chunks, hid, 4)

            transposes_x(2)
            pe.wait_ge(u_free, u.n)

            def mlstm_in(j):
                i = chunk("mlstm_in", j * WC)
                w = slot_up(i % SLOTS)
                for g in range(2):
                    b = bank()
                    for c in range(2):
                        ins = up_tile(b[:, c * S:(c + 1) * S], w, 2 * g + c)
                    ins.then_inc(u_full, 1)

            for j in range(4):
                mlstm_in(j)

            def gate_products(t):
                pe.wait_ge(u_free, FILLS["qkv"] + 2 * (t + 1))
                if t == 0:
                    pe.wait_ge(small_loaded, 16 * 7)
                    pe.wait_ge(t_free, 5)
                for m, src in enumerate((xm[:, t, PAD:PAD + S], k_in[:, t], vT2[:, t % 2])):
                    ins = pe.matmul(ps[32 * m:32 * m + 2 * MH, 4 + m, 0:S], w_gates[:, m * IT + t, :], src,
                                    start=(t == 0), stop=(t == IT - 1))
                ins.then_inc(gates_full, 1)

            for t in range(IT):
                pe.wait_ge(xc_ready, t // 4 + 1)
                pe.wait_ge(bd_ready, t + 1)
                blocks = bd[:, t % 2]
                xt = xm[:, t, PAD:PAD + S]
                b = bank()
                pe.matmul(b[:, 0:S], blocks[:, 2], xt, start=True, stop=True)
                pe.matmul(b[:, S:S + P], xt[:, 0:P], blocks[:, 2], start=True, stop=True)
                pe.matmul(b[:, S + P:2 * S], xt[:, P:S], blocks[:, 2], start=True, stop=True).then_inc(u_full, 1)
                b = bank()
                pe.matmul(b[:, 0:S], blocks[:, 0], xc[:, t], start=True, stop=True)
                pe.matmul(b[:, S:2 * S], blocks[:, 1], xc[:, t], start=True, stop=True).then_inc(u_full, 1)
                if t:
                    gate_products(t - 1)
            gate_products(IT - 1)
            pe.wait_ge(gates_T_ready, 1)
            for t in range(TT):
                ins = pe.matmul(ps[:, 7, t * 2 * MH:(t + 1) * 2 * MH], gates_T[:, t * P:(t + 1) * P], eight[:], start=True, stop=True)
            ins.then_inc(gates_full, 1)
            pe.wait_ge(logf_ready, 1)
            pe.matmul(ps[:, 6, 0:MH], tri[:], logf[:, 0], start=True, stop=True)
            pe.matmul(ps[:, 6, MH:2 * MH], ones[:], logf[:, 0], start=True, stop=False)
            pe.matmul(ps[:, 6, MH:2 * MH], tri[:], logf[:, 1], start=False, stop=True).then_inc(cum_full, 1)
            for t in range(TT):
                pe.wait_ge(diag_ready, 3 + t)
                pe.matmul(ps[:, 4 + t], ones[:], diag_m, start=True, stop=True).then_inc(cum_full, 1)

            def m_scores(h):
                b = bank()
                for k in range(MK):
                    pe.matmul(b[:, 0:P], xm[:, MK * h + k, PAD:PAD + P], k_in[:, MK * h + k, 0:P],
                              start=(k == 0), stop=(k == MK - 1))
                for k in range(MK):
                    ins = pe.matmul(b[:, P:3 * P], xm[:, MK * h + k, PAD + P:PAD + S], k_in[:, MK * h + k, :],
                                    start=(k == 0), stop=(k == MK - 1))
                ins.then_inc(u_full, 1)

            def m_values(h, scored):
                w, wT = head_weights(h)
                pe.wait_ge(u_free, scored)
                b = bank()
                for i in range(3):
                    ins = pe.transpose(b[:, i * P:(i + 1) * P], w[:, i * P:(i + 1) * P], ident[:])
                ins.then_inc(u_full, 1)
                pe.wait_ge(u_free, u.n)
                c = slice(h * MD, (h + 1) * MD)
                pe.matmul(ps[:, 6], wT[:, 0:P], v_in[:, 0, c], start=True, stop=True)
                pe.matmul(ps[:, 7], wT[:, P:2 * P], v_in[:, 0, c], start=True, stop=False)
                pe.matmul(ps[:, 7], wT[:, 2 * P:3 * P], v_in[:, 1, c], start=False, stop=True).then_inc(num_full, 1)

            def m_turn(h):
                pe.wait_ge(hh_ready, h + 1)
                for g in range(2):
                    b = bank()
                    for c in range(2):
                        for t in range(TT):
                            k = MK * h + 2 * g + c
                            ins = pe.transpose(b[:, c * S + t * P:c * S + (t + 1) * P], v_in[:, t, k * P:(k + 1) * P], ident[:])
                    ins.then_inc(u_full, 1)

            for h in range(MH):
                m_scores(h)
                scored = u.n
                mlstm_in(4 + h)
                if h:
                    m_turn(h - 1)
                m_values(h, scored)
            m_turn(MH - 1)
            broadcast_gate(5)
            pe.wait_ge(m_out_ready, MH)
            project("mlstm_out", [(k, DK) for k in range(0, IT, DK)], xc, 5)

            transposes_x(3)
            pe.wait_ge(u_free, u.n)
            pe.wait_ge(t_free, 6)
            for t in range(TT):
                for k in range(KT):
                    ins = pe.matmul(ps[:, 4 + t, 0:E], hT[:, k, t * P:(t + 1) * P], w_router[:, k, :],
                                    start=(k == 0), stop=(k == KT - 1))
            ins.then_inc(logits_full, 1)
            pe.wait_ge(route, 3)
            chosen = lambda t: rt[:, t, 6, :]
            b = ps[:, 6]
            pe.matmul(b[:, 0:E], tri_strict[:], chosen(0), start=True, stop=True)
            pe.matmul(b[:, E:2 * E], ones[:], chosen(0), start=True, stop=False)
            pe.matmul(b[:, E:2 * E], tri_strict[:], chosen(1), start=False, stop=True)
            pe.matmul(b[:, 2 * E:3 * E], ones[:], chosen(0), start=True, stop=False)
            pe.matmul(b[:, 2 * E:3 * E], ones[:], chosen(1), start=False, stop=True).then_inc(logits_full, 1)
            broadcast_gate(6)
            assert u.n == FILLS["moe"], u.n

            def expert(e, width):
                tiles, sw = shape_of(width)
                wide = max(width, P)

                def arrived(c):
                    pe.wait_ge(landed[c % SLOTS], e * (16 * EC // SLOTS) + 16 * (PRE_USES + c // SLOTS + 1))

                pe.wait_ge(sel_ready, e + 1)
                for i in range(KT // 2):
                    for j in range(2):
                        k = 2 * i + j
                        for t in range(TT):
                            ins = pe.matmul(ps[:, i, j * S:j * S + wide], xn[:, t, k * P:(k + 1) * P], sel[:, t, 0:wide],
                                            start=(t == 0), stop=(t == TT - 1))
                    ins.then_inc(gather_full, 1)
                pe.wait_ge(y_added, e + 1)
                for st in range(tiles):
                    for t in range(TT):
                        ins = pe.transpose(ps[:, 4, st * S + t * P:st * S + (t + 1) * P],
                                           selw[:, t, st * P:(st + 1) * P], ident[:])
                ins.then_inc(scat_full, 1)
                pe.wait_ge(xg_ready, e * (KT // 2) + 2)

                def step(j):
                    arrived(2 * j)
                    arrived(2 * j + 1)
                    if j >= 2:
                        pe.wait_ge(hx_ready, step_count(e, j - 2))
                    wg, wu = slot_up((2 * j) % SLOTS), slot_up((2 * j + 1) % SLOTS)
                    b = 2 * (j % 2)
                    low = second_half(width)
                    for k in range(KT):
                        if j == 0 and k >= KT // 2 and k % 2 == 0:
                            pe.wait_ge(xg_ready, e * (KT // 2) + (k // 2 + 1))
                        x_k = xg[:, k, 0:width]
                        pe.matmul(ps[0:width, b], x_k, wg[:, k, :], start=(k == 0), stop=(k == KT - 1))
                        ins = pe.matmul(ps[low, b + 1], x_k, wu[:, k, :], start=(k == 0), stop=(k == KT - 1))
                    ins.then_inc(step_full, STEP)

                def turn(j, chunks_read):
                    pe.wait_ge(hx_ready, step_count(e, j))
                    if j >= 2:
                        pe.wait_ge(turn_free, step_count(e, j - 2))
                    for c in range(STEP):
                        ins = pe.transpose(ps[:, 6 + j % 2, c * P:(c + 1) * P], hx[:, j % 2, c * P:(c + 1) * P], ident[:])
                        if c == 0 and chunks_read:
                            ins.then_inc(freed, chunks_read)
                    ins.then_inc(turn_full, STEP)

                def hidden_tile(ft):
                    j, c = ft // STEP, ft % STEP
                    if c == 0:
                        arrived(2 * j)
                        arrived(2 * j + 1)
                    if ft >= UB:
                        pe.wait_ge(hx_ready, ft_count(e, ft - UB))
                    for half in range(2):
                        w = slot_up((2 * j + half) % SLOTS)
                        dst = ps[:, ft % UB, half * S:half * S + width]
                        for k in range(KT):
                            if ft == half == 0 and k >= KT // 2 and k % 2 == 0:
                                pe.wait_ge(xg_ready, e * (KT // 2) + (k // 2 + 1))
                            ins = pe.matmul(dst, w[:, k, c * P:(c + 1) * P], xg[:, k, 0:width], start=(k == 0), stop=(k == KT - 1))
                            if half == 0 and k == 0 and c == 0 and j:
                                ins.then_inc(freed, 2)
                    ins.then_inc(step_full, 1)

                def down(j):
                    c = 2 * EJ + j
                    arrived(c)
                    if tiles == 1:
                        pe.wait_ge(turn_free, step_count(e, j))
                    else:
                        pe.wait_ge(hx_ready, step_count(e, j))
                    w = slot_down(c % SLOTS)
                    for st in range(tiles):
                        for k in range(DK):
                            ft = DK * j + k
                            for n in range(2):
                                r = second_half(sw[st]) if n else slice(0, sw[st])
                                ins = pe.matmul(ps[r, 4 + 2 * st + n], eh[:, ft, st * P:st * P + sw[st]],
                                                w[:, k, n * 512:(n + 1) * 512], start=(ft == 0), stop=(ft == ET - 1))
                                if tiles == 2 and ft == st == n == 0:
                                    ins.then_inc(freed, 2)
                    ins.then_inc(freed, 1)

                if tiles == 1:
                    for j in range(EJ):
                        step(j)
                        if j:
                            turn(j - 1, 4 if j == 1 else 2)
                    pe.wait_ge(scat_ready, e + 1)
                    down(0)
                    turn(EJ - 1, 0)
                else:
                    for ft in range(ET):
                        hidden_tile(ft)
                    pe.nop().then_inc(turn_full, ET)
                    pe.wait_ge(scat_ready, e + 1)
                    down(0)
                for j in range(1, ET // DK):
                    down(j)
                pe.wait_ge(ye_ready, e + 1)
                pe.wait_ge(half_ready, e + 1)
                for t in range(TT):
                    for n in range(2):
                        for st in range(tiles):
                            ins = pe.matmul(ps[:, 4 + 2 * t + n], scat[0:sw[st], st, t * P:(t + 1) * P],
                                            ye[0:sw[st], st, n * 512:(n + 1) * 512], start=(st == 0), stop=(st == tiles - 1))
                ins.then_inc(spread, 1)

            pe.wait_ge(u_free, u.n)
            pe.nop().then_inc(step_full, 2)
            pe.nop().then_inc(turn_full, 2)
            pe.wait_ge(counts_ready, 1)
            with pe.Fori(0, E) as e:
                by_width(pe, e, expert)

        def dve_program(dve):
            steps = Count()
            u = Count()
            powers = Count()
            xs = Count()
            sums = Count()
            t_reads = [3, 5, 6]

            def link(ins):
                ins.then_inc(dstep, 1)
                dve.wait_ge(dstep, steps.next())

            def full():
                n = u.next()
                dve.wait_ge(u_full, n)
                return ps[:, (n - 1) % UB]

            def mod_chunk(layer, j, n):
                i = order[(f"mod{layer}", j * WC)]
                wait_chunk(dve, i)
                if n >= 2:
                    dve.wait_ge(mod_summed, n - 1)
                w = slot_up(i % SLOTS)
                acc = mod_acc[:, n % 2]
                link(dve.tensor_scalar(acc, w[:, 0], cond[:, 0:1], None, ALU.mult))
                for k in range(1, KT):
                    ins = dve.scalar_tensor_tensor(out=acc, in0=w[:, k], scalar=cond[:, k:k + 1], in1=acc,
                                                   op0=ALU.mult, op1=ALU.add)
                    if k < KT - 1:
                        link(ins)
                ins.then_inc(acc_ready, 1)

            def modulation(n, first, last):
                layer = n // 3
                dve.wait_ge(mod_summed, MOD_ENDS[n - 1])
                dve.tensor_copy(mod_rows, ps[:, 7, 0:P]).then_inc(mod_rows_ready, 1)
                dve.wait_ge(mod_turned, n)
                c = lambda v: v[:, layer, 4 * first:4 * last].rearrange("p (j i) -> p j i", i=4)
                turned = ps[:, 6, 0:P].rearrange("p (i j) -> p j i", i=4)[:, first:last]
                dve.tensor_tensor(c(modc), turned, c(mod_b), ALU.add).then_inc(t_free, 1)
                dve.wait_ge(t_free, (1, 2, 4)[n - 1])

            def emptied(ins):
                return ins.then_inc(u_free, 1)

            def variance(t):
                dve.wait_ge(sq_ready, sums.next())
                dve.tensor_scalar(var[:, t:t + 1], sq_sum[:, t:t + 1], 1.0 / D, EPS, ALU.mult, ALU.add).then_inc(var_ready, 1)
                powers.next()

            def modulated(n):
                layer, i = n // 2, n % 2
                for g in range(KT // 2):
                    b = full()
                    for j in range(2):
                        k = 2 * g + j
                        ins = dve.tensor_scalar(hT[:, k, :], b[:, j * S:(j + 1) * S], mul_c[:, n, k:k + 1],
                                                modc[:, layer, 24 * i + k:24 * i + k + 1], ALU.mult, ALU.add)
                    emptied(ins)

            def gate_diagonals(n):
                for k in range(KT):
                    ins = dve.tensor_scalar(scratch[:, k * P:(k + 1) * P], ident[:], gate_c[:, n, k:k + 1], None, ALU.mult)
                ins.then_inc(diag_ready, 1)

            def gate_rows():
                for i in range(2):
                    emptied(dve.tensor_copy(gate_bc[:, i * 512:(i + 1) * 512], full()))
                dve.wait_ge(u_free, u.n)

            def add_output(y, t, power, in_psum):
                dve.wait_ge(rstd_ready, power)
                if t:
                    dve.wait_ge(x_new, xs.n)
                ins = dve.scalar_tensor_tensor(out=scratch, in0=y, scalar=rstd[:, t:t + 1], in1=gate_bc, op0=ALU.mult, op1=ALU.mult)
                if in_psum and t == TT - 1:
                    ins.then_inc(t_free, 1)
                    dve.wait_ge(t_free, t_reads.pop(0))
                else:
                    link(ins)
                dve.tensor_tensor(x[:, t], x[:, t], scratch, ALU.add).then_inc(x_new, 1)
                xs.next()

            def output_to_input():
                for t in range(TT):
                    variance(t)
                    add_output(y_banks(t), t, powers.n, True)
                    variance(t)

            b = full()
            emptied(dve.tensor_copy(vecs[:], b[:, 0:3 * P]))
            dve.wait_ge(u_free, 1)
            dve.wait_ge(lam_loaded, 16)
            link(dve.tensor_tensor(lam_in[:, 0:4:2], lam_in[:, 0:4:2], lam_in[:, 1:4:2], ALU.mult))
            dve.tensor_reduce(lam_s, lam_in[:, 0:4:2], AX_X, ALU.add).then_inc(lam_ready, 1)
            dve.wait_ge(consts, 1)
            link(dve.tensor_tensor(eight[:], ident[:, 0:2 * MH], ident[:, 32:32 + 2 * MH], ALU.add))
            link(dve.tensor_tensor(eight[:], eight[:], ident[:, 64:64 + 2 * MH], ALU.add))
            link(dve.scalar_tensor_tensor(out=dist, in0=dist, scalar=-1.0, in1=dist, op0=ALU.mult, op1=ALU.max))
            dve.memset(dist[0:CHUNK, CHUNK:P], BIG)
            link(dve.memset(dist[0:CHUNK, 2 * P + CHUNK:3 * P], BIG))
            dve.wait_ge(lam_ready, 2)
            link(dve.tensor_tensor(neg_lam, lam_e[:, 1:2], lam_e[:, 0:1], ALU.subtract))
            link(dve.tensor_scalar(neg_lam, neg_lam, -LAMBDA_INIT, None, ALU.add))
            for t in range(TT):
                variance(t)
            dve.wait_ge(cond_ready, 1)
            mods = 0
            for j in range(4):
                mod_chunk(0, j, mods)
                mods += 1
            modulation(1, 0, 4)
            link(dve.scalar_tensor_tensor(out=mul_c[:, 0], in0=modc[:, 0, 8:16], scalar=1.0, in1=norm_g(0, 0),
                                          op0=ALU.add, op1=ALU.mult))
            modulated(0)
            for j in range(6):
                for g in range(2):
                    b = full()
                    pair = slice((4 * j + 2 * g) % 8, (4 * j + 2 * g) % 8 + 2)
                    b2 = b.rearrange("p (k s) -> p k s", k=2)
                    if j < 2:
                        ins = dve.tensor_scalar(qT[:, pair], b2, float(DA) ** -0.5, None, ALU.mult)
                    elif j < 4:
                        ins = dve.tensor_copy(kT[:, pair], b2)
                    else:
                        ins = dve.tensor_copy(v_nat[:, g, (j - 4) * 512:(j - 3) * 512], b)
                    emptied(ins)
                for m in MODS[0][j]:
                    mod_chunk(0, m, mods)
                    mods += 1
            modulation(2, 4, 12)
            dve.tensor_tensor(gate_c[:, 0], modc[:, 0, 16:24], norm_g(0, 1), ALU.mult)
            dve.tensor_tensor(gate_c[:, 1], modc[:, 0, 40:48], norm_g(0, 3), ALU.mult)
            link(dve.scalar_tensor_tensor(out=mul_c[:, 1], in0=modc[:, 0, 32:40], scalar=1.0, in1=norm_g(0, 2),
                                          op0=ALU.add, op1=ALU.mult))
            gate_diagonals(0)

            def logits(h):
                bb = h % 2
                if h >= 2:
                    dve.wait_ge(aT_full, h - 1)
                slope = 2.0 ** (-8.0 * (h + 1) / HEADS)
                for c in range(2):
                    emptied(dve.scalar_tensor_tensor(out=probs[:, bb, c], in0=dist, scalar=-slope, in1=full()[:, 0:384],
                                                     op0=ALU.mult, op1=ALU.add))
                dve.wait_ge(u_free, u.n)
                for c in range(2):
                    i = bb * 4 + c * 2
                    dve.tensor_reduce(nmax[:, i:i + 1], probs[:, bb, c, 0:P], AX_X, ALU.max, negate=True)
                    ins = dve.tensor_reduce(nmax[:, i + 1:i + 2], probs[:, bb, c, P:3 * P], AX_X, ALU.max, negate=True)
                ins.then_inc(maxed, 1)

            def difference(h):
                bb = h % 2
                dve.wait_ge(probs_ready, h + 1)
                link(dve.reciprocal(prec[:, bb * 4:bb * 4 + 4], psum_s[:, bb * 4:bb * 4 + 4]))
                link(dve.tensor_scalar(prec[:, bb * 4 + 2:bb * 4 + 4], prec[:, bb * 4 + 2:bb * 4 + 4], neg_lam, None, ALU.mult))
                for q, r in enumerate((slice(0, P), slice(P, 3 * P))):
                    i = bb * 4 + q
                    ins = dve.tensor_scalar(probs[:, bb, 0, r], probs[:, bb, 0, r], prec[:, i:i + 1], None, ALU.mult)
                link(ins)
                for q, r in enumerate((slice(0, P), slice(P, 3 * P))):
                    i = bb * 4 + 2 + q
                    ins = dve.scalar_tensor_tensor(out=probs[:, bb, 0, r], in0=probs[:, bb, 1, r], scalar=prec[:, i:i + 1],
                                                   in1=probs[:, bb, 0, r], op0=ALU.mult, op1=ALU.add)
                ins.then_inc(a_ready, 1)

            for h in range(HEADS + 1):
                if h < HEADS:
                    logits(h)
                if h:
                    difference(h - 1)
            gate_rows()
            dve.wait_ge(o_ready, HEADS)
            o16 = o_nat.rearrange("p t (h e) -> p (t h) e", e=HD)
            dve.tensor_scalar(var16, sq16, 1.0 / HD, EPS, ALU.mult, ALU.add).then_inc(var_ready, 1)
            dve.wait_ge(rstd_ready, powers.next())
            for t in range(TT):
                r = slice(t * HEADS, (t + 1) * HEADS)
                dve.tensor_tensor(o16[:, r], o16[:, r], rstd16[:, r].unsqueeze(2).broadcast_to([P, HEADS, HD]),
                                  ALU.mult).then_inc(on_ready, 1)
            for g in range(KT // 2):
                emptied(dve.tensor_scalar(oT[:, 2 * g:2 * g + 2], full().rearrange("p (k s) -> p k s", k=2), subln,
                                          1.0 - LAMBDA_INIT, ALU.mult, ALU.mult))
            output_to_input()

            modulated(1)
            for j in range(6):
                n = min(WC, FF - j * WC)
                for c in range(n // P):
                    ft = 4 * j + c
                    b = full()
                    dve.wait_ge(silu_ready, ft + 1)
                    emptied(dve.tensor_tensor(hid[:, ft], hid[:, ft], b[:, S:2 * S], ALU.mult))
                for m in MODS[1][j]:
                    mod_chunk(1, m, mods)
                    mods += 1
            gate_diagonals(1)
            modulation(3, 0, 12)
            gate_rows()
            for i in range(2):
                dve.tensor_tensor(gate_c[:, 2 + i], modc[:, 1, 24 * i + 16:24 * i + 24], norm_g(1, 2 * i + 1), ALU.mult)
                ins = dve.scalar_tensor_tensor(out=mul_c[:, 2 + i], in0=modc[:, 1, 24 * i + 8:24 * i + 16], scalar=1.0,
                                               in1=norm_g(1, 2 * i), op0=ALU.add, op1=ALU.mult)
            link(ins)
            output_to_input()

            modulated(2)
            dve.wait_ge(consts, 2)
            for j in range(4):
                for g in range(2):
                    t0 = 4 * j + 2 * g
                    emptied(dve.tensor_copy(xm[:, t0:t0 + 2, PAD:PAD + S], full().rearrange("p (k s) -> p k s", k=2)))
                dve.wait_ge(u_free, u.n)
                for tap in range(CONV):
                    for t in range(4 * j, 4 * j + 4):
                        if tap == 0:
                            ins = dve.tensor_scalar(xc[:, t], xm[:, t, 0:S], conv_w(0, t), None, ALU.mult)
                        else:
                            ins = dve.scalar_tensor_tensor(out=xc[:, t], in0=xm[:, t, tap:tap + S], scalar=conv_w(tap, t),
                                                           in1=xc[:, t], op0=ALU.mult, op1=ALU.add)
                    if tap < CONV - 1:
                        link(ins)
                ins.then_inc(conv_ready, 1)
            for t in range(IT):
                b = full()
                if t >= 2:
                    dve.wait_ge(gates_full, t - 1)
                dve.tensor_copy(vT2[:, t % 2], b[:, 0:S])
                emptied(dve.tensor_copy(v_in[:, :, t * P:(t + 1) * P], b[:, S:2 * S].rearrange("p (t s) -> p t s", t=TT)))
                b = full()
                dve.tensor_copy(xm[:, t, PAD:PAD + S], b[:, 0:S])
                emptied(dve.tensor_copy(k_in[:, t], b[:, S:2 * S]))
                dve.tensor_scalar(xc[:, t], xc[:, t], skip(t), None, ALU.mult)
            dve.wait_ge(bd_ready, IT)
            dve.wait_ge(u_full, u.n)
            dve.memset(gates_T, 0.0).then_inc(gates_T_clear, 1)
            dve.wait_ge(gates_T_clear, 1)
            dve.wait_ge(gates_full, IT)
            for m in range(3):
                r = slice(32 * m, 32 * m + 2 * MH)
                ins = dve.tensor_copy(gates_T[r], ps[r, 4 + m, 0:S])
            ins.then_inc(gates_T_ready, 1)
            dve.wait_ge(gates_full, IT + 1)
            for t in range(TT):
                ins = dve.tensor_tensor(gates[:, t], ps[:, 7, t * 2 * MH:(t + 1) * 2 * MH], b_gates[:], ALU.add)
            link(ins)
            fg = gates[:, :, MH:2 * MH]
            dve.scalar_tensor_tensor(out=f_abs, in0=fg, scalar=-1.0, in1=fg, op0=ALU.mult, op1=ALU.max).then_inc(logf_in, 1)
            link(dve.tensor_scalar(logf, fg, 0.0, None, ALU.min))
            dve.wait_ge(logf_ln, 1)
            dve.tensor_tensor(logf, logf, f_exp, ALU.subtract).then_inc(logf_ready, 1)
            dve.wait_ge(cum_full, 1)
            link(dve.tensor_copy(cumf, ps[:, 6, 0:TT * MH].rearrange("p (t g) -> p t g", t=TT)))
            link(dve.tensor_tensor(a_col, gates[:, :, 0:MH], cumf, ALU.subtract))
            for t in range(TT):
                if t:
                    dve.wait_ge(cum_full, 2)
                for h in range(MH):
                    ins = dve.tensor_scalar(diag_m[:, h * P:(h + 1) * P], ident[:], a_col[:, t, h:h + 1], None, ALU.mult)
                ins.then_inc(diag_ready, 1)
            dve.wait_ge(cum_full, 3)

            def exponents(h):
                b = h % 2
                r = slice(h * P, (h + 1) * P)
                if h:
                    dve.wait_ge(dw_ready, h)
                dve.tensor_tensor(dw[:, b, 0:P], ps[:, 4, r], causal[:], ALU.add)
                dve.tensor_copy(dw[:, b, P:2 * P], ps[:, 4, r])
                link(dve.tensor_tensor(dw[:, b, 2 * P:3 * P], ps[:, 5, r], causal[:], ALU.add))
                dve.tensor_reduce(run_max[:, 0:1], dw[:, b, 0:P], AX_X, ALU.max)
                link(dve.tensor_reduce(run_max[:, 1:2], dw[:, b, P:3 * P], AX_X, ALU.max))
                link(dve.tensor_scalar(run_max, run_max, 0.0, None, ALU.max))
                dve.tensor_scalar(neg_m, run_max, -1.0, None, ALU.mult)
                dve.tensor_tensor(m_sum, cumf[:, :, h], run_max, ALU.add).then_inc(rmax_ready, 1)

            def weigh(h):
                w, wT = head_weights(h)
                b = h % 2
                bank = full()
                dve.wait_ge(dw_ready, h + 1)
                dve.tensor_tensor_reduce(out=w[:, 0:P], in0=bank[:, 0:P], in1=dw[:, b, 0:P], scale=float(MD) ** -0.5,
                                         scalar=0.0, op0=ALU.mult, op1=ALU.add, accum_out=den[:, 0:1])
                emptied(dve.tensor_tensor_reduce(out=w[:, P:3 * P], in0=bank[:, P:3 * P], in1=dw[:, b, P:3 * P],
                                                 scale=float(MD) ** -0.5, scalar=0.0, op0=ALU.mult, op1=ALU.add,
                                                 accum_out=den[:, 1:2]))
                dve.wait_ge(u_free, u.n)
                link(dve.scalar_tensor_tensor(out=rden, in0=den, scalar=-1.0, in1=den, op0=ALU.mult, op1=ALU.max))
                link(dve.tensor_tensor(rden, rden, e_m, ALU.max))
                link(dve.reciprocal(rden, rden))

            def turned_weights(h):
                w, wT = head_weights(h)
                emptied(dve.tensor_copy(wT, full()[:, 0:3 * P]))

            def outputs(h):
                c = slice(h * MD, (h + 1) * MD)
                dve.wait_ge(num_full, h + 1)
                for t in range(TT):
                    ins = dve.tensor_scalar(v_in[:, t, c], ps[:, 6 + t], rden[:, t:t + 1], None, ALU.mult)
                link(ins)
                for t in range(TT):
                    ins = dve.bn_stats(bn6[:, t], v_in[:, t, c])
                link(ins)
                for t in range(TT):
                    ins = dve.bn_aggr(mean_var[:, t], bn6[:, t])
                link(ins)
                dve.tensor_scalar(var, mean_var[:, :, 1], EPS, None, ALU.add).then_inc(var_ready, 1)
                dve.wait_ge(rstd_ready, powers.next())
                for t in range(TT):
                    ins = dve.tensor_scalar(v_in[:, t, c], v_in[:, t, c], mean_var[:, t, 0:1], rstd[:, t:t + 1],
                                            ALU.subtract, ALU.mult)
                ins.then_inc(hh_ready, 1)

            def turned_outputs(h):
                for g in range(2):
                    b = full()
                    for c in range(2):
                        t = MK * h + 2 * g + c
                        ins = dve.scalar_tensor_tensor(out=xc[:, t], in0=b[:, c * S:(c + 1) * S], scalar=norm_m(t),
                                                       in1=xc[:, t], op0=ALU.mult, op1=ALU.add)
                    emptied(ins)
                dve.wait_ge(u_free, u.n)
                dve.wait_ge(silu_ready, FT + h + 1)
                dve.tensor_tensor(xc[:, MK * h:MK * (h + 1)], xc[:, MK * h:MK * (h + 1)], z_in(h), ALU.mult)\
                    .then_inc(m_out_ready, 1)

            for h in range(MH):
                exponents(h)
                weigh(h)
                for g in range(2):
                    t0 = MK * h + 2 * g
                    emptied(dve.tensor_copy(xm[:, t0:t0 + 2, PAD:PAD + S], full().rearrange("p (k s) -> p k s", k=2)))
                if h:
                    turned_outputs(h - 1)
                turned_weights(h)
                outputs(h)
            turned_outputs(MH - 1)
            gate_diagonals(2)
            gate_rows()
            output_to_input()

            modulated(3)
            logit, top, e2, w12 = rt[:, :, 0], rt[:, :, 1], rt[:, :, 3], rt[:, :, 4]
            index, chosen, weight, pick = rt[:, :, 5], rt[:, :, 6], rt[:, :, 7], rt[:, :, 8]
            dve.wait_ge(logits_full, 1)
            for t in range(TT):
                ins = dve.tensor_tensor(logit[:, t], ps[:, 4 + t, 0:E], b_router[:], ALU.add)
            link(ins)
            for t in range(TT):
                ins = dve.max(top[:, t], logit[:, t])
            link(ins)
            for t in range(TT):
                ins = dve.max_index(top_i[:, t], top[:, t], logit[:, t])
            link(ins)
            dve.tensor_tensor(e2[:, :, 0], top[:, :, 1], top[:, :, 0], ALU.subtract).then_inc(route, 1)
            link(dve.tensor_copy(index, top_i[:]))
            dve.wait_ge(route, 2)
            link(dve.tensor_scalar(w12[:, :, 0], e2[:, :, 1], 1.0, None, ALU.add))
            link(dve.reciprocal(w12[:, :, 0], w12[:, :, 0]))
            link(dve.tensor_tensor(w12[:, :, 1], w12[:, :, 0], e2[:, :, 1], ALU.mult))
            for t in range(TT):
                dve.tensor_scalar(chosen[:, t], iota8, index[:, t, 0:1], None, ALU.is_equal)
                dve.tensor_scalar(weight[:, t], iota8, index[:, t, 0:1], w12[:, t, 0:1], ALU.is_equal, ALU.mult)
                dve.tensor_scalar(pick[:, t], iota8, index[:, t, 1:2], None, ALU.is_equal)
                ins = dve.tensor_scalar(rt[:, t, 9], iota8, index[:, t, 1:2], w12[:, t, 1:2], ALU.is_equal, ALU.mult)
            link(ins)
            dve.tensor_tensor(weight, weight, rt[:, :, 9], ALU.add)
            ins = dve.tensor_tensor(chosen, chosen, pick, ALU.add)
            ins.then_inc(route, 1)
            dve.wait_ge(route, 3)
            for t in range(TT):
                dve.tensor_copy(per_e[:, :, 2 + t], chosen[:, t])
                dve.tensor_copy(per_e[:, :, 4 + t], weight[:, t])
            dve.wait_ge(logits_full, 2)
            for t in range(TT):
                dve.tensor_copy(per_e[:, :, t], ps[:, 6, t * E:(t + 1) * E])
            totals = ps[:, 6, 2 * E:3 * E]
            link(dve.scalar_tensor_tensor(out=keys, in0=totals, scalar=float(E), in1=iota8, op0=ALU.mult, op1=ALU.add))
            link(dve.memset(keys[:, FIRST:FIRST + 1], float(2 * E * S)))
            by_place = lambda v: v.unsqueeze(2).broadcast_to([P, E, E])
            by_expert = lambda v: v.unsqueeze(1).broadcast_to([P, E, E])
            link(dve.tensor_tensor(pairs[:, 0], by_expert(keys), by_place(keys), ALU.is_gt))
            link(dve.tensor_reduce(ranks, pairs[:, 0], AX_X, ALU.add))
            link(dve.tensor_tensor(pairs[:, 0], by_expert(ranks), by_place(rank_at[:]), ALU.is_equal))
            link(dve.tensor_tensor(pairs[:, 1], pairs[:, 0], by_expert(iota8), ALU.mult))
            link(dve.tensor_tensor(pairs[:, 0], pairs[:, 0], by_expert(totals), ALU.mult))
            for b in range(2):
                ins = dve.tensor_reduce(placed[:, b], pairs[:, b], AX_X, ALU.add)
            link(ins)
            dve.tensor_copy(counts[:], placed[:, 0])
            dve.memset(order_e[:, E:E + 1], 0)
            dve.tensor_copy(order_e[:, 0:E], placed[:, 1]).then_inc(counts_ready, 1)
            gate_diagonals(3)
            gate_rows()
            dve.memset(y_sum, 0.0).then_inc(y_added, 1)
            dve.memset(ye, 0.0).then_inc(hx_ready, 2)
            dve.wait_ge(counts_ready, 1)
            assert u.n == FILLS["moe"], u.n

            def select(e):
                which = dve.value_load(order_e[0:1, bass.ds(e, 1)], min_val=0, max_val=E - 1)
                dve.tensor_copy(cur[:], per_e[:, bass.ds(which, 1), :].rearrange("p a n -> p (a n)")).then_inc(cur_ready, 1)
                dve.wait_ge(cur_ready, e + 1)
                for t in range(TT):
                    dve.tensor_scalar(sel[:, t], slot_iota[:], cur[:, t:t + 1], cur[:, 2 + t:3 + t], ALU.is_equal, ALU.mult)
                    ins = dve.tensor_scalar(selw[:, t], slot_iota[:], cur[:, t:t + 1], cur[:, 4 + t:5 + t],
                                            ALU.is_equal, ALU.mult)
                ins.then_inc(sel_ready, 1)

            def expert(e, width):
                tiles, sw = shape_of(width)
                for i in range(KT // 2):
                    dve.wait_ge(gather_full, e * (KT // 2) + (i + 1))
                    for j in range(2):
                        k = 2 * i + j
                        ins = dve.tensor_scalar(xg[:, k, 0:width], ps[:, i, j * S:j * S + width], mul_c[:, 3, k:k + 1],
                                                modc[:, 1, 24 + k:25 + k], ALU.mult, ALU.add)
                    ins.then_inc(xg_ready, 1)
                if tiles == 1:
                    for j in range(EJ):
                        dve.wait_ge(silu_moe, step_count(e, j))
                        dve.tensor_tensor(hx[0:width, j % 2, 0:WC], hx[0:width, j % 2, 0:WC],
                                          ps[second_half(width), 2 * (j % 2) + 1], ALU.mult).then_inc(hx_ready, STEP)
                else:
                    for ft in range(ET):
                        dve.wait_ge(silu_moe, ft_count(e, ft))
                        dve.tensor_tensor(eh[:, ft, 0:width], eh[:, ft, 0:width], ps[:, ft % UB, S:S + width],
                                          ALU.mult).then_inc(hx_ready, 1)
                dve.wait_ge(scat_full, e + 1)
                select(e + 1)
                if tiles == 1:
                    dve.wait_ge(freed, e * EC + (SLOTS + EC))
                    dve.tensor_copy(ye[0:width, 0, 512:1024], ps[second_half(width), 5]).then_inc(half_ready, 1)
                else:
                    dve.nop().then_inc(half_ready, 1)
                dve.wait_ge(y_added, e + 1)
                dve.wait_ge(spread, e + 1)
                for t in range(TT):
                    for c in range(2):
                        r = slice(c * 512, (c + 1) * 512)
                        ins = dve.tensor_tensor(y_sum[:, t, r], y_sum[:, t, r], ps[:, 4 + 2 * t + c], ALU.add)
                ins.then_inc(y_added, 1)

            select(0)
            with dve.Fori(0, E) as e:
                by_width(dve, e, expert)
            for t in range(TT):
                variance(t)
            for t in range(TT):
                add_output(y_sum[:, t], t, powers.n - 1 + t, False)

        silu_moe = sem("silu_moe")
        gather_full = sem("gather_full")
        xg_ready = sem("xg_ready")
        step_full = sem("step_full")
        hx_ready = sem("hx_ready")
        turn_full = sem("turn_full")
        turn_free = sem("turn_free")
        half_ready = sem("half_ready")
        cur_ready = sem("cur_ready")

        block = ctx.enter_context(nc.Block())

        @block.sync
        def _(sp):
            sp_program(sp)

        @block.gpsimd
        def _(pool):
            pool_program(pool)

        @block.scalar
        def _(act):
            act_program(act)

        @block.tensor
        def _(pe):
            pe_program(pe)

        @block.vector
        def _(dve):
            dve_program(dve)


_NAMES = ["x", "c", "mod_w", "mod_b", "norm_g", "attn_w_in", "attn_w_out", "attn_lambda", "attn_subln",
          "ffn_w_gate", "ffn_w_up", "ffn_w_down", "mlstm_w_in", "mlstm_conv_w", "mlstm_conv_b", "mlstm_w_q",
          "mlstm_w_k", "mlstm_w_v", "mlstm_w_gate", "mlstm_b_gate", "mlstm_skip", "mlstm_norm", "mlstm_w_out",
          "moe_w_router", "moe_b_router", "moe_w_gate", "moe_w_up", "moe_w_down"]


def kernel(**inputs):
    import numpy as np
    import concourse.bacc as bacc
    from concourse.bass_utils import run_bass_kernel_spmd

    nc = bacc.Bacc("TRN2", target_bir_lowering=False, num_devices=1)
    arrays, args = {}, {}
    for name in _NAMES:
        v = np.ascontiguousarray(inputs[name])
        arrays[f"in_{name}"] = v
        args[name] = nc.dram_tensor(f"in_{name}", v.shape, mybir.dt.from_np(v.dtype), kind="ExternalInput").ap()
    out = nc.dram_tensor("out_0", (1, S, D), F32, kind="ExternalOutput").ap()
    trunk(nc, args, out)
    r = run_bass_kernel_spmd(nc, [arrays], core_ids=[0])
    return r.results[0]["out_0"]
```
